# Optimizing a Trainium2 kernel written in Bass

```python
import math
import jax, jax.numpy as jnp
from jax import lax
import numpy as np

D_MODEL = 1024
BATCH = 1
SEQ = 256
DEPTH = 2
DEC_BATCH = 1
DEC_SEQ = 2048
PAST_LEN = 512

GRID_W = 64
MIX_W = D_MODEL
FOURIER_W = MIX_W // 4
CONV_W = MIX_W // 4
ATTN_W = MIX_W // 2
N_HEADS = 4
HEAD_DIM = ATTN_W // (2 * N_HEADS)
QK_W = 2 * HEAD_DIM
CONV_K = 3
ROPE_BASE = 10000.0
Q_BLOCK = 128
EPS = 1e-6
IN_DIM = 2 * FOURIER_W + 4 * CONV_W + 4 * ATTN_W

kernel_name = "hybrid_fourier_conv_diffattn_dit_step"

def _split_points():
    sizes = [FOURIER_W, FOURIER_W, CONV_W, CONV_W, CONV_W, CONV_W, ATTN_W, ATTN_W, ATTN_W]
    return [int(s) for s in np.cumsum(sizes)]

def _rmsnorm(x, g):
    xf = x.astype(jnp.float32)
    y = xf * lax.rsqrt(jnp.mean(xf * xf, axis=-1, keepdims=True) + EPS)
    return (y * g.astype(jnp.float32)).astype(x.dtype)

def _fourier(u):
    f = jnp.fft.fft2(u.astype(jnp.float32), axes=(1, 2), norm="ortho")
    return jnp.real(f).astype(u.dtype)

def _short_conv(b_gate, c_gate, h, w, bias):
    z = c_gate * h
    n = z.shape[1]
    zp = jnp.pad(z, ((0, 0), (1, 1), (0, 0)))
    y = zp[:, 0:n] * w[0] + zp[:, 1:n + 1] * w[1] + zp[:, 2:n + 2] * w[2] + bias
    return b_gate * y

def _rope_axis(t, pos):
    r = t.shape[-1]
    half = r // 2
    inv = 1.0 / (ROPE_BASE ** (jnp.arange(0, r, 2, dtype=jnp.float32) / r))
    ang = pos.astype(jnp.float32)[:, None] * inv[None, :]
    ang = jnp.concatenate([ang, ang], axis=-1)
    cos = jnp.cos(ang)[None, :, None, None, :]
    sin = jnp.sin(ang)[None, :, None, None, :]
    tf = t.astype(jnp.float32)
    rot = jnp.concatenate([-tf[..., half:], tf[..., :half]], axis=-1)
    return (tf * cos + rot * sin).astype(t.dtype)

def _rope_2d(t, row, col):
    b, n, h, _ = t.shape
    t = t.reshape(b, n, h, 2, HEAD_DIM)
    half = HEAD_DIM // 2
    tr = _rope_axis(t[..., :half], row)
    tc = _rope_axis(t[..., half:], col)
    return jnp.concatenate([tr, tc], axis=-1).reshape(b, n, h, QK_W)

def _diff_attention(q, k, v, lam):
    b, n, h, _ = q.shape
    nb = n // Q_BLOCK
    scale = HEAD_DIM ** -0.5
    k1 = k[..., :HEAD_DIM]
    k2 = k[..., HEAD_DIM:]
    qb = q.reshape(b, nb, Q_BLOCK, h, QK_W).transpose(1, 0, 2, 3, 4)

    def block(qblk):
        s1 = jnp.einsum('bqhd,bkhd->bhqk', qblk[..., :HEAD_DIM], k1,
                        preferred_element_type=jnp.float32) * scale
        s2 = jnp.einsum('bqhd,bkhd->bhqk', qblk[..., HEAD_DIM:], k2,
                        preferred_element_type=jnp.float32) * scale
        p = jax.nn.softmax(s1, axis=-1) - lam * jax.nn.softmax(s2, axis=-1)
        return jnp.einsum('bhqk,bkhd->bqhd', p.astype(v.dtype), v)

    o = lax.map(block, qb)
    return o.transpose(1, 0, 2, 3, 4).reshape(b, n, h, v.shape[-1])

def _layer(x, mod, norm_g, w_in, conv_w, conv_b, lam_vec, subln_g, w_out,
           layer_idx, pos, ctx_kv):
    shift, scale, gate = jnp.split(mod, 3, axis=-1)
    h = _rmsnorm(x, norm_g) * (1.0 + scale) + shift
    z = h @ w_in
    fa, ga, bg, cg, hc, gb, q, k, v, gc = jnp.split(z, _split_points(), axis=-1)
    b, n, _ = x.shape
    ya = _fourier(fa) * jax.nn.silu(ga)
    yb = _short_conv(bg, cg, hc, conv_w, conv_b) * jax.nn.silu(gb)
    q = q.reshape(b, n, N_HEADS, QK_W)
    k = k.reshape(b, n, N_HEADS, QK_W)
    v = v.reshape(b, n, N_HEADS, QK_W)
    if pos is not None:
        q = _rope_2d(q, pos[0], pos[1])
        k = _rope_2d(k, pos[0], pos[1])
    if ctx_kv is not None:
        keys = jnp.concatenate([ctx_kv[0].astype(k.dtype), k], axis=1)
        vals = jnp.concatenate([ctx_kv[1].astype(v.dtype), v], axis=1)
    else:
        keys, vals = k, v
    lam_init = 0.8 - 0.6 * math.exp(-0.3 * layer_idx)
    lv = lam_vec.astype(jnp.float32)
    lam = jnp.exp(jnp.sum(lv[0] * lv[1])) - jnp.exp(jnp.sum(lv[2] * lv[3])) + lam_init
    o = _diff_attention(q, keys, vals, lam)
    o = _rmsnorm(o, subln_g) * (1.0 - lam_init)
    yc = o.reshape(b, n, ATTN_W) * jax.nn.silu(gc)
    out = jnp.concatenate([ya, yb, yc], axis=-1) @ w_out
    return x + gate * out, k, v

def setup_inputs(seed: int = 0) -> dict:
    key = jax.random.key(seed)
    ks = jax.random.split(key, 16)
    f32 = jnp.float32
    nrm = lambda k, s: jax.random.normal(k, s, dtype=f32)
    return {
        "x_prompt": nrm(ks[0], (BATCH, SEQ, D_MODEL)),
        "x_sample": nrm(ks[1], (DEC_BATCH, DEC_SEQ, D_MODEL)),
        "cache_k": nrm(ks[2], (DEC_BATCH, DEPTH, PAST_LEN, N_HEADS, QK_W)),
        "cache_v": nrm(ks[3], (DEC_BATCH, DEPTH, PAST_LEN, N_HEADS, QK_W)),
        "c": nrm(ks[4], (DEC_BATCH, D_MODEL)),
        "c_ctx": nrm(ks[5], (D_MODEL,)),
        "norm_g": 1.0 + 0.02 * nrm(ks[6], (DEPTH, D_MODEL)),
        "w_mod": nrm(ks[7], (DEPTH, D_MODEL, 3 * D_MODEL)) * D_MODEL ** -0.5,
        "b_mod": 0.02 * nrm(ks[8], (DEPTH, 3 * D_MODEL)),
        "w_in": nrm(ks[9], (DEPTH, D_MODEL, IN_DIM)) * D_MODEL ** -0.5,
        "conv_w": nrm(ks[10], (DEPTH, CONV_K, CONV_W)) * CONV_K ** -0.5,
        "conv_b": 0.02 * nrm(ks[11], (DEPTH, CONV_W)),
        "lam_vec": 0.1 * nrm(ks[12], (DEPTH, 4, HEAD_DIM)),
        "subln_g": 1.0 + 0.02 * nrm(ks[13], (DEPTH, QK_W)),
        "w_out": nrm(ks[14], (DEPTH, MIX_W, D_MODEL)) * MIX_W ** -0.5,
        "final_g": 1.0 + 0.02 * nrm(ks[15], (D_MODEL,)),
    }

def reference(x_prompt, x_sample, cache_k, cache_v, c, c_ctx, norm_g, w_mod, b_mod,
              w_in, conv_w, conv_b, lam_vec, subln_g, w_out, final_g):
    xc = x_prompt
    sc = jax.nn.silu(c_ctx)
    ks, vs = [], []
    for l in range(DEPTH):
        mod = sc @ w_mod[l] + b_mod[l]
        xc, kl, vl = _layer(xc, mod, norm_g[l], w_in[l], conv_w[l], conv_b[l],
                            lam_vec[l], subln_g[l], w_out[l], l, None, None)
        ks.append(kl)
        vs.append(vl)
    y_prompt = _rmsnorm(xc, final_g)
    new_k = jnp.stack(ks, axis=1)
    new_v = jnp.stack(vs, axis=1)

    n = x_sample.shape[1]
    rows = n // GRID_W
    row = jnp.repeat(jnp.arange(rows, dtype=jnp.int32), GRID_W)
    col = jnp.tile(jnp.arange(GRID_W, dtype=jnp.int32), rows)
    sl = jax.nn.silu(c)
    xl = x_sample
    for l in range(DEPTH):
        mod = (sl @ w_mod[l] + b_mod[l])[:, None, :]
        xl, _, _ = _layer(xl, mod, norm_g[l], w_in[l], conv_w[l], conv_b[l],
                          lam_vec[l], subln_g[l], w_out[l], l, (row, col),
                          (cache_k[:, l], cache_v[:, l]))
    y_sample = _rmsnorm(xl, final_g)
    return (y_prompt, y_sample, new_k, new_v)


_drawn_inputs = setup_inputs


def setup_inputs(seed=0):
    import zlib

    import numpy as np

    out = dict(_drawn_inputs(seed))
    spreads = {}
    factors = {'cache_k': 3.213,
     'cache_v': 3.012,
     'conv_b': 6.569,
     'lam_vec': 4.213,
     'subln_g': 7.908,
     'final_g': 2.802}
    for name, (base, spread) in spreads.items():
        noise = np.random.default_rng([zlib.crc32(name.encode()), seed]).standard_normal(out[name].shape)
        drawn = base * np.exp(spread * noise) if base else spread * noise
        out[name] = __import__('jax').numpy.asarray(drawn.astype(out[name].dtype))
    for name, factor in factors.items():
        out[name] = (out[name] * factor).astype(out[name].dtype)
    return out
```

```python
from contextlib import ExitStack
import math

import numpy as np

import concourse.bass as bass
from concourse import mybir

F32 = mybir.dt.float32
F32R = mybir.dt.float32r
BF16 = mybir.dt.bfloat16
ACT = mybir.ActivationFunctionType
ALU = mybir.AluOpType
AX_X = mybir.AxisListType.X

P = 128
D = 1024
KT = D // P
DEPTH = 2
NS = 2048
NP = 256
NTOK = NS + NP
TILES = NTOK // P
PAST = 512
G = 256
NG = NTOK // G
HEADS = 4
HD = 64
QKW = 2 * HD
AW = HEADS * QKW
FW = 256
CW = 256
WT = 2 * FW + 4 * CW
WN = 4 * AW
MT = WT // P
KEYS = PAST + NS
KEYS_A = 3 * 512
KTILES = KEYS // P
HEAD_TILES = NS // P
EPS = 1e-6
NH = NS // 2
SCALE = HD ** -0.5
GRID_W = 64

T_ORDER = [("fa", 0), ("fa", 1), ("ga", 0), ("ga", 1), ("cg", 0), ("hc", 0), ("gb", 0), ("bg", 0),
           ("cg", 1), ("hc", 1), ("gb", 1), ("bg", 1)]
T_COLUMN = {"fa": 0, "ga": FW, "bg": 2 * FW, "cg": 2 * FW + CW, "hc": 2 * FW + 2 * CW, "gb": 2 * FW + 3 * CW}
T_ACT = [m for m, (w, _) in enumerate(T_ORDER) if w not in ("hc", "bg")]
T_DVE = [m for m, (w, _) in enumerate(T_ORDER) if w in ("hc", "bg")]
T_BANKS = 6
T_FILL_AFTER = {3: 0, 5: 1, 7: 2, 9: 3}
N_FILL_AFTER = {0: 0, 1: 1, 4: 2, 5: 3}
A_ORDER = [("q", 0), ("t", 0), ("t", 1), ("q", 1), ("v", 0), ("t", 2), ("v", 1), ("q", 2), ("t", 3), ("v", 2),
           ("t", 4), ("q", 3), ("v", 3), ("v", 4)]


def backbone(nc, ins, y_all, new_k, new_v):
    es = ExitStack()
    with es:
        def scratch(name, shape):
            return nc.dram_tensor(name, shape, F32, kind="Internal").ap()

        x_scr = scratch("x_scr", (NTOK, D))
        fa_scr = scratch("fa_scr", (NG, P, 2, G))
        sga_scr = scratch("sga_scr", (NG, P, 2, G))
        yt_scr = scratch("yt_scr", (P, 4, NTOK))
        q_scr = scratch("q_scr", (TILES, P, 8, 2, P))
        k_scr = scratch("k_scr", (P, 8, KEYS + NP))
        v_scr = scratch("v_scr", (NTOK, AW))
        sgc_scr = scratch("sgc_scr", (NTOK, AW))
        o_scr = scratch("o_scr", (NTOK, AW))

        def keep(name, shape, dt=F32):
            return es.enter_context(nc.sbuf_tensor(name, shape, dt))

        id_sb = keep("id_sb", [P, P])
        ones = keep("ones", [P, P])
        cond_in = keep("cond_in", [P, KT, 2])
        cond_act = keep("cond_act", [P, KT, 2])
        mod = keep("mod", [P, 24, 2])
        bmod_sb = keep("bmod_sb", [P, DEPTH, 24])
        ng_sb = keep("ng_sb", [P, DEPTH, KT])
        one_scale = keep("one_scale", [P, KT, 2])
        gate_row = keep("gate_row", [P, 2, D])
        sqsum = keep("sqsum", [P, 2])
        meansq = keep("meansq", [P, 2])
        rstd = keep("rstd", [P, TILES])
        neg_half = keep("neg_half", [P, 4])
        conv_sb = keep("conv_sb", [P, DEPTH, 2, 4])
        lam_in = keep("lam_in", [P, 4, HD])
        lam_pr = keep("lam_pr", [P, 2, HD])
        lam_sum = keep("lam_sum", [P, 2])
        lam_exp = keep("lam_exp", [P, 2])
        lam = keep("lam", [P, 1])

        def region(prefix, shapes):
            with ExitStack() as st:
                return {n: st.enter_context(nc.sbuf_tensor(prefix + n, s, d)) for n, s, d in shapes}

        norm_bufs = [("xt0", [P, D], F32), ("xt1", [P, D], F32), ("hf", [P, 2, 4, P], F32),
                     ("hh0", [P, KT, G], F32R), ("hh1", [P, KT, G], F32R),
                     ("hl0", [P, KT, G], F32R), ("hl1", [P, KT, G], F32R)]
        M = region("m_", [("w0", [P, 3 * D], F32), ("w1", [P, 3 * D], F32), ("dg", [P, 2 * KT, P], F32)])
        with ExitStack() as conv_stack:
            z = conv_stack.enter_context(nc.sbuf_tensor("conv_z", [P, 2, NTOK], F32))
            bgs = conv_stack.enter_context(nc.sbuf_tensor("conv_bgs", [P, 2, NTOK], F32))
            T = region("t_", norm_bufs + [
                ("junk", [P, D], BF16), ("wh", [P, KT, WT], F32R), ("wl", [P, KT, WT], F32R),
                ("ws0", [P, WT // 2], F32), ("ws1", [P, WT // 2], F32),
                ("fa", [P, 2, G], F32), ("ga", [P, 2, G], F32), ("cg", [P, G], F32), ("gb", [P, G], F32)])
            F = region("f_", [
                ("fa", [P, 2, NTOK], F32), ("sga", [P, 2, NTOK], F32), ("ya", [P, 2, NTOK], F32),
                ("fe", [P, 2, NH + 1], F32), ("fo", [P, 2, NH], F32), ("pq", [P, 8, 2 * FW], F32),
                ("plast", [1, FW], F32), ("pqp", [P, 2, 2 * FW], F32),
                ("cc", [P, 2, FW], F32), ("cs", [P, 2, FW], F32),
                ("ct", [P, 8, 512], F32), ("st", [P, 8, 512], F32), ("sr", [1, 512], F32),
                ("scol", [P, 1], F32), ("pc", [P, 2, NP], F32), ("ps", [P, 2, NP], F32),
                ("sq0", [P, 512], F32), ("sq1", [P, 512], F32), ("cy", [P, NTOK], F32)])
        N = region("n_", norm_bufs + [
            ("wh", [P, KT, WN], F32R), ("wl", [P, KT, WN], F32R),
            ("rope", [P, 2, HD], F32), ("m1", [P, AW], F32), ("m2", [P, AW], F32),
            ("vs", [P, AW], F32), ("gs", [P, AW], F32),
            ("dup", [P, 8, 2, HD], F32), ("qst", [P, 4, 2, P], F32), ("kst", [P, 4, P], F32)])
        A = region("a_", [
            ("kt0", [P, 2, KEYS], F32R), ("kt1", [P, 2, KEYS], F32R), ("v0", [P, KTILES, P], F32), ("v1", [P, KTILES, P], F32),
            ("q0", [P, 2, 2, P], F32R), ("q1", [P, 2, 2, P], F32R),
            ("e0", [P, 2, KEYS], F32), ("e1", [P, 2, KEYS], F32), ("d0", [P, KEYS], F32), ("d1", [P, KEYS], F32),
            ("dt", [P, 5, 4 * P], F32), ("os0", [P, P], F32), ("os1", [P, P], F32),
            ("s0", [P, 24], F32), ("s1", [P, 24], F32),
            ])
        B = region("b_", [
            ("kt", [P, 8, NP], F32R), ("v", [P, 2, AW], F32), ("q", [P, 8, 2, P], F32R),
            ("e", [P, 8, NP], F32), ("d", [P, 4, NP], F32), ("dt", [P, 8, P], F32), ("os", [P, AW], F32),
            ("mx", [P, 8], F32), ("nb", [P, 8], F32), ("ls", [P, 8], F32), ("rl", [P, 8], F32),
            ("c", [P, 4], F32), ("nr", [P, 4], F32)])
        O = region("o_", [
            ("wh", [P, KT, D], F32R), ("wl", [P, KT, D], F32R), ("ws0", [P, D], F32), ("ws1", [P, D], F32),
            ("subln", [P, P], F32), ("fg", [P, D], F32), ("junk", [P, D], BF16), ("junk2", [P, D], BF16),
            ("o0", [P, AW], F32), ("o1", [P, AW], F32), ("g0", [P, AW], F32), ("g1", [P, AW], F32),
            ("x0", [P, D], F32), ("x1", [P, D], F32), ("yf0", [P, KT, P], F32), ("yf1", [P, KT, P], F32),
            ("yh0", [P, KT, P], F32R), ("yh1", [P, KT, P], F32R), ("yl0", [P, KT, P], F32R), ("yl1", [P, KT, P], F32R),
            ("on", [P, AW], F32), ("on2", [P, AW], F32), ("on3", [P, AW], F32),
            ("t0", [P, D], F32), ("t1", [P, D], F32), ("xn0", [P, D], F32), ("xn1", [P, D], F32),
            ("y0", [P, D], F32), ("y1", [P, D], F32),
            ("sm0", [P, 16], F32), ("sm1", [P, 16], F32)])

        psum = es.enter_context(nc.psum_tensor("psum", [P, 8, 512], F32))

        sems = {}

        def S(name):
            if name not in sems:
                sems[name] = es.enter_context(nc.semaphore(name))
            return sems[name]

        def upto(value):
            if isinstance(value, int):
                return max(value, 0)
            assert value.min_val > 0
            return value

        STAGES = 6

        def stage_begin(eng, l, n):
            eng.wait_ge(S("stage_left"), upto(5 * (STAGES * l + n)))

        def stage_end(eng):
            eng.drain().then_inc(S("stage_left"), 1)

        def groups(eng, first, pair, last):
            first(0, 0)
            with eng.Fori(0, 3) as m:
                pair(2 * m + 1, 1)
                pair(2 * m + 2, 0)
            pair(7, 1)
            last(8, 0)

        def pairs(eng, body):
            body(0)
            with eng.Fori(1, TILES // 2 - 1) as m:
                body(m)

        def head_pairs(eng, h, body, last=HEAD_TILES // 2):
            first = 3 if h == 0 else 1
            for m in range(1, first):
                body(m)
            with eng.Fori(first, last) as m:
                body(m)


        def x_load(sp, p, R, l, i):
            for s in (0, 1):
                if not (isinstance(i, int) and i == 0):
                    sp.wait_ge(S(p + "tr"), upto(l * 4 * NG + 4 * (i - 1) + 2 * s + 2))
                src = ins["x_all"] if l == 0 else x_scr
                r0 = i * G + s * P
                sp.dma_start(R[f"xt{s}"][:], src[bass.ds(r0, P), :]).then_inc(S(p + f"x{s}"), 16)

        def norm_act(act, p, R, l, i):
            for s in (0, 1):
                act.wait_ge(S(p + f"x{s}"), 16 * (l * NG + i + 1))
                if s == 0:
                    act.wait_ge(S(p + "ms"), upto(l * NG + i))
                act.wait_ge(S(p + "sq"), upto(2 * (l * NG + i) + s))
                nc.scalar.activation(R["junk"][:], R[f"xt{s}"][:], ACT.Square, accum_out=sqsum[:, s:s + 1]).then_inc(S(p + "sq"), 1)

        def norm_pool(pool, p, l, i):
            pool.wait_ge(S(p + "ms"), l * NG + i + 1)
            nc.gpsimd.tensor_tensor(rstd[:, bass.ds(2 * i, 2)], meansq[:], neg_half[:, 0:2], ALU.pow).then_inc(S(p + "rs"), 1)

        def norm_dve(dve, p, R, l, i, stats):
            if stats:
                dve.wait_ge(S(p + "sq"), 2 * (l * NG + i + 1))
                dve.wait_ge(S(p + "rs"), upto(l * NG + i))
                nc.vector.tensor_scalar(meansq[:], sqsum[:], 1.0 / D, EPS, ALU.mult, ALU.add).then_inc(S(p + "ms"), 1)
                dve.wait_ge(S(p + "rs"), l * NG + i + 1)
            for s in (0, 1):
                dve.wait_ge(S(p + f"x{s}"), 16 * (l * NG + i + 1))
                xt = R[f"xt{s}"]
                nc.vector.tensor_scalar(xt[:], xt[:], rstd[:, bass.ds(2 * i + s, 1)], None, ALU.mult).then_inc(S(p + "xn"), 1)

        def fill_pe(pe, p, R, l, i, q):
            s, kh = q // 2, q % 2
            n = l * 4 * NG + 4 * i + q
            pe.wait_ge(S(p + "xn"), l * 2 * NG + 2 * i + s + 1)
            if not (isinstance(i, int) and i == 0 and q < 2):
                pe.wait_ge(S(p + "ev"), upto(n - 1))
            for kk in range(4):
                k = 4 * kh + kk
                last = nc.tensor.transpose(psum[:, 6 + q % 2, kk * P:(kk + 1) * P], R[f"xt{s}"][:, k * P:(k + 1) * P], id_sb[:])
            last.then_inc(S(p + "tr"), 1)

        def fill_act(act, p, R, l, i, q):
            kh = q % 2
            g = 1 if isinstance(i, int) and i == NG - 1 else 0
            n = l * 4 * NG + 4 * i + q
            act.wait_ge(S(p + "tr"), n + 1)
            if not (isinstance(i, int) and i == 0 and q < 2):
                act.wait_ge(S(p + "lo"), upto(n - 1))
            for kk in range(4):
                k = 4 * kh + kk
                last = nc.scalar.activation(R["hf"][:, q % 2, kk, :], psum[:, 6 + q % 2, kk * P:(kk + 1) * P], ACT.Identity,
                                            bias=mod[:, k, g:g + 1], scale=one_scale[:, k, g:g + 1])
            last.then_inc(S(p + "ev"), 1)

        def fill_dve(dve, p, R, l, i, b, q, mm_per_group):
            s, kh = q // 2, q % 2
            n = l * 4 * NG + 4 * i + q
            dve.wait_ge(S(p + "ev"), n + 1)
            if not (isinstance(i, int) and i == 0):
                dve.wait_ge(S(p + "mm"), upto(mm_per_group * (l * NG + i - 1)))
            nc.vector.tensor_copy(R[f"hh{b}"][:, 4 * kh:4 * kh + 4, s * P:(s + 1) * P], R["hf"][:, q % 2]).then_inc(S(p + "hi"), 1)

        def fill_pool(pool, p, R, l, i, b, q, mm_per_group):
            s, kh = q // 2, q % 2
            pool.wait_ge(S(p + "hi"), l * 4 * NG + 4 * i + q + 1)
            hi = R[f"hh{b}"][:, 4 * kh:4 * kh + 4, s * P:(s + 1) * P]
            nc.gpsimd.tensor_tensor(R[f"hl{b}"][:, 4 * kh:4 * kh + 4, s * P:(s + 1) * P], R["hf"][:, q % 2], hi.bitcast(F32),
                                    ALU.subtract).then_inc(S(p + "lo"), 1)

        def weights_sp(sp, p, l, src, stage, chunks, width):
            for n in range(KT * chunks):
                k, c = n // chunks, n % chunks
                sp.wait_ge(S(p + "wl"), upto(l * KT * chunks + n - 1 if n >= 2 else 0))
                sp.dma_start(stage[n % 2][:], src[l, k * P:(k + 1) * P, c * width:(c + 1) * width]).then_inc(S(p + f"w{n % 2}"), 16)

        def weights_act(act, p, l, stage, hi, chunks, width):
            for n in range(KT * chunks):
                k, c = n // chunks, n % chunks
                act.wait_ge(S(p + f"w{n % 2}"), 16 * (l * KT * chunks // 2 + n // 2 + 1))
                nc.scalar.activation(hi[:, k, c * width:(c + 1) * width], stage[n % 2][:], ACT.Copy).then_inc(S(p + "wh"), 1)

        def weights_dve(dve, p, l, stage, hi, lo, chunks, width):
            for n in range(KT * chunks):
                k, c = n // chunks, n % chunks
                dve.wait_ge(S(p + "wh"), l * KT * chunks + n + 1)
                nc.vector.tensor_tensor(lo[:, k, c * width:(c + 1) * width], stage[n % 2][:],
                                        hi[:, k, c * width:(c + 1) * width].bitcast(F32), ALU.subtract).then_inc(S(p + "wl"), 1)

        def split_products(out, terms, inc=None):
            n = len(terms)
            for j, ((wh, wl), (xh, xl)) in enumerate(terms):
                nc.tensor.matmul(out, wh, xh, start=(j == 0), stop=False)
                nc.tensor.matmul(out, wh, xl, start=False, stop=False)
                last = nc.tensor.matmul(out, wl, xh, start=False, stop=(j == n - 1))
            return last

        T_STAGE = [T["ws0"], T["ws1"]]
        N_STAGE = [N["m1"], N["m2"]]
        O_STAGE = [O["ws0"], O["ws1"]]

        block = es.enter_context(nc.Block())

        @block.sync
        def _(sp):
            for dst, name in ((id_sb[:], "ident"), (cond_in[:], "cond"), (bmod_sb[:], "b_mod"), (ng_sb[:], "norm_g"), (conv_sb[:], "conv_wb")):
                sp.dma_start(dst, ins[name]).then_inc(S("consts"), 16)
            for l in range(DEPTH):
                stage_begin(sp, l, 0)
                sp.dma_start(lam_in[:], ins["lam_vec"][l:l + 1].partition_broadcast(P)).then_inc(S("lam_in"), 16)
                for k in range(KT):
                    sp.wait_ge(S("mod_mm"), upto(l * KT + k - 1 if k >= 2 else 0))
                    sp.dma_start(M[f"w{k % 2}"][:], ins["w_mod"][l, k * P:(k + 1) * P, :]).then_inc(S(f"mod_w{k % 2}"), 16)
                sp.wait_ge(S(f"mod_w{1}"), upto(16 * (l + 1) * KT // 2))
                sp.wait_ge(S("lam_in"), 16 * (l + 1))
                stage_end(sp)

                stage_begin(sp, l, 1)
                x_load(sp, "t_", T, l, 0)
                weights_sp(sp, "t_", l, ins["w_in_t"], T_STAGE, 2, WT // 2)

                def t_group(i, b, nxt=True):
                    if nxt:
                        x_load(sp, "t_", T, l, i + 1)
                    for j, (w, scr) in enumerate((("fa", fa_scr), ("ga", sga_scr))):
                        sp.wait_ge(S("t_act"), upto(len(T_ACT) * (l * NG + i) + 2 * j + 2))
                        sp.dma_start(scr[bass.ds(i, 1)].rearrange("g p j n -> (g p) j n"), T[w][:]).then_inc(S("t_st_" + w), 16)
                groups(sp, t_group, t_group, lambda i, b: t_group(i, b, False))
                sp.wait_ge(S("t_st_fa"), upto(16 * (l + 1) * NG))
                sp.wait_ge(S("t_st_ga"), upto(16 * (l + 1) * NG))
                stage_end(sp)

                stage_begin(sp, l, 2)
                def by_group(dst, scr):
                    return [(dst[:, j].rearrange("p (g n) -> p g n", g=NG), scr[:, :, j].rearrange("g p n -> p g n")) for j in (0, 1)]
                for dst, src in by_group(F["fa"], fa_scr) + [(F["cc"][:], ins["chan_cos"]), (F["cs"][:], ins["chan_sin"])]:
                    sp.dma_start(dst, src).then_inc(S("f_in"), 16)
                for dst, src in ((F["ct"], ins["seq_cos"][0]), (F["st"], ins["seq_sin"][0]), (F["sr"], ins["sign_row"]),
                                 (F["scol"], ins["sign_col"]), (F["pc"], ins["prompt_cos"]), (F["ps"], ins["prompt_sin"])):
                    sp.dma_start(dst[:], src).then_inc(S("f_tab"), 16)
                for dst, src in by_group(F["sga"], sga_scr):
                    sp.dma_start(dst, src).then_inc(S("f_sga"), 16)
                sp.wait_ge(S("f_sd"), upto(l * 4 + 2))
                for dst, src in ((F["ct"], ins["seq_cos"][1]), (F["st"], ins["seq_sin"][1])):
                    sp.dma_start(dst[:], src).then_inc(S("f_tab2"), 16)
                for j in (0, 1):
                    sp.wait_ge(S("cv_y"), l * 2 + j + 1)
                    sp.dma_start(yt_scr[:, 2 + j, :], F["cy"][:]).then_inc(S("cv_st"), 16)
                sp.wait_ge(S("f_ya"), l + 1)
                sp.dma_start(yt_scr[:, 0:2, :], F["ya"][:]).then_inc(S("f_st"), 16)
                sp.wait_ge(S("f_st"), 16 * (l + 1))
                sp.wait_ge(S("cv_st"), 32 * (l + 1))
                stage_end(sp)

                stage_begin(sp, l, 3)
                x_load(sp, "n_", N, l, 0)
                weights_sp(sp, "n_", l, ins["w_in_n"], N_STAGE, 4, WN // 4)

                def k_store(fill, col, f):
                    sp.wait_ge(S("n_flo"), fill + 1)
                    sp.dma_start(k_scr[:, 4 * f:4 * f + 4, bass.ds(col, P)], N["kst"][:]).then_inc(S("n_kst"), 16)

                for t in range(PAST // P):
                    sp.wait_ge(S("n_wl"), upto((l + 1) * KT * 4))
                    sp.wait_ge(S("n_dup"), upto(l * 40 + t))
                    sp.dma_start(N["m1"][:], ins["cache_k"][l, t * P:(t + 1) * P, :]).then_inc(S("n_ck"), 16)
                    for f in (0, 1):
                        k_store(l * 80 + 2 * t + f, t * P, f)

                def n_group(i, b, nxt=True, new=False):
                    if nxt:
                        x_load(sp, "n_", N, l, i + 1)
                    for s in (0, 1):
                        tt = 2 * i + s
                        n = l * TILES + tt
                        sp.wait_ge(S("n_rope"), upto(l * TILES * 4 + 4 * tt))
                        sp.dma_start(N["rope"][:], ins["rope"][bass.ds(tt * P, P)]).then_inc(S("n_tab"), 16)
                        sp.wait_ge(S("n_vs"), n + 1)
                        sp.dma_start(v_scr[bass.ds(tt * P, P), :], N["vs"][:]).then_inc(S("n_vst"), 16)
                        if new:
                            sp.dma_start(new_v[l, s * P:(s + 1) * P, :], N["vs"][:]).then_inc(S("n_newv"), 16)
                        for f in (0, 1):
                            sp.wait_ge(S("n_flo"), l * 80 + 8 + 4 * tt + f + 1)
                            sp.dma_start(q_scr[bass.ds(tt, 1), :, 4 * f:4 * f + 4].rearrange("t p j c n -> p (t j) c n"), N["qst"][:]).then_inc(S("n_qst"), 16)
                        sp.wait_ge(S("n_gs"), n + 1)
                        sp.dma_start(sgc_scr[bass.ds(tt * P, P), :], N["gs"][:]).then_inc(S("n_gst"), 16)
                        if new:
                            sp.wait_ge(S("n_dup"), upto(l * 40 + 4 + 2 * tt + 2))
                            sp.dma_start(new_k[l, s * P:(s + 1) * P, :].rearrange("p (j d) -> p j d", j=8), N["dup"][:, :, 0, :]).then_inc(S("n_newk"), 16)
                        for f in (0, 1):
                            k_store(l * 80 + 8 + 4 * tt + 2 + f, tt * P + PAST, f)
                groups(sp, n_group, n_group, lambda i, b: n_group(i, b, False, True))
                sp.wait_ge(S("n_vst"), 16 * TILES * (l + 1))
                sp.wait_ge(S("n_gst"), 16 * TILES * (l + 1))
                sp.wait_ge(S("n_qst"), 16 * 2 * TILES * (l + 1))
                sp.wait_ge(S("n_kst"), 16 * 44 * (l + 1))
                sp.wait_ge(S("n_newv"), 32 * (l + 1))
                sp.wait_ge(S("n_newk"), 32 * (l + 1))
                stage_end(sp)

                stage_begin(sp, l, 4)
                U = l * 64

                def head_load(h):
                    hb = h % 2
                    if h >= 2:
                        sp.wait_ge(S("a_o"), upto(U + 16 * (h - 1)))
                    sp.dma_start(A[f"kt{hb}"][:].bitcast(F32), k_scr[:, 2 * h:2 * h + 2, 0:KEYS]).then_inc(S(f"a_k{hb}"), 16)
                    sp.dma_start(A[f"v{hb}"][:, 0:PAST // P, :], ins["cache_v"][l, :, h * P:(h + 1) * P].rearrange("(t p) d -> p t d", p=P)).then_inc(S(f"a_v{hb}"), 16)
                    sp.dma_start(A[f"v{hb}"][:, PAST // P:, :], v_scr[0:NS, h * P:(h + 1) * P].rearrange("(t p) d -> p t d", p=P)).then_inc(S(f"a_v{hb}"), 16)

                def q_load(h, t, b):
                    if not (isinstance(t, int) and h == 0 and t < 2):
                        sp.wait_ge(S("a_qk"), upto(4 * (U + 16 * h + t - 1)))
                    sp.dma_start(A[f"q{b}"][:].bitcast(F32), q_scr[bass.ds(t, 1), :, 2 * h:2 * h + 2].rearrange("t p j c n -> p (t j) c n")).then_inc(S(f"a_q{b}"), 16)

                def o_store(h, t, b):
                    sp.wait_ge(S("a_os"), U + 16 * h + t + 1)
                    sp.dma_start(o_scr[bass.ds(t * P, P), h * P:(h + 1) * P], A[f"os{b}"][:]).then_inc(S(f"a_st{b}"), 16)

                head_load(0)
                q_load(0, 0, 0)
                head_load(1)
                for h in range(HEADS):
                    for b in (0, 1):
                        q_load(h, 1 + b, 1 - b)
                        if h:
                            o_store(h - 1, 14 + b, b)
                    if 1 <= h < HEADS - 1:
                        head_load(h + 1)

                    def pair(m):
                        q_load(h, 2 * m + 1, 1)
                        o_store(h, 2 * m - 2, 0)
                        q_load(h, 2 * m + 2, 0)
                        o_store(h, 2 * m - 1, 1)
                    head_pairs(sp, h, pair, HEAD_TILES // 2 - 1)
                    q_load(h, 15, 1)
                    o_store(h, 12, 0)
                    if h < HEADS - 1:
                        q_load(h + 1, 0, 0)
                    o_store(h, 13, 1)
                o_store(HEADS - 1, 14, 0)
                o_store(HEADS - 1, 15, 1)
                for b in (0, 1):
                    sp.wait_ge(S(f"a_st{b}"), 16 * 32 * (l + 1))
                sp.wait_ge(S("a_o"), upto(U + 64))
                sp.wait_ge(S("a_os"), upto(U + 64))
                sp.dma_start(B["kt"][:].bitcast(F32), k_scr[:, :, KEYS:KEYS + NP]).then_inc(S("b_kv"), 16)
                sp.dma_start(B["v"][:], v_scr[NS:NTOK, :].rearrange("(t p) d -> p t d", p=P)).then_inc(S("b_kv"), 16)
                for t in (0, 1):
                    sp.wait_ge(S("b_qk"), upto(2 * l + t))
                    sp.dma_start(B["q"][:].bitcast(F32), q_scr[NS // P + t]).then_inc(S("b_q"), 16)
                    sp.wait_ge(S("b_os"), 2 * l + t + 1)
                    sp.dma_start(o_scr[NS + t * P:NS + (t + 1) * P, :], B["os"][:]).then_inc(S("b_st"), 16)
                sp.wait_ge(S("b_st"), 32 * (l + 1))
                stage_end(sp)

                stage_begin(sp, l, 5)
                sp.dma_start(O["subln"][:], ins["subln_g"][l:l + 1].partition_broadcast(P)).then_inc(S("o_c"), 16)
                sp.dma_start(O["fg"][:], ins["final_g"].partition_broadcast(P)).then_inc(S("o_c"), 16)

                def o_load(t, b):
                    r = bass.ds(t * P, P)
                    if not (isinstance(t, int) and t < 2):
                        sp.wait_ge(S("o_mm"), upto(2 * (l * TILES + t - 1)))
                        sp.wait_ge(S("o_xn"), upto(l * TILES + t - 1))
                    for dst, src in ((O[f"o{b}"][:], o_scr[r, :]), (O[f"g{b}"][:], sgc_scr[r, :]),
                                     (O[f"yf{b}"][:, 0:4, :], yt_scr[:, :, r]), (O[f"x{b}"][:], (ins["x_all"] if l == 0 else x_scr)[r, :])):
                        sp.dma_start(dst, src).then_inc(S(f"o_in{b}"), 16)
                o_load(0, 0)
                o_load(1, 1)
                for k in range(KT):
                    sp.wait_ge(S("o_wl"), upto(l * KT + k - 1 if k >= 2 else 0))
                    sp.dma_start(O_STAGE[k % 2][:], ins["w_out"][l, k * P:(k + 1) * P, :]).then_inc(S(f"o_w{k % 2}"), 16)

                def o_out(t, b):
                    r = bass.ds(t * P, P)
                    if l == DEPTH - 1:
                        sp.wait_ge(S("o_y"), t + 1)
                        sp.dma_start(y_all[r, :], O[f"y{b}"][:]).then_inc(S(f"o_st{b}"), 16)
                    else:
                        sp.wait_ge(S("o_xn"), l * TILES + t + 1)
                        sp.dma_start(x_scr[r, :], O[f"xn{b}"][:]).then_inc(S(f"o_st{b}"), 16)

                def o_pair(m):
                    for b in (0, 1):
                        o_load(2 * m + 2 + b, b)
                        o_out(2 * m + b, b)
                pairs(sp, o_pair)
                o_out(TILES - 2, 0)
                o_out(TILES - 1, 1)
                for b in (0, 1):
                    sp.wait_ge(S(f"o_st{b}"), upto(16 * (l + 1) * TILES // 2))
                stage_end(sp)

        @block.tensor
        def _(pe):
            pe.wait_ge(S("consts"), 16 * 5)
            pe.wait_ge(S("ones_set"), 3)
            for l in range(DEPTH):
                stage_begin(pe, l, 0)
                pe.wait_ge(S("cond_act"), 1)
                pe.wait_ge(S("mod_zero"), l + 1)
                for k in range(KT):
                    pe.wait_ge(S(f"mod_w{k % 2}"), 16 * (l * KT // 2 + k // 2 + 1))
                    for m in range(24):
                        last = nc.tensor.matmul(psum[:, 0, 2 * m:2 * m + 2], M[f"w{k % 2}"][:, m * P:(m + 1) * P], cond_act[:, k, :],
                                                start=False, stop=(k == KT - 1), skip_group_check=True)
                    last.then_inc(S("mod_mm"), 1)
                pe.wait_ge(S("mod_dg"), l + 1)
                for g in (0, 1):
                    for k in range(KT):
                        last = nc.tensor.matmul(psum[:, 1 + 2 * g + k // 4, (k % 4) * P:(k % 4 + 1) * P], ones[:], M["dg"][:, g * KT + k, :], start=True, stop=True)
                last.then_inc(S("mod_gate"), 1)
                stage_end(pe)

                stage_begin(pe, l, 1)
                for q in range(4):
                    fill_pe(pe, "t_", T, l, 0, q)
                pe.wait_ge(S("t_wl"), upto((l + 1) * KT * 2))

                def t_group(i, b, nxt=True):
                    pe.wait_ge(S("t_lo"), 4 * (l * NG + i + 1))
                    for m, (w, j) in enumerate(T_ORDER):
                        c = T_COLUMN[w] + j * P
                        first = isinstance(i, int) and i == 0
                        if m >= T_BANKS or not first:
                            o = (m - T_BANKS) % MT
                            back = l * NG + i - (m < T_BANKS)
                            if o in T_ACT:
                                pe.wait_ge(S("t_act"), len(T_ACT) * back + T_ACT.index(o) + 1)
                            else:
                                pe.wait_ge(S("t_dve"), len(T_DVE) * back + T_DVE.index(o) + 1)
                        split_products(psum[:, m % T_BANKS, 0:G],
                                       [((T["wh"][:, k, c:c + P], T["wl"][:, k, c:c + P]), (T[f"hh{b}"][:, k, :], T[f"hl{b}"][:, k, :]))
                                        for k in range(KT)]).then_inc(S("t_mm"), 1)
                        if nxt and m in T_FILL_AFTER:
                            fill_pe(pe, "t_", T, l, i + 1, T_FILL_AFTER[m])
                groups(pe, t_group, t_group, lambda i, b: t_group(i, b, False))
                stage_end(pe)

                stage_begin(pe, l, 2)
                pe.wait_ge(S("f_in"), 64 * (l + 1))
                pe.wait_ge(S("f_fold"), l + 1)
                for t in range(8):
                    pe.wait_ge(S("f_pq"), upto(l * 11 + t - 1 if t >= 2 else 0))
                    for part, (seq, tab) in enumerate(((F["fe"], F["cc"]), (F["fo"], F["cs"]))):
                        for j in (0, 1):
                            last = nc.tensor.matmul(psum[:, t % 2, part * FW:(part + 1) * FW], seq[:, j, t * P:(t + 1) * P], tab[:, j, :], start=(j == 0), stop=(j == 1))
                    last.then_inc(S("f_ch"), 1)
                for j in (0, 1):
                    last = nc.tensor.matmul(psum[0:1, 2, 0:FW], F["fe"][:, j, NH:NH + 1], F["cc"][:, j, :], start=(j == 0), stop=(j == 1))
                last.then_inc(S("f_ch"), 1)
                for t in (0, 1):
                    for part, tab in enumerate((F["cc"], F["cs"])):
                        for j in (0, 1):
                            last = nc.tensor.matmul(psum[:, 3 + t, part * FW:(part + 1) * FW], F["fa"][:, j, NS + t * P:NS + (t + 1) * P], tab[:, j, :], start=(j == 0), stop=(j == 1))
                    last.then_inc(S("f_ch"), 1)
                pe.wait_ge(S("f_tab"), 96 * (l + 1))
                pe.wait_ge(S("f_pq"), upto(l * 11 + 9))
                n = l * 4
                for kc in (0, 1):
                    if kc:
                        pe.wait_ge(S("f_tab2"), 32 * (l + 1))
                    for ct in (0, 1):
                        c = ct * P
                        pe.wait_ge(S("f_out"), upto(n - 1 if 2 * kc + ct >= 2 else 0))
                        cb, sb_ = (5, 6) if ct == 0 else (7, 2)
                        for t in range(8):
                            nc.tensor.matmul(psum[:, cb, :], F["pq"][:, t, c:c + P], F["ct"][:, t, :], start=(t == 0), stop=False)
                        nc.tensor.matmul(psum[:, cb, :], F["plast"][0:1, c:c + P], F["sr"][0:1, :], start=False, stop=True)
                        for t in range(8):
                            last = nc.tensor.matmul(psum[:, sb_, :], F["pq"][:, t, FW + c:FW + c + P], F["st"][:, t, :], start=(t == 0), stop=(t == 7))
                        last.then_inc(S("f_sd"), 1)
                        n += 1
                for ct in (0, 1):
                    c = ct * P
                    for t in range(8):
                        nc.tensor.matmul(psum[:, 0, ct:ct + 1], F["pq"][:, t, c:c + P], F["scol"][:, 0:1], start=(t == 0), stop=False)
                    last = nc.tensor.matmul(psum[:, 0, ct:ct + 1], F["plast"][0:1, c:c + P], ones[0:1, 0:1], start=False, stop=True)
                last.then_inc(S("f_nyq"), 1)
                pe.wait_ge(S("f_pq"), upto(l * 11 + 11))
                for ct in (0, 1):
                    c = ct * P
                    for t in (0, 1):
                        nc.tensor.matmul(psum[:, 1, ct * NP:(ct + 1) * NP], F["pqp"][:, t, c:c + P], F["pc"][:, t, :], start=(t == 0), stop=False)
                        last = nc.tensor.matmul(psum[:, 1, ct * NP:(ct + 1) * NP], F["pqp"][:, t, FW + c:FW + c + P], F["ps"][:, t, :], start=False, stop=(t == 1))
                last.then_inc(S("f_nyq"), 1)
                stage_end(pe)

                stage_begin(pe, l, 3)
                for q in range(4):
                    fill_pe(pe, "n_", N, l, 0, q)

                def dup_fill(n, dups, f):
                    pe.wait_ge(S("n_dup"), upto(dups))
                    if not (isinstance(n, int) and n < 2):
                        pe.wait_ge(S("n_fhi"), upto(n - 1))
                        pe.wait_ge(S("n_flo"), upto(n - 1))
                    for j in range(4):
                        last = nc.tensor.transpose(psum[:, 4 + f, j * P:(j + 1) * P], N["dup"][:, 4 * f + j].rearrange("p a d -> p (a d)"), id_sb[:])
                    last.then_inc(S("n_ftr"), 1)

                for t in range(PAST // P):
                    for f in (0, 1):
                        dup_fill(l * 80 + 2 * t + f, l * 40 + t + 1, f)
                pe.wait_ge(S("n_wl"), upto((l + 1) * KT * 4))

                def n_group(i, b, nxt=True):
                    pe.wait_ge(S("n_lo"), 4 * (l * NG + i + 1))
                    first = isinstance(i, int) and i == 0
                    for s in (0, 1):
                        tt = 2 * i + s
                        for n in range(4):
                            if s or not first:
                                if n < 2:
                                    pe.wait_ge(S("n_rope"), upto(4 * (l * TILES + tt - 1) + 2 * n + 2))
                                else:
                                    pe.wait_ge(S("n_vs" if n == 2 else "n_gs"), upto(l * TILES + tt))
                            split_products(psum[:, n, :],
                                           [((N[f"hh{b}"][:, k, s * P:(s + 1) * P], N[f"hl{b}"][:, k, s * P:(s + 1) * P]),
                                             (N["wh"][:, k, n * AW:(n + 1) * AW], N["wl"][:, k, n * AW:(n + 1) * AW])) for k in range(KT)]).then_inc(S("n_mm"), 1)
                            if n >= 2:
                                for f in (0, 1):
                                    dup_fill(l * 80 + 8 + 4 * tt + 2 * (n - 2) + f, l * 40 + 4 + 2 * tt + n - 1, f)
                            if nxt and 4 * s + n in N_FILL_AFTER:
                                fill_pe(pe, "n_", N, l, i + 1, N_FILL_AFTER[4 * s + n])
                groups(pe, n_group, n_group, lambda i, b: n_group(i, b, False))
                stage_end(pe)

                stage_begin(pe, l, 4)
                U = l * 64

                def scores(h, t, b, part):
                    half, kp = part // 2, part % 2
                    u = U + 16 * h + t
                    if part == 0:
                        pe.wait_ge(S(f"a_q{b}"), 16 * (l * 32 + (8 * h + (t - b) // 2 if isinstance(t, int) else 8 * h + t_pair[0]) + 1))
                        if isinstance(t, int) and t == 0:
                            pe.wait_ge(S(f"a_k{h % 2}"), 16 * (2 * l + h // 2 + 1))
                    if not (isinstance(t, int) and 16 * h + t == 0 and part < 2):
                        pe.wait_ge(S("a_exp"), upto(4 * u + part - 1))
                    q = A[f"q{b}"]
                    kt = A[f"kt{h % 2}"]
                    for bank in ((0, 1, 2), (3, 4))[kp]:
                        keys = kt[:, half, bank * 512:(bank + 1) * 512]
                        nc.tensor.matmul(psum[:, bank, :], q[:, half, 0, :], keys, start=True, stop=False)
                        last = nc.tensor.matmul(psum[:, bank, :], q[:, half, 1, :], keys, start=False, stop=True)
                    last.then_inc(S("a_qk"), 1)

                def turn(u, b, f):
                    if f == 0:
                        pe.wait_ge(S("a_dA"), u + 1)
                    if f == 3:
                        pe.wait_ge(S("a_dB"), u + 1)
                    if f >= 2:
                        if f % 2 == 0:
                            pe.wait_ge(S("a_tevS"), 3 * u + f // 2)
                        else:
                            pe.wait_ge(S("a_tevV"), 2 * u + 1)
                    elif not (isinstance(u, int) and u == 0):
                        if f == 0:
                            pe.wait_ge(S("a_tevV"), 2 * u)
                        else:
                            pe.wait_ge(S("a_tevS"), 3 * u)
                    for j in range(4):
                        kt_ = 4 * f + j
                        last = nc.tensor.transpose(psum[:, 5 + (b + f) % 2, j * P:(j + 1) * P], A[f"d{b}"][:, kt_ * P:(kt_ + 1) * P], id_sb[:])
                    last.then_inc(S("a_tr"), 1)

                def values(h, u, f):
                    if f == 0:
                        if not (isinstance(u, int) and u == 0):
                            pe.wait_ge(S("a_os"), upto(u))
                        pe.wait_ge(S(f"a_v{h % 2}"), 32 * (2 * l + h // 2 + 1))
                    if f % 2 == 0:
                        pe.wait_ge(S("a_tevS"), 3 * u + f // 2 + 1)
                    else:
                        pe.wait_ge(S("a_tevV"), 2 * u + f // 2 + 1)
                    for j in range(4):
                        last = nc.tensor.matmul(psum[:, 7, 0:P], A["dt"][:, f, j * P:(j + 1) * P], A[f"v{h % 2}"][:, 4 * f + j, :],
                                                start=(f == 0 and j == 0), stop=(f == 4 and j == 3))
                    if f == 4:
                        last.then_inc(S("a_o"), 1)

                t_pair = [0]

                def unit(h, t, b, prev):
                    for what, n in A_ORDER:
                        if what == "q":
                            scores(h, t, b, n)
                        elif prev is None:
                            continue
                        elif what == "t":
                            turn(prev[1], b, n)
                        else:
                            values(prev[0], prev[1], n)

                for h in range(HEADS):
                    for b in (0, 1):
                        t_pair[0] = 0
                        unit(h, b, b, (h - 1, U + 16 * h - 2 + b) if h else None)

                    def pair(m):
                        t_pair[0] = m
                        for b in (0, 1):
                            unit(h, 2 * m + b, b, (h, U + 16 * h + 2 * m - 2 + b))
                    head_pairs(pe, h, pair)
                for b in (0, 1):
                    for f in range(5):
                        turn(U + 62 + b, b, f)
                        if f:
                            values(HEADS - 1, U + 62 + b, f - 1)
                    values(HEADS - 1, U + 62 + b, 4)
                pe.wait_ge(S("b_kv"), 32 * (l + 1))
                pe.wait_ge(S("a_os"), upto(U + 64))
                for t in (0, 1):
                    n = 2 * l + t
                    pe.wait_ge(S("b_q"), 16 * (n + 1))
                    pe.wait_ge(S("b_exp"), upto(n))
                    for j in range(8):
                        out = psum[:, j // 2, (j % 2) * NP:(j % 2 + 1) * NP]
                        nc.tensor.matmul(out, B["q"][:, j, 0, :], B["kt"][:, j, :], start=True, stop=False)
                        last = nc.tensor.matmul(out, B["q"][:, j, 1, :], B["kt"][:, j, :], start=False, stop=True)
                    last.then_inc(S("b_qk"), 1)
                    pe.wait_ge(S("b_d"), n + 1)
                    for h in range(HEADS):
                        for k in (0, 1):
                            j = 2 * h + k
                            last = nc.tensor.transpose(psum[:, 4 + j // 4, (j % 4) * P:(j % 4 + 1) * P], B["d"][:, h, k * P:(k + 1) * P], id_sb[:])
                    last.then_inc(S("b_tr"), 1)
                    pe.wait_ge(S("b_dt"), n + 1)
                    for h in range(HEADS):
                        for k in (0, 1):
                            last = nc.tensor.matmul(psum[:, 6, h * P:(h + 1) * P], B["dt"][:, 2 * h + k, :], B["v"][:, k, h * P:(h + 1) * P], start=(k == 0), stop=(k == 1))
                    last.then_inc(S("b_o"), 1)
                stage_end(pe)

                stage_begin(pe, l, 5)
                pe.wait_ge(S("o_wl"), upto((l + 1) * KT))

                def o_turn(t):
                    n = l * TILES + t
                    pe.wait_ge(S("o_y3"), n + 1)
                    for j in range(4):
                        last = nc.tensor.transpose(psum[:, 6, j * P:(j + 1) * P], O["on3"][:, j * P:(j + 1) * P], id_sb[:])
                    last.then_inc(S("o_tr"), 1)

                def o_products(t, b):
                    n = l * TILES + t
                    pe.wait_ge(S("o_lo"), n + 1)
                    for c in (0, 1):
                        if not (isinstance(t, int) and t < 2):
                            pe.wait_ge(S("o_gated"), 2 * (n - 2) + c + 1)
                        split_products(psum[:, 2 * b + c, :],
                                       [((O[f"yh{b}"][:, k, :], O[f"yl{b}"][:, k, :]), (O["wh"][:, k, c * 512:(c + 1) * 512], O["wl"][:, k, c * 512:(c + 1) * 512]))
                                        for k in range(KT)]).then_inc(S("o_mm"), 1)
                o_turn(0)

                def o_pair(m):
                    o_turn(2 * m + 1)
                    o_products(2 * m, 0)
                    o_turn(2 * m + 2)
                    o_products(2 * m + 1, 1)
                pairs(pe, o_pair)
                o_turn(TILES - 1)
                o_products(TILES - 2, 0)
                o_products(TILES - 1, 1)
                stage_end(pe)

        @block.scalar
        def _(act):
            act.wait_ge(S("consts"), 16 * 5)
            nc.scalar.activation(cond_act[:], cond_in[:], ACT.Silu).then_inc(S("cond_act"), 1)
            for l in range(DEPTH):
                stage_begin(act, l, 0)
                act.wait_ge(S("lam_sum"), l + 1)
                nc.scalar.activation(lam_exp[:], lam_sum[:], ACT.Exp).then_inc(S("lam_exp"), 1)
                act.wait_ge(S("mod_gate"), l + 1)
                for g in (0, 1):
                    nc.scalar.activation(gate_row[:, g, :].rearrange("p (a b) -> p a b", a=2), psum[:, 1 + 2 * g:3 + 2 * g, :], ACT.Copy)
                stage_end(act)

                stage_begin(act, l, 1)
                norm_act(act, "t_", T, l, 0)
                for q in range(4):
                    fill_act(act, "t_", T, l, 0, q)
                weights_act(act, "t_", l, T_STAGE, T["wh"], 2, WT // 2)

                def t_group(i, b, nxt=True):
                    if nxt:
                        norm_act(act, "t_", T, l, i + 1)
                    gi = l * NG + i
                    for m, (w, j) in enumerate(T_ORDER):
                        if m in T_ACT:
                            act.wait_ge(S("t_mm"), MT * gi + m + 1)
                            src = psum[:, m % T_BANKS, 0:G]
                            if w in ("fa", "ga"):
                                if j == 0:
                                    act.wait_ge(S("t_st_" + w), upto(16 * gi))
                                ins_ = nc.scalar.activation(T[w][:, j, :], src, ACT.Copy if w == "fa" else ACT.Silu)
                            elif w == "cg":
                                act.wait_ge(S("t_dve"), upto(4 * gi + (1 if j else 0)))
                                ins_ = nc.scalar.activation(T["cg"][:], src, ACT.Copy)
                            else:
                                act.wait_ge(S("t_dve"), upto(4 * gi + (2 if j else 0)))
                                ins_ = nc.scalar.activation(T["gb"][:], src, ACT.Silu)
                            ins_.then_inc(S("t_act"), 1)
                        if nxt and m in T_FILL_AFTER:
                            fill_act(act, "t_", T, l, i + 1, T_FILL_AFTER[m])
                groups(act, t_group, t_group, lambda i, b: t_group(i, b, False))
                stage_end(act)

                stage_begin(act, l, 2)
                for t in range(8):
                    act.wait_ge(S("f_ch"), l * 11 + t + 1)
                    nc.scalar.activation(F["pq"][:, t, :], psum[:, t % 2, :], ACT.Copy).then_inc(S("f_pq"), 1)
                act.wait_ge(S("f_ch"), upto(l * 11 + 9))
                nc.scalar.activation(F["plast"][0:1, :], psum[0:1, 2, 0:FW], ACT.Copy).then_inc(S("f_pq"), 1)
                for t in (0, 1):
                    act.wait_ge(S("f_ch"), upto(l * 11 + 10 + t))
                    nc.scalar.activation(F["pqp"][:, t, :], psum[:, 3 + t, :], ACT.Copy).then_inc(S("f_pq"), 1)
                for j in (0, 1):
                    act.wait_ge(S("cv_st"), upto(16 * (2 * l + j)))
                    nc.scalar.activation(F["cy"][:], z[:, j, :], ACT.Identity, bias=conv_sb[:, l, j, 3:4], scale=conv_sb[:, l, j, 1:2]).then_inc(S("cv_mid"), 1)
                for n in range(4):
                    act.wait_ge(S("f_sd"), l * 4 + n + 1)
                    act.wait_ge(S("f_out"), upto(l * 4 + n - 1 if n >= 2 else 0))
                    nc.scalar.activation(F[f"sq{n % 2}"][:], psum[:, 6 if n % 2 == 0 else 2, :], ACT.Copy).then_inc(S("f_sq"), 1)
                stage_end(act)

                stage_begin(act, l, 3)
                for q in range(4):
                    fill_act(act, "n_", N, l, 0, q)
                weights_act(act, "n_", l, N_STAGE, N["wh"], 4, WN // 4)

                def dup_hi(n, kind, stores, f):
                    act.wait_ge(S("n_ftr"), n + 1)
                    act.wait_ge(S("n_" + kind), upto(16 * stores))
                    src = psum[:, 4 + f, :].rearrange("p (j n) -> p j n", j=4)
                    dst = N["qst"][:, :, 0, :] if kind == "qst" else N["kst"][:]
                    nc.scalar.activation(dst.bitcast(F32R), src, ACT.Copy).then_inc(S("n_fhi"), 1)

                for t in range(PAST // P):
                    for f in (0, 1):
                        dup_hi(l * 80 + 2 * t + f, "kst", l * 44 + 2 * t + f, f)

                def n_group(i, b, nxt=True):
                    for s in (0, 1):
                        tt = 2 * i + s
                        nt = l * TILES + tt
                        for n in range(4):
                            if n == 2:
                                act.wait_ge(S("n_mm"), upto(4 * nt + 3))
                                act.wait_ge(S("n_vst"), upto(16 * nt))
                                if isinstance(i, int) and i == NG - 1:
                                    act.wait_ge(S("n_newv"), upto(16 * (2 * l + s)))
                                nc.scalar.activation(N["vs"][:], psum[:, 2, :], ACT.Copy).then_inc(S("n_vs"), 1)
                                for f in (0, 1):
                                    dup_hi(l * 80 + 8 + 4 * tt + f, "qst", 2 * nt + f, f)
                            if n == 3:
                                act.wait_ge(S("n_mm"), upto(4 * nt + 4))
                                act.wait_ge(S("n_gst"), upto(16 * nt))
                                nc.scalar.activation(N["gs"][:], psum[:, 3, :], ACT.Silu).then_inc(S("n_gs"), 1)
                                for f in (0, 1):
                                    dup_hi(l * 80 + 8 + 4 * tt + 2 + f, "kst", l * 44 + 8 + 2 * tt + f, f)
                            if nxt and 4 * s + n in N_FILL_AFTER:
                                fill_act(act, "n_", N, l, i + 1, N_FILL_AFTER[4 * s + n])
                groups(act, n_group, n_group, lambda i, b: n_group(i, b, False))
                stage_end(act)

                stage_begin(act, l, 4)
                U = l * 64

                def exps(u, b, part):
                    half, kp = part // 2, part % 2
                    st = A[f"s{b}"]
                    act.wait_ge(S("a_nb"), 4 * u + part + 1)
                    if part == 0 and not (isinstance(u, int) and u < 2):
                        act.wait_ge(S("a_dA"), upto(u - 1))
                        act.wait_ge(S("a_dB"), upto(u - 1))
                    keys = slice(0, KEYS_A) if kp == 0 else slice(KEYS_A, KEYS)
                    nc.scalar.activation(A[f"e{b}"][:, half, keys].rearrange("p (o w) -> p o w", w=512), psum[:, 3 * kp:5 if kp else 3, :],
                                         ACT.Exp, bias=st[:, 4 + part:5 + part], scale=SCALE, accum_out=st[:, 8 + part:9 + part]).then_inc(S("a_exp"), 1)
                    if kp == 1:
                        nc.scalar.activation(st[:, 12 + half:13 + half], st[:, part - 1:part], ACT.Exp, bias=st[:, 4 + part:5 + part],
                                             scale=SCALE).then_inc(S("a_al"), 1)

                def turn_act(u, b, f):
                    act.wait_ge(S("a_tr"), 5 * u + f + 1)
                    nc.scalar.activation(A["dt"][:, f, :], psum[:, 5 + (b + f) % 2, :], ACT.Copy).then_inc(S("a_tevS"), 1)

                def output(u, b, stored):
                    act.wait_ge(S("a_o"), u + 1)
                    act.wait_ge(S(f"a_st{b}"), upto(16 * stored))
                    nc.scalar.activation(A[f"os{b}"][:], psum[:, 7, 0:P], ACT.Identity, scale=A[f"s{b}"][:, 20:21]).then_inc(S("a_os"), 1)

                def unit(u, b, prev):
                    if prev is not None:
                        turn_act(prev, b, 0)
                    exps(u, b, 0)
                    exps(u, b, 1)
                    if prev is not None:
                        turn_act(prev, b, 2)
                    exps(u, b, 2)
                    if prev is not None:
                        turn_act(prev, b, 4)
                    exps(u, b, 3)

                for h in range(HEADS):
                    u0 = U + 16 * h
                    for b in (0, 1):
                        if h:
                            output(u0 - 3 + b, 1 - b, u0 // 2 - 2 + b)
                        unit(u0 + b, b, u0 - 2 + b if h else None)

                    def pair(m):
                        for b in (0, 1):
                            if not (isinstance(m, int) and h == 0 and 2 * m + b < 3):
                                output(u0 + 2 * m - 3 + b, 1 - b, u0 // 2 + m - 2 + b)
                            unit(u0 + 2 * m + b, b, u0 + 2 * m - 2 + b)
                    head_pairs(act, h, pair)
                for b in (0, 1):
                    output(U + 61 + b, 1 - b, U // 2 + 30 + b)
                    for f in (0, 2, 4):
                        turn_act(U + 62 + b, b, f)
                output(U + 63, 1, U // 2 + 31)
                for t in (0, 1):
                    n = 2 * l + t
                    act.wait_ge(S("b_nb"), n + 1)
                    act.wait_ge(S("b_d"), upto(n))
                    for j in range(8):
                        last = nc.scalar.activation(B["e"][:, j, :], psum[:, j // 2, (j % 2) * NP:(j % 2 + 1) * NP], ACT.Exp,
                                                    bias=B["nb"][:, j:j + 1], scale=SCALE, accum_out=B["ls"][:, j:j + 1])
                    last.then_inc(S("b_exp"), 1)
                    act.wait_ge(S("b_tr"), n + 1)
                    nc.scalar.activation(B["dt"][:].rearrange("p (a b) n -> p a (b n)", a=2), psum[:, 4:6, :], ACT.Copy).then_inc(S("b_dt"), 1)
                stage_end(act)

                stage_begin(act, l, 5)
                for k in range(KT):
                    act.wait_ge(S(f"o_w{k % 2}"), 16 * (l * KT // 2 + k // 2 + 1))
                    nc.scalar.activation(O["wh"][:, k, :], O_STAGE[k % 2][:], ACT.Copy).then_inc(S("o_wh"), 1)

                def o_norm(t, b):
                    n = l * TILES + t
                    act.wait_ge(S(f"o_in{b}"), 64 * (l * TILES // 2 + (t_half[0]) + 1))
                    if not (isinstance(t, int) and t < 2):
                        act.wait_ge(S("o_rs"), upto(n - 1))
                    act.wait_ge(S("o_sq"), upto(n))
                    for h in range(HEADS):
                        last = nc.scalar.activation(O["junk"][:, h * P:(h + 1) * P], O[f"o{b}"][:, h * P:(h + 1) * P], ACT.Square,
                                                    accum_out=O[f"sm{b}"][:, h:h + 1])
                    last.then_inc(S("o_sq"), 1)

                def o_hi(t, b):
                    n = l * TILES + t
                    act.wait_ge(S("o_tr"), n + 1)
                    nc.scalar.activation(O[f"yf{b}"][:, 4:8, :].rearrange("p a n -> p (a n)"), psum[:, 6, :], ACT.Copy).then_inc(S("o_yf"), 1)
                    act.wait_ge(S("o_yf"), n + 1)
                    if not (isinstance(t, int) and t < 2):
                        act.wait_ge(S("o_mm"), upto(2 * (n - 1)))
                    nc.scalar.activation(O[f"yh{b}"][:], O[f"yf{b}"][:], ACT.Copy).then_inc(S("o_hi"), 1)

                def o_final(t, b):
                    if l < DEPTH - 1:
                        return
                    n = l * TILES + t
                    act.wait_ge(S("o_xn"), n + 1)
                    act.wait_ge(S("o_fsq"), upto(t))
                    nc.scalar.activation(O["junk2"][:], O[f"xn{b}"][:], ACT.Square, accum_out=O[f"sm{b}"][:, 12:13]).then_inc(S("o_fsq"), 1)

                t_half = [0]
                o_norm(0, 0)
                o_hi(0, 0)

                def o_pair(m):
                    t_half[0] = m
                    o_norm(2 * m + 1, 1)
                    o_hi(2 * m + 1, 1)
                    o_final(2 * m, 0)
                    t_half[0] = m + 1
                    o_norm(2 * m + 2, 0)
                    o_hi(2 * m + 2, 0)
                    o_final(2 * m + 1, 1)
                pairs(act, o_pair)
                t_half[0] = TILES // 2 - 1
                o_norm(TILES - 1, 1)
                o_hi(TILES - 1, 1)
                o_final(TILES - 2, 0)
                o_final(TILES - 1, 1)
                stage_end(act)

        @block.vector
        def _(dve):
            chain = [0]

            def linked(instruction):
                chain[0] += 1
                instruction.then_inc(S("dve_chain"), 1)
                dve.wait_ge(S("dve_chain"), chain[0])

            nc.vector.memset(ones[:], 1.0).then_inc(S("ones_set"), 1)
            nc.vector.memset(neg_half[:], -0.5).then_inc(S("ones_set"), 1)
            nc.vector.memset(lam_sum[:], 0.0).then_inc(S("ones_set"), 1)
            dve.wait_ge(S("consts"), 16 * 5)
            for l in range(DEPTH):
                stage_begin(dve, l, 0)
                nc.vector.memset(psum[:, 0, 0:48], 0.0).then_inc(S("mod_zero"), 1)
                dve.wait_ge(S("lam_in"), 16 * (l + 1))
                linked(nc.vector.tensor_tensor(lam_pr[:], lam_in[:, 0::2, :], lam_in[:, 1::2, :], ALU.mult))
                nc.vector.tensor_reduce(lam_sum[:], lam_pr[:], AX_X, ALU.add).then_inc(S("lam_sum"), 1)
                dve.wait_ge(S("lam_exp"), l + 1)
                lam_init = 0.8 - 0.6 * math.exp(-0.3 * l)
                linked(nc.vector.scalar_tensor_tensor(lam[:], lam_exp[:, 0:1], lam_init, lam_exp[:, 1:2], ALU.add, ALU.subtract))
                dve.wait_ge(S("mod_mm"), KT * (l + 1))
                linked(nc.vector.tensor_tensor(mod[:], psum[:, 0, 0:48].rearrange("p (m g) -> p m g", g=2),
                                               bmod_sb[:, l].unsqueeze(2).broadcast_to([P, 24, 2]), ALU.add))
                for g in (0, 1):
                    for k in range(KT):
                        last = nc.vector.tensor_scalar(M["dg"][:, g * KT + k, :], id_sb[:], mod[:, 16 + k, g:g + 1], None, ALU.mult)
                last.then_inc(S("mod_dg"), 1)
                linked(nc.vector.tensor_scalar(one_scale[:], mod[:, 8:16, :], 1.0, None, ALU.add))
                linked(nc.vector.tensor_tensor(one_scale[:], one_scale[:], ng_sb[:, l].unsqueeze(2).broadcast_to([P, KT, 2]), ALU.mult))
                stage_end(dve)

                stage_begin(dve, l, 1)
                norm_dve(dve, "t_", T, l, 0, True)
                for q in range(4):
                    fill_dve(dve, "t_", T, l, 0, 0, q, MT)
                weights_dve(dve, "t_", l, T_STAGE, T["wh"], T["wl"], 2, WT // 2)

                def t_group(i, b, nxt=True):
                    if nxt:
                        norm_dve(dve, "t_", T, l, i + 1, True)
                    gi = l * NG + i
                    for m, (w, j) in enumerate(T_ORDER):
                        if m in T_DVE:
                            dve.wait_ge(S("t_mm"), MT * gi + m + 1)
                            dve.wait_ge(S("t_act"), len(T_ACT) * gi + T_ACT.index(m - 1) + 1)
                            dst, other = (z, T["cg"]) if w == "hc" else (bgs, T["gb"])
                            nc.vector.tensor_tensor(dst[:, j, bass.ds(i * G, G)], psum[:, m % T_BANKS, 0:G], other[:], ALU.mult).then_inc(S("t_dve"), 1)
                        if nxt and m in T_FILL_AFTER:
                            fill_dve(dve, "t_", T, l, i + 1, 1 - b, T_FILL_AFTER[m], MT)
                groups(dve, t_group, t_group, lambda i, b: t_group(i, b, False))
                stage_end(dve)

                stage_begin(dve, l, 2)
                dve.wait_ge(S("f_in"), 64 * (l + 1))
                fa, fe, fo, ya, sga = F["fa"], F["fe"], F["fo"], F["ya"], F["sga"]
                for j in (0, 1):
                    nc.vector.tensor_tensor(fe[:, j, 1:NH], fa[:, j, 1:NH], fa[:, j, NS - 1:NH:-1], ALU.add)
                    nc.vector.tensor_tensor(fo[:, j, 1:NH], fa[:, j, 1:NH], fa[:, j, NS - 1:NH:-1], ALU.subtract)
                nc.vector.tensor_copy(fe[:, :, 0:NH + 1:NH], fa[:, :, 0:NH + 1:NH])
                nc.vector.memset(fo[:, :, 0:1], 0.0).then_inc(S("f_fold"), 1)
                for j in (0, 1):
                    dve.wait_ge(S("cv_mid"), 2 * l + j + 1)
                    cy = F["cy"]
                    for tap, to, frm in ((0, 1, 0), (2, 0, 1)):
                        for a, b in ((0, NS), (NS, NTOK)):
                            ins_ = nc.vector.scalar_tensor_tensor(cy[:, a + to:b - frm], z[:, j, a + frm:b - to], conv_sb[:, l, j, tap:tap + 1],
                                                                  cy[:, a + to:b - frm], ALU.mult, ALU.add)
                        linked(ins_)
                    nc.vector.tensor_tensor(cy[:], cy[:], bgs[:, j, :], ALU.mult).then_inc(S("cv_y"), 1)
                for n in range(4):
                    kc, ct = n // 2, n % 2
                    dve.wait_ge(S("f_sq"), l * 4 + n + 1)
                    cb = psum[:, 5 if ct == 0 else 7, :]
                    sq = F[f"sq{n % 2}"]
                    a = kc * 512
                    nc.vector.tensor_tensor(ya[:, ct, a:a + 512], cb, sq[:], ALU.subtract)
                    o = 1 if kc == 0 else 0
                    top = NS - a - o
                    nc.vector.tensor_tensor(ya[:, ct, top:top - (512 - o):-1], cb[:, o:512], sq[:, o:512], ALU.add).then_inc(S("f_out"), 1)
                dve.wait_ge(S("f_nyq"), 2 * (l + 1))
                nc.vector.tensor_copy(ya[:, :, NH:NH + 1], psum[:, 0, 0:2].unsqueeze(2))
                linked(nc.vector.tensor_copy(ya[:, :, NS:NTOK], psum[:, 1, :].rearrange("p (a b) -> p a b", a=2)))
                dve.wait_ge(S("f_sga"), 32 * (l + 1))
                nc.vector.tensor_tensor(ya[:], ya[:], sga[:], ALU.mult).then_inc(S("f_ya"), 1)
                stage_end(dve)

                stage_begin(dve, l, 3)
                norm_dve(dve, "n_", N, l, 0, False)
                for q in range(4):
                    fill_dve(dve, "n_", N, l, 0, 0, q, 8)
                weights_dve(dve, "n_", l, N_STAGE, N["wh"], N["wl"], 4, WN // 4)

                def dup_lo(n, kind, f):
                    dve.wait_ge(S("n_fhi"), n + 1)
                    if kind == "qst":
                        src = psum[:, 4 + f, :].rearrange("p (j n) -> p j n", j=4)
                        ins_ = nc.vector.tensor_tensor(N["qst"][:, :, 1, :].bitcast(F32R), src, N["qst"][:, :, 0, :], ALU.subtract)
                    else:
                        src = psum[HD:P, 4 + f, :].rearrange("p (j n) -> p j n", j=4)
                        ins_ = nc.vector.tensor_tensor(N["kst"][HD:P].bitcast(F32R), src, N["kst"][HD:P], ALU.subtract)
                    ins_.then_inc(S("n_flo"), 1)
                    return ins_

                for t in range(PAST // P):
                    for f in (0, 1):
                        dup_lo(l * 80 + 2 * t + f, "kst", f)

                def rope(tt, n):
                    nt = l * TILES + tt
                    dve.wait_ge(S("n_mm"), 4 * nt + n + 1)
                    dve.wait_ge(S("n_tab"), 16 * (nt + 1))
                    dve.wait_ge(S("n_dup"), upto(l * 40 + 4 + 2 * tt + n))
                    cos = N["rope"][:, 0].unsqueeze(1).broadcast_to([P, 8, HD])
                    nc.vector.tensor_tensor(N["m1"][:].rearrange("p (j d) -> p j d", j=8), psum[:, n, :].rearrange("p (j d) -> p j d", j=8), cos, ALU.mult).then_inc(S("n_rope"), 1)
                    src = psum[:, n, :].rearrange("p (j r a w) -> p j r a w", j=8, r=2, a=2)
                    dst = N["m2"][:].rearrange("p (j r a w) -> p j r a w", j=8, r=2, a=2)
                    sin = N["rope"][:, 1].rearrange("p (r a w) -> p r a w", r=2, a=2)
                    for a in (0, 1):
                        ins_ = nc.vector.tensor_tensor(dst[:, :, :, a, :], src[:, :, :, 1 - a, :], sin[:, :, a, :].unsqueeze(1).broadcast_to([P, 8, 2, 16]), ALU.mult)
                    ins_.then_inc(S("n_rope"), 1)

                def n_group(i, b, nxt=True):
                    if nxt:
                        norm_dve(dve, "n_", N, l, i + 1, False)
                    for s in (0, 1):
                        tt = 2 * i + s
                        for n in range(4):
                            if n < 2:
                                rope(tt, n)
                            if n == 2:
                                for f in (0, 1):
                                    dup_lo(l * 80 + 8 + 4 * tt + f, "qst", f)
                            if n == 3:
                                for f in (0, 1):
                                    dup_lo(l * 80 + 8 + 4 * tt + 2 + f, "kst", f)
                            if nxt and 4 * s + n in N_FILL_AFTER:
                                fill_dve(dve, "n_", N, l, i + 1, 1 - b, N_FILL_AFTER[4 * s + n], 8)
                groups(dve, n_group, n_group, lambda i, b: n_group(i, b, False))
                stage_end(dve)

                stage_begin(dve, l, 4)
                U = l * 64

                def maxima(u, b, part):
                    half, kp = part // 2, part % 2
                    st = A[f"s{b}"]
                    dve.wait_ge(S("a_qk"), 4 * u + part + 1)
                    if part == 0 and not (isinstance(u, int) and u < 2):
                        dve.wait_ge(S("a_dB"), upto(u - 1))
                    nc.vector.tensor_reduce(st[:, part:part + 1], psum[:, 3 * kp:5 if kp else 3, :], mybir.AxisListType.XY,
                                            ALU.max).then_inc(S("a_mx"), 1)
                    dve.wait_ge(S("a_mx"), 4 * u + part + 1)
                    if kp == 0:
                        nc.vector.tensor_scalar(st[:, 4 + part:5 + part], st[:, part:part + 1], -SCALE, None, ALU.mult).then_inc(S("a_nb"), 1)
                    else:
                        nc.vector.tensor_scalar(st[:, 4 + part:5 + part], st[:, part:part + 1], st[:, part - 1:part], -SCALE, ALU.max, ALU.mult).then_inc(S("a_nb"), 1)

                SMALL = 3

                def small(u, n, ins_):
                    ins_.then_inc(S("a_sm"), 1)
                    dve.wait_ge(S("a_sm"), SMALL * u + n + 1)

                def factors(u, b):
                    st = A[f"s{b}"]
                    c = lambda i, w=1: st[:, i:i + w]
                    dve.wait_ge(S("a_exp"), upto(4 * u + 4))
                    dve.wait_ge(S("a_al"), upto(2 * u + 2))
                    if not (isinstance(u, int) and u < 2):
                        dve.wait_ge(S("a_os"), upto(u - 1))
                    for half in (0, 1):
                        ins_ = nc.vector.scalar_tensor_tensor(c(14 + half), c(8 + 2 * half), c(12 + half), c(9 + 2 * half), ALU.mult, ALU.add)
                    small(u, 0, ins_)
                    small(u, 1, nc.vector.reciprocal(c(16, 2), c(14, 2)))
                    nc.vector.tensor_scalar(c(20), c(16), -1.0, None, ALU.mult)
                    small(u, 2, nc.vector.scalar_tensor_tensor(c(18), c(14), lam[:, 0:1], c(17), ALU.mult, ALU.mult))
                    nc.vector.tensor_scalar(c(19), c(18), c(13), None, ALU.mult).then_inc(S("a_c"), 1)

                def combine(u, b):
                    e = A[f"e{b}"]
                    dve.wait_ge(S("a_c"), u + 1)
                    dve.wait_ge(S("a_e1"), u + 1)
                    if not (isinstance(u, int) and u < 2):
                        dve.wait_ge(S("a_tr"), upto(5 * (u - 1)))
                    nc.vector.scalar_tensor_tensor(A[f"d{b}"][:, 0:KEYS_A], e[:, 1, 0:KEYS_A], A[f"s{b}"][:, 19:20], e[:, 0, 0:KEYS_A],
                                                   ALU.mult, ALU.subtract).then_inc(S("a_dA"), 1)

                def turn_dve(u, b, f):
                    dve.wait_ge(S("a_tr"), 5 * u + f + 1)
                    nc.vector.tensor_copy(A["dt"][:, f, :], psum[:, 5 + (b + f) % 2, :]).then_inc(S("a_tevV"), 1)

                def unit(u, b, first=False):
                    lone = first and b == 0
                    maxima(u, b, 0)
                    if not first:
                        turn_dve(u - 2, b, 1)
                    if not lone:
                        factors(u - 1, 1 - b)
                    maxima(u, b, 1)
                    maxima(u, b, 2)
                    if not first:
                        turn_dve(u - 2, b, 3)
                    if not lone:
                        combine(u - 1, 1 - b)
                    maxima(u, b, 3)

                for h in range(HEADS):
                    u0 = U + 16 * h
                    for b in (0, 1):
                        unit(u0 + b, b, h == 0)

                    def pair(m):
                        for b in (0, 1):
                            unit(u0 + 2 * m + b, b)
                    head_pairs(dve, h, pair)
                factors(U + 63, 1)
                turn_dve(U + 62, 0, 1)
                turn_dve(U + 62, 0, 3)
                combine(U + 63, 1)
                turn_dve(U + 63, 1, 1)
                turn_dve(U + 63, 1, 3)
                for t in (0, 1):
                    n = 2 * l + t
                    dve.wait_ge(S("b_qk"), n + 1)
                    linked(nc.vector.tensor_reduce(B["mx"][:], psum[:, 0:4, :].rearrange("p a (b n) -> p (a b) n", b=2), AX_X, ALU.max))
                    nc.vector.tensor_scalar(B["nb"][:], B["mx"][:], -SCALE, None, ALU.mult).then_inc(S("b_nb"), 1)
                    dve.wait_ge(S("b_exp"), n + 1)
                    linked(nc.vector.reciprocal(B["rl"][:], B["ls"][:]))
                    linked(nc.vector.tensor_scalar(B["nr"][:], B["rl"][:, 0::2], -1.0, None, ALU.mult))
                    linked(nc.vector.scalar_tensor_tensor(B["c"][:], B["ls"][:, 0::2], lam[:, 0:1], B["rl"][:, 1::2], ALU.mult, ALU.mult))
                    dve.wait_ge(S("b_tr"), upto(n))
                    for h in range(HEADS):
                        last = nc.vector.scalar_tensor_tensor(B["d"][:, h, :], B["e"][:, 2 * h + 1, :], B["c"][:, h:h + 1], B["e"][:, 2 * h, :], ALU.mult, ALU.subtract)
                    last.then_inc(S("b_d"), 1)
                    dve.wait_ge(S("b_o"), n + 1)
                    dve.wait_ge(S("b_st"), upto(16 * n))
                    nc.vector.tensor_tensor(B["os"][:].rearrange("p (h d) -> p h d", h=HEADS), psum[:, 6, :].rearrange("p (h d) -> p h d", h=HEADS),
                                            B["nr"][:].unsqueeze(2).broadcast_to([P, HEADS, P]), ALU.mult).then_inc(S("b_os"), 1)
                stage_end(dve)

                stage_begin(dve, l, 5)
                dve.wait_ge(S("o_c"), 32 * (l + 1))
                linked(nc.vector.tensor_scalar(O["subln"][:], O["subln"][:], 1.0 - lam_init, None, ALU.mult))

                def o_scale(t, b):
                    n = l * TILES + t
                    sm = O[f"sm{b}"]
                    dve.wait_ge(S("o_sq"), n + 1)
                    nc.vector.tensor_scalar(sm[:, 4:8], sm[:, 0:4], 1.0 / P, EPS, ALU.mult, ALU.add).then_inc(S("o_ms"), 1)
                    dve.wait_ge(S("o_rs"), n + 1)
                    hv = lambda x: x[:].rearrange("p (h d) -> p h d", h=HEADS)
                    nc.vector.tensor_tensor(hv(O["on"]), hv(O[f"o{b}"]), sm[:, 8:12].unsqueeze(2).broadcast_to([P, HEADS, P]), ALU.mult).then_inc(S("o_y1"), 1)
                    dve.wait_ge(S("o_y1"), n + 1)
                    nc.vector.tensor_tensor(hv(O["on2"]), hv(O["on"]), O["subln"][:].unsqueeze(1).broadcast_to([P, HEADS, P]), ALU.mult).then_inc(S("o_y2"), 1)
                    dve.wait_ge(S("o_y2"), n + 1)
                    dve.wait_ge(S("o_tr"), upto(n))
                    nc.vector.tensor_tensor(O["on3"][:], O["on2"][:], O[f"g{b}"][:], ALU.mult).then_inc(S("o_y3"), 1)

                def o_residual(t, b, g):
                    n = l * TILES + t
                    dve.wait_ge(S("o_mm"), 2 * n + 1)
                    if not (isinstance(t, int) and t < 2):
                        dve.wait_ge(S("o_xn"), upto(n - 1))
                    for c in (0, 1):
                        dve.wait_ge(S("o_mm"), 2 * n + c + 1)
                        nc.vector.tensor_tensor(O[f"t{b}"][:, c * 512:(c + 1) * 512], psum[:, 2 * b + c, :], gate_row[:, g, c * 512:(c + 1) * 512], ALU.mult).then_inc(S("o_gated"), 1)

                def o_final(t, b):
                    if l < DEPTH - 1:
                        return
                    sm = O[f"sm{b}"]
                    dve.wait_ge(S("o_fsq"), t + 1)
                    nc.vector.tensor_scalar(sm[:, 13:14], sm[:, 12:13], 1.0 / D, EPS, ALU.mult, ALU.add).then_inc(S("o_fms"), 1)
                    dve.wait_ge(S("o_frs"), t + 1)
                    if not (isinstance(t, int) and t < 2):
                        dve.wait_ge(S(f"o_st{b}"), upto(16 * (l * TILES // 2 + half_[0])))
                    nc.vector.scalar_tensor_tensor(O[f"y{b}"][:], O[f"xn{b}"][:], sm[:, 14:15], O["fg"][:], ALU.mult, ALU.mult).then_inc(S("o_y"), 1)

                half_ = [0]
                for k in range(KT):
                    dve.wait_ge(S("o_wh"), l * KT + k + 1)
                    nc.vector.tensor_tensor(O["wl"][:, k, :], O_STAGE[k % 2][:], O["wh"][:, k, :].bitcast(F32), ALU.subtract).then_inc(S("o_wl"), 1)
                o_scale(0, 0)

                def o_pair(m):
                    half_[0] = m
                    o_scale(2 * m + 1, 1)
                    o_residual(2 * m, 0, 0)
                    o_final(2 * m, 0)
                    o_scale(2 * m + 2, 0)
                    o_residual(2 * m + 1, 1, 0)
                    o_final(2 * m + 1, 1)
                pairs(dve, o_pair)
                half_[0] = TILES // 2 - 1
                o_scale(TILES - 1, 1)
                o_residual(TILES - 2, 0, 1)
                o_final(TILES - 2, 0)
                o_residual(TILES - 1, 1, 1)
                o_final(TILES - 1, 1)
                stage_end(dve)

        @block.gpsimd
        def _(pool):
            pool.wait_ge(S("ones_set"), 3)
            for l in range(DEPTH):
                stage_begin(pool, l, 0)
                stage_end(pool)

                stage_begin(pool, l, 1)
                norm_pool(pool, "t_", l, 0)
                for q in range(4):
                    fill_pool(pool, "t_", T, l, 0, 0, q, MT)

                def t_group(i, b, nxt=True):
                    if nxt:
                        norm_pool(pool, "t_", l, i + 1)
                        for q in range(4):
                            fill_pool(pool, "t_", T, l, i + 1, 1 - b, q, MT)
                groups(pool, t_group, t_group, lambda i, b: t_group(i, b, False))
                stage_end(pool)

                stage_begin(pool, l, 2)
                stage_end(pool)

                stage_begin(pool, l, 3)
                for q in range(4):
                    fill_pool(pool, "n_", N, l, 0, 0, q, 8)
                dup = N["dup"]
                for t in range(PAST // P):
                    pool.wait_ge(S("n_ck"), 16 * (4 * l + t + 1))
                    pool.wait_ge(S("n_ftr"), upto(l * 80 + 2 * t))
                    for a in (0, 1):
                        ins_ = nc.gpsimd.tensor_copy(dup[:, :, a, :], N["m1"][:].rearrange("p (j d) -> p j d", j=8))
                    ins_.then_inc(S("n_dup"), 1)

                def n_group(i, b, nxt=True):
                    for s in (0, 1):
                        tt = 2 * i + s
                        for n in range(4):
                            if n < 2:
                                pool.wait_ge(S("n_rope"), upto(4 * (l * TILES + tt) + 2 * n + 2))
                                pool.wait_ge(S("n_ftr"), upto(l * 80 + 8 + 4 * tt + 2 * n))
                                if isinstance(i, int) and i == NG - 1:
                                    pool.wait_ge(S("n_newk"), upto(16 * (2 * l + s)))
                                for a in (0, 1):
                                    ins_ = nc.gpsimd.tensor_tensor(dup[:, :, a, :], N["m1"][:].rearrange("p (j d) -> p j d", j=8),
                                                                   N["m2"][:].rearrange("p (j d) -> p j d", j=8), ALU.add)
                                ins_.then_inc(S("n_dup"), 1)
                            if nxt and 4 * s + n in N_FILL_AFTER:
                                fill_pool(pool, "n_", N, l, i + 1, 1 - b, N_FILL_AFTER[4 * s + n], 8)
                groups(pool, n_group, n_group, lambda i, b: n_group(i, b, False))
                stage_end(pool)

                stage_begin(pool, l, 4)
                U = l * 64

                def combine(u, b):
                    e = A[f"e{b}"]
                    st = A[f"s{b}"]
                    pool.wait_ge(S("a_c"), u + 1)
                    e1 = e[:, 0, 0:KEYS_A]
                    nc.gpsimd.tensor_tensor(e1, e1, st[:, 12:13].broadcast_to([P, KEYS_A]), ALU.mult).then_inc(S("a_e1"), 1)
                    e2 = e[:, 1, KEYS_A:KEYS]
                    nc.gpsimd.tensor_tensor(e2, e2, st[:, 18:19].broadcast_to([P, KEYS - KEYS_A]), ALU.mult).then_inc(S("a_e2"), 1)
                    pool.wait_ge(S("a_e2"), u + 1)
                    if not (isinstance(u, int) and u < 2):
                        pool.wait_ge(S("a_tr"), upto(5 * (u - 1)))
                    nc.gpsimd.tensor_tensor(A[f"d{b}"][:, KEYS_A:KEYS], e2, e[:, 0, KEYS_A:KEYS], ALU.subtract).then_inc(S("a_dB"), 1)

                for h in range(HEADS):
                    u0 = U + 16 * h
                    for b in (0, 1):
                        if h or b:
                            combine(u0 + b - 1, 1 - b)

                    def pair(m):
                        for b in (0, 1):
                            combine(u0 + 2 * m + b - 1, 1 - b)
                    head_pairs(pool, h, pair)
                combine(U + 63, 1)
                stage_end(pool)

                stage_begin(pool, l, 5)

                def o_rstd(t, b):
                    n = l * TILES + t
                    sm = O[f"sm{b}"]
                    pool.wait_ge(S("o_ms"), n + 1)
                    nc.gpsimd.tensor_tensor(sm[:, 8:12], sm[:, 4:8], neg_half[:], ALU.pow).then_inc(S("o_rs"), 1)

                def o_lo(t, b):
                    n = l * TILES + t
                    pool.wait_ge(S("o_hi"), n + 1)
                    nc.gpsimd.tensor_tensor(O[f"yl{b}"][:], O[f"yf{b}"][:], O[f"yh{b}"][:].bitcast(F32), ALU.subtract).then_inc(S("o_lo"), 1)

                def o_add(t, b):
                    n = l * TILES + t
                    pool.wait_ge(S("o_gated"), upto(2 * n + 2))
                    if not (isinstance(t, int) and t < 2):
                        if l < DEPTH - 1:
                            pool.wait_ge(S(f"o_st{b}"), upto(16 * (l * TILES // 2 + half_[0])))
                        else:
                            pool.wait_ge(S("o_y"), upto(t - 1))
                    nc.gpsimd.tensor_tensor(O[f"xn{b}"][:], O[f"t{b}"][:], O[f"x{b}"][:], ALU.add).then_inc(S("o_xn"), 1)

                def o_frs(t, b):
                    if l < DEPTH - 1:
                        return
                    sm = O[f"sm{b}"]
                    pool.wait_ge(S("o_fms"), t + 1)
                    nc.gpsimd.tensor_tensor(sm[:, 14:15], sm[:, 13:14], neg_half[:, 0:1], ALU.pow).then_inc(S("o_frs"), 1)

                half_ = [0]
                o_rstd(0, 0)
                o_lo(0, 0)

                def o_pair(m):
                    half_[0] = m
                    for b in (0, 1):
                        o_rstd(2 * m + 1 + b, 1 - b)
                        o_lo(2 * m + 1 + b, 1 - b)
                        o_add(2 * m + b, b)
                        o_frs(2 * m + b, b)
                pairs(pool, o_pair)
                half_[0] = TILES // 2 - 1
                o_rstd(TILES - 1, 1)
                o_lo(TILES - 1, 1)
                for b in (0, 1):
                    o_add(TILES - 2 + b, b)
                    o_frs(TILES - 2 + b, b)
                stage_end(pool)


def _tables():
    f32 = np.float32
    t = {}
    c = np.arange(FW)
    ang = 2 * np.pi * ((c[:, None] * c[None, :]) % FW) / FW
    norm = 1.0 / math.sqrt(NS * FW)
    lay = lambda a: np.ascontiguousarray(a.reshape(-1, P, a.shape[1]).transpose(1, 0, 2))
    t["chan_cos"] = lay((np.cos(ang) * norm).astype(f32))
    t["chan_sin"] = lay((np.sin(ang) * norm).astype(f32))
    n = np.arange(NH)
    ang = 2 * np.pi * ((n[:, None] * n[None, :]) % NS) / NS
    for name, tab in (("seq_cos", np.cos(ang)), ("seq_sin", np.sin(ang))):
        tab = tab.astype(f32).reshape(8, P, 2, 512)
        t[name] = np.ascontiguousarray(tab.transpose(2, 1, 0, 3))
    sign = np.where(np.arange(512) % 2, -1.0, 1.0).astype(f32)
    t["sign_row"] = sign[None, :]
    t["sign_col"] = np.ascontiguousarray(sign[:P, None])
    n = np.arange(NP)
    ang = 2 * np.pi * ((n[:, None] * n[None, :]) % NP) / NP
    up = math.sqrt(NS / NP)
    t["prompt_cos"] = lay((np.cos(ang) * up).astype(f32))
    t["prompt_sin"] = lay((-np.sin(ang) * up).astype(f32))
    t["ident"] = np.eye(P, dtype=f32)
    half = HD // 2
    inv = (f32(1.0) / (f32(10000.0) ** (np.arange(0, half, 2, dtype=f32) / f32(half)))).astype(f32)
    tok = np.arange(NS)
    rope = np.zeros((NTOK, 2, HD), f32)
    rope[NS:, 0] = 1.0
    for a, pos in enumerate((tok // GRID_W, tok % GRID_W)):
        ang = (pos.astype(f32)[:, None] * inv[None, :]).astype(f32).astype(np.float64)
        w = half // 2
        for b in (0, 1):
            col = a * half + b * w
            rope[:NS, 0, col:col + w] = np.cos(ang)
            rope[:NS, 1, col:col + w] = np.sin(ang) * (-1.0 if b == 0 else 1.0)
    t["rope"] = rope
    return t


def kernel(x_prompt, x_sample, cache_k, cache_v, c, c_ctx, norm_g, w_mod, b_mod, w_in, conv_w, conv_b, lam_vec,
           subln_g, w_out, final_g):
    import concourse.bacc as _bacc
    from concourse.bass_utils import run_bass_kernel_spmd as _run

    a = lambda x: np.ascontiguousarray(np.asarray(x))
    arrays = {
        "x_all": a(np.concatenate([np.asarray(x_sample)[0], np.asarray(x_prompt)[0]])),
        "cond": a(np.stack([np.asarray(c)[0], np.asarray(c_ctx)]).reshape(2, KT, P).transpose(2, 1, 0)),
        "b_mod": a(np.asarray(b_mod).reshape(DEPTH, 24, P).transpose(2, 0, 1)),
        "norm_g": a(np.asarray(norm_g).reshape(DEPTH, KT, P).transpose(2, 0, 1)),
        "w_mod": a(w_mod),
        "w_in_t": a(np.asarray(w_in)[:, :, :WT]),
        "w_in_n": a(np.asarray(w_in)[:, :, WT:]),
        "conv_wb": a(np.concatenate([np.asarray(conv_w), np.asarray(conv_b)[:, None]], 1).reshape(DEPTH, 4, 2, P).transpose(3, 0, 2, 1)),
        "lam_vec": a(lam_vec),
        "subln_g": a(subln_g),
        "w_out": a(w_out),
        "final_g": a(np.asarray(final_g)[None]),
        "cache_k": a(np.asarray(cache_k)[0].reshape(DEPTH, PAST, AW)),
        "cache_v": a(np.asarray(cache_v)[0].reshape(DEPTH, PAST, AW)),
        **_tables(),
    }
    nc = _bacc.Bacc("TRN2", target_bir_lowering=False, num_devices=1)
    ins = {n: nc.dram_tensor(n, v.shape, F32, kind="ExternalInput").ap() for n, v in arrays.items()}
    y_all = nc.dram_tensor("y_all", (NTOK, D), F32, kind="ExternalOutput").ap()
    new_k = nc.dram_tensor("new_k", (DEPTH, NP, AW), F32, kind="ExternalOutput").ap()
    new_v = nc.dram_tensor("new_v", (DEPTH, NP, AW), F32, kind="ExternalOutput").ap()
    backbone(nc, ins, y_all, new_k, new_v)
    r = _run(nc, [arrays], core_ids=[0]).results[0]
    y = r["y_all"]
    return (y[NS:].reshape(1, NP, D), y[:NS].reshape(1, NS, D), r["new_k"].reshape(1, DEPTH, NP, HEADS, QKW),
            r["new_v"].reshape(1, DEPTH, NP, HEADS, QKW))
```

```python
from contextlib import ExitStack
import math

import numpy as np

import concourse.bass as bass
from concourse import mybir

F32 = mybir.dt.float32
F32R = mybir.dt.float32r
BF16 = mybir.dt.bfloat16
ACT = mybir.ActivationFunctionType
ALU = mybir.AluOpType
AX_X = mybir.AxisListType.X

P = 128
D = 1024
KT = D // P
DEPTH = 2
NS = 2048
NP = 256
NTOK = NS + NP
TILES = NTOK // P
PAST = 512
G = 256
NG = NTOK // G
HEADS = 4
HD = 64
QKW = 2 * HD
AW = HEADS * QKW
FW = 256
CW = 256
WT = 2 * FW + 4 * CW
WN = 4 * AW
MT = WT // P
KEYS = PAST + NS
KEYS_A = 3 * 512
KTILES = KEYS // P
HEAD_TILES = NS // P
EPS = 1e-6
NH = NS // 2
SCALE = HD ** -0.5
GRID_W = 64

T_ORDER = [("fa", 0), ("fa", 1), ("ga", 0), ("ga", 1), ("cg", 0), ("hc", 0), ("gb", 0), ("bg", 0),
           ("cg", 1), ("hc", 1), ("gb", 1), ("bg", 1)]
T_COLUMN = {"fa": 0, "ga": FW, "bg": 2 * FW, "cg": 2 * FW + CW, "hc": 2 * FW + 2 * CW, "gb": 2 * FW + 3 * CW}
T_ACT = [m for m, (w, _) in enumerate(T_ORDER) if w not in ("hc", "bg")]
T_DVE = [m for m, (w, _) in enumerate(T_ORDER) if w in ("hc", "bg")]
T_BANKS = 6
T_FILL_AFTER = {3: 0, 5: 1, 7: 2, 9: 3}
N_FILL_AFTER = {0: 0, 1: 1, 4: 2, 5: 3}
A_ORDER = [("q", 0), ("t", 0), ("t", 1), ("q", 1), ("v", 0), ("t", 2), ("v", 1), ("t", 3), ("q", 2), ("t", 4),
           ("v", 2), ("q", 3), ("v", 3), ("v", 4)]

W_OUT_SLOTS = [[(), ()], [(0,), (1,)], [(2,), (3,)], [(4, 5), (6, 7)]]


def backbone(nc, ins, y_all, new_k, new_v):
    es = ExitStack()
    with es:
        def scratch(name, shape):
            return nc.dram_tensor(name, shape, F32, kind="Internal").ap()

        x_scr = scratch("x_scr", (NTOK, D))
        fa_scr = scratch("fa_scr", (NG, P, 2, G))
        sga_scr = scratch("sga_scr", (NG, P, 2, G))
        yt_scr = scratch("yt_scr", (P, 4, NTOK))
        q_scr = scratch("q_scr", (TILES, P, 8, 2, P))
        k_scr = scratch("k_scr", (P, 8, KEYS + NP))
        v_scr = scratch("v_scr", (NTOK, AW))
        sgc_scr = scratch("sgc_scr", (NTOK, AW))
        gate_scr = scratch("gate_scr", (2, D))
        o_scr = scratch("o_scr", (NTOK, AW))

        def keep(name, shape, dt=F32):
            return es.enter_context(nc.sbuf_tensor(name, shape, dt))

        id_sb = keep("id_sb", [P, P])
        ones = keep("ones", [P, P])
        cond_in = keep("cond_in", [P, KT, 2])
        cond_act = keep("cond_act", [P, KT, 2])
        mod = keep("mod", [P, 16, 2])
        bmod_sb = keep("bmod_sb", [P, DEPTH, 24])
        ng_sb = keep("ng_sb", [P, DEPTH, KT])
        one_scale = keep("one_scale", [P, KT, 2])
        sqsum = keep("sqsum", [P, 2])
        meansq = keep("meansq", [P, 2])
        rstd = keep("rstd", [P, TILES])
        neg_half = keep("neg_half", [P, 4])
        conv_sb = keep("conv_sb", [P, DEPTH, 2, 4])
        lam_in = keep("lam_in", [P, 4, HD])
        lam_pr = keep("lam_pr", [P, 2, HD])
        lam_sum = keep("lam_sum", [P, 2])
        lam_exp = keep("lam_exp", [P, 2])
        lam = keep("lam", [P, 1])

        def region(prefix, shapes):
            with ExitStack() as st:
                return {n: st.enter_context(nc.sbuf_tensor(prefix + n, s, d)) for n, s, d in shapes}

        def weight_buffers(stack, prefix, width):
            wh = stack.enter_context(nc.sbuf_tensor(prefix + "wh", [P, KT, width], F32R))
            wraw = region(prefix, [("wraw", [P, KT, width], F32)])["wraw"]
            wl = stack.enter_context(nc.sbuf_tensor(prefix + "wl", [P, KT, width], F32R))
            return {"wh": wh, "wraw": wraw, "wl": wl}

        norm_bufs = [("xt0", [P, D], F32), ("xt1", [P, D], F32), ("hf", [P, 2, 4, P], F32),
                     ("hh0", [P, KT, G], F32R), ("hh1", [P, KT, G], F32R),
                     ("hl0", [P, KT, G], F32R), ("hl1", [P, KT, G], F32R)]
        with ExitStack() as conv_stack:
            z = conv_stack.enter_context(nc.sbuf_tensor("conv_z", [P, 2, NTOK], F32))
            bgs = conv_stack.enter_context(nc.sbuf_tensor("conv_bgs", [P, 2, NTOK], F32))
            with ExitStack() as weights_stack:
                T_W = weight_buffers(weights_stack, "t_", WT)
                M = region("m_", [("w0", [P, 3 * D], F32), ("w1", [P, 3 * D], F32), ("w2", [P, 3 * D], F32),
                                  ("row", [2, 3 * D], F32)])
                T = region("t_", norm_bufs + [
                    ("junk", [P, D], BF16), ("fa", [P, 2, G], F32), ("ga", [P, 2, G], F32), ("cg", [P, G], F32), ("gb", [P, G], F32)])
                T.update(T_W)
            F = region("f_", [
                ("fa", [P, 2, NTOK], F32), ("sga", [P, 2, NTOK], F32), ("ya", [P, 2, NTOK], F32),
                ("fe", [P, 2, NH + 1], F32), ("fo", [P, 2, NH], F32), ("pq", [P, 8, 2 * FW], F32),
                ("plast", [1, FW], F32), ("pqp", [P, 2, 2 * FW], F32),
                ("cc", [P, 2, FW], F32), ("cs", [P, 2, FW], F32),
                ("ct", [P, 8, 512], F32), ("st", [P, 8, 512], F32), ("sr", [1, 512], F32),
                ("scol", [P, 1], F32), ("pc", [P, 2, NP], F32), ("ps", [P, 2, NP], F32),
                ("sq0", [P, 512], F32), ("sq1", [P, 512], F32), ("cy", [P, NTOK], F32)])
        with ExitStack() as weights_stack:
            N_W = weight_buffers(weights_stack, "n_", WN)
            N = region("n_", norm_bufs + [
                ("rope", [P, 2, HD], F32), ("m1", [P, AW], F32), ("m2", [P, AW], F32),
                ("vs", [P, AW], F32), ("gs", [P, AW], F32),
                ("dup", [P, 8, 2, HD], F32), ("qst0", [P, 4, 2, P], F32), ("qst1", [P, 4, 2, P], F32),
                ("kst0", [P, 4, P], F32), ("kst1", [P, 4, P], F32)])
            N.update(N_W)
            CACHED = [N["m1"], N["m2"], N["vs"], N["gs"]]
        with ExitStack() as weights_stack:
            O_W = weight_buffers(weights_stack, "o_", D)
            A = region("a_", [
                ("kt0", [P, 2, KEYS], F32R), ("kt1", [P, 2, KEYS], F32R), ("v0", [P, KTILES, P], F32), ("v1", [P, KTILES, P], F32),
                ("q0", [P, 2, 2, P], F32R), ("q1", [P, 2, 2, P], F32R),
                ("e0", [P, 2, KEYS], F32), ("e1", [P, 2, KEYS], F32), ("d0", [P, KEYS], F32), ("d1", [P, KEYS], F32),
                ("dt", [P, 5, 4 * P], F32), ("os0", [P, P], F32), ("os1", [P, P], F32),
                ("s0", [P, 24], F32), ("s1", [P, 24], F32)])
            B = region("b_", [
                ("kt", [P, 8, NP], F32R), ("v", [P, 2, AW], F32), ("q", [P, 8, 2, P], F32R),
                ("e", [P, 8, NP], F32), ("d", [P, 4, NP], F32), ("dt", [P, 8, P], F32), ("os", [P, AW], F32),
                ("mx", [P, 8], F32), ("nb", [P, 8], F32), ("ls", [P, 8], F32), ("rl", [P, 8], F32),
                ("c", [P, 4], F32), ("nr", [P, 4], F32)])
            O = region("o_", [
                ("subln", [P, P], F32), ("fg", [P, D], F32), ("gate", [P, 2, D], F32), ("gate_bias", [P, D], F32), ("junk", [P, D], BF16), ("junk2", [P, D], BF16),
                ("o0", [P, AW], F32), ("o1", [P, AW], F32), ("g0", [P, AW], F32), ("g1", [P, AW], F32),
                ("x0", [P, D], F32), ("x1", [P, D], F32), ("yf0", [P, KT, P], F32), ("yf1", [P, KT, P], F32),
                ("yh0", [P, KT, P], F32R), ("yh1", [P, KT, P], F32R), ("yl0", [P, KT, P], F32R), ("yl1", [P, KT, P], F32R),
                ("on", [P, AW], F32), ("on2", [P, AW], F32), ("gated0", [P, AW], F32), ("gated1", [P, AW], F32),
                ("t0", [P, D], F32), ("t1", [P, D], F32), ("xn0", [P, D], F32), ("xn1", [P, D], F32),
                ("y0", [P, D], F32), ("y1", [P, D], F32),
                ("sm0", [P, 16], F32), ("sm1", [P, 16], F32)])
            O.update(O_W)

        psum = es.enter_context(nc.psum_tensor("psum", [P, 8, 512], F32))

        sems = {}

        def S(name):
            if name not in sems:
                sems[name] = es.enter_context(nc.semaphore(name))
            return sems[name]

        def upto(value):
            if isinstance(value, int):
                return max(value, 0)
            assert value.min_val > 0
            return value

        STAGES = 6

        def stage_begin(eng, l, n):
            eng.wait_ge(S("stage_left"), upto(5 * (STAGES * l + n)))

        def stage_end(eng):
            eng.drain().then_inc(S("stage_left"), 1)

        def groups(eng, first, pair, last):
            first(0, 0)
            with eng.Fori(0, 3) as m:
                pair(2 * m + 1, 1)
                pair(2 * m + 2, 0)
            pair(7, 1)
            last(8, 0)

        def near(t, d):
            return not isinstance(t, int) or 0 <= t + d < TILES

        def out_steps(eng, step):
            def pair(m):
                step(2 * m, 0, m)
                step(2 * m + 1, 1, m)
            pair(0)
            pair(1)
            with eng.Fori(2, 7) as m:
                pair(m)
            pair(7)
            pair(8)
            step(TILES, 0, TILES // 2)

        def head_pairs(eng, h, body, last=HEAD_TILES // 2):
            first = 3 if h == 0 else 1
            for m in range(1, first):
                body(m)
            with eng.Fori(first, last) as m:
                body(m)


        def x_load(sp, p, R, l, i):
            for s in (0, 1):
                if not (isinstance(i, int) and i == 0):
                    sp.wait_ge(S(p + "tr"), upto(l * 4 * NG + 4 * (i - 1) + 2 * s + 2))
                src = ins["x_all"] if l == 0 else x_scr
                r0 = i * G + s * P
                sp.dma_start(R[f"xt{s}"][:], src[bass.ds(r0, P), :]).then_inc(S(p + f"x{s}"), 16)

        def norm_act(act, p, R, l, i):
            for s in (0, 1):
                act.wait_ge(S(p + f"x{s}"), 16 * (l * NG + i + 1))
                if s == 0:
                    act.wait_ge(S(p + "ms"), upto(l * NG + i))
                act.wait_ge(S(p + "sq"), upto(2 * (l * NG + i) + s))
                nc.scalar.activation(R["junk"][:], R[f"xt{s}"][:], ACT.Square, accum_out=sqsum[:, s:s + 1]).then_inc(S(p + "sq"), 1)

        def norm_pool(pool, p, l, i):
            pool.wait_ge(S(p + "ms"), l * NG + i + 1)
            nc.gpsimd.tensor_tensor(rstd[:, bass.ds(2 * i, 2)], meansq[:], neg_half[:, 0:2], ALU.pow).then_inc(S(p + "rs"), 1)

        def norm_dve(dve, p, R, l, i, stats):
            if stats:
                dve.wait_ge(S(p + "sq"), 2 * (l * NG + i + 1))
                dve.wait_ge(S(p + "rs"), upto(l * NG + i))
                nc.vector.tensor_scalar(meansq[:], sqsum[:], 1.0 / D, EPS, ALU.mult, ALU.add).then_inc(S(p + "ms"), 1)
                dve.wait_ge(S(p + "rs"), l * NG + i + 1)
            for s in (0, 1):
                dve.wait_ge(S(p + f"x{s}"), 16 * (l * NG + i + 1))
                xt = R[f"xt{s}"]
                nc.vector.tensor_scalar(xt[:], xt[:], rstd[:, bass.ds(2 * i + s, 1)], None, ALU.mult).then_inc(S(p + "xn"), 1)

        def fill_pe(pe, p, R, l, i, q):
            s, kh = q // 2, q % 2
            n = l * 4 * NG + 4 * i + q
            pe.wait_ge(S(p + "xn"), l * 2 * NG + 2 * i + s + 1)
            if not (isinstance(i, int) and i == 0 and q < 2):
                pe.wait_ge(S(p + "ev"), upto(n - 1))
            for kk in range(4):
                k = 4 * kh + kk
                last = nc.tensor.transpose(psum[:, 6 + q % 2, kk * P:(kk + 1) * P], R[f"xt{s}"][:, k * P:(k + 1) * P], id_sb[:])
            last.then_inc(S(p + "tr"), 1)

        def fill_act(act, p, R, l, i, q):
            kh = q % 2
            g = 1 if isinstance(i, int) and i == NG - 1 else 0
            n = l * 4 * NG + 4 * i + q
            act.wait_ge(S(p + "tr"), n + 1)
            if not (isinstance(i, int) and i == 0 and q < 2):
                act.wait_ge(S(p + "lo"), upto(n - 1))
            for kk in range(4):
                k = 4 * kh + kk
                last = nc.scalar.activation(R["hf"][:, q % 2, kk, :], psum[:, 6 + q % 2, kk * P:(kk + 1) * P], ACT.Identity,
                                            bias=mod[:, k, g:g + 1], scale=one_scale[:, k, g:g + 1])
            last.then_inc(S(p + "ev"), 1)

        def fill_dve(dve, p, R, l, i, b, q, mm_per_group):
            s, kh = q // 2, q % 2
            n = l * 4 * NG + 4 * i + q
            dve.wait_ge(S(p + "ev"), n + 1)
            if not (isinstance(i, int) and i == 0):
                dve.wait_ge(S(p + "mm"), upto(mm_per_group * (l * NG + i - 1)))
            nc.vector.tensor_copy(R[f"hh{b}"][:, 4 * kh:4 * kh + 4, s * P:(s + 1) * P], R["hf"][:, q % 2]).then_inc(S(p + "hi"), 1)

        def fill_pool(pool, p, R, l, i, b, q, mm_per_group):
            s, kh = q // 2, q % 2
            pool.wait_ge(S(p + "hi"), l * 4 * NG + 4 * i + q + 1)
            hi = R[f"hh{b}"][:, 4 * kh:4 * kh + 4, s * P:(s + 1) * P]
            nc.gpsimd.tensor_tensor(R[f"hl{b}"][:, 4 * kh:4 * kh + 4, s * P:(s + 1) * P], R["hf"][:, q % 2], hi.bitcast(F32),
                                    ALU.subtract).then_inc(S(p + "lo"), 1)

        PIECES = 4

        def piece(w, c):
            return w[:, 2 * c:2 * c + 2, :]

        def weights_sp(sp, p, l, src, raw):
            for c in range(PIECES):
                sp.dma_start(piece(raw, c), src[l, 2 * c * P:(2 * c + 2) * P, :].rearrange("(k p) w -> p k w", p=P)).then_inc(S(p + f"w{c}"), 16)

        def weights_act(act, p, l, R):
            for c in range(PIECES):
                act.wait_ge(S(p + f"w{c}"), 16 * (l + 1))
                nc.scalar.activation(piece(R["wh"], c), piece(R["wraw"], c), ACT.Copy).then_inc(S(p + "wh"), 1)

        def weights_dve(dve, p, l, R):
            for c in range(PIECES):
                dve.wait_ge(S(p + "wh"), l * PIECES + c + 1)
                nc.vector.tensor_tensor(piece(R["wl"], c), piece(R["wraw"], c), piece(R["wh"], c).bitcast(F32), ALU.subtract).then_inc(S(p + "wl"), 1)

        def split_products(out, terms, inc=None):
            n = len(terms)
            for j, ((wh, wl), (xh, xl)) in enumerate(terms):
                nc.tensor.matmul(out, wh, xh, start=(j == 0), stop=False)
                nc.tensor.matmul(out, wh, xl, start=False, stop=False)
                last = nc.tensor.matmul(out, wl, xh, start=False, stop=(j == n - 1))
            return last

        block = es.enter_context(nc.Block())

        @block.sync
        def _(sp):
            for dst, name in ((id_sb[:], "ident"), (cond_in[:], "cond"), (bmod_sb[:], "b_mod"), (ng_sb[:], "norm_g"), (conv_sb[:], "conv_wb")):
                sp.dma_start(dst, ins[name]).then_inc(S("consts"), 16)
            for l in range(DEPTH):
                stage_begin(sp, l, 0)
                sp.dma_start(lam_in[:], ins["lam_vec"][l:l + 1].partition_broadcast(P)).then_inc(S("lam_in"), 16)
                for k in range(KT):
                    if k >= 3:
                        sp.wait_ge(S("mod_mm"), l * KT + k - 2)
                    sp.dma_start(M[f"w{k % 3}"][:], ins["w_mod"][l, k * P:(k + 1) * P, :]).then_inc(S(f"mod_w{k % 3}"), 16)
                weights_sp(sp, "t_", l, ins["w_in_t"], T["wraw"])
                sp.wait_ge(S("lam_in"), 16 * (l + 1))
                sp.wait_ge(S("mod_row"), l + 1)
                sp.dma_start(gate_scr, M["row"][0:2, 2 * D:3 * D]).then_inc(S("mod_gate"), 16)
                sp.wait_ge(S("mod_gate"), 16 * (l + 1))
                stage_end(sp)

                stage_begin(sp, l, 1)
                x_load(sp, "t_", T, l, 0)

                def t_group(i, b, nxt=True):
                    if nxt:
                        x_load(sp, "t_", T, l, i + 1)
                    for j, (w, scr) in enumerate((("fa", fa_scr), ("ga", sga_scr))):
                        sp.wait_ge(S("t_act"), upto(len(T_ACT) * (l * NG + i) + 2 * j + 2))
                        sp.dma_start(scr[bass.ds(i, 1)].rearrange("g p j n -> (g p) j n"), T[w][:]).then_inc(S("t_st_" + w), 16)
                groups(sp, t_group, t_group, lambda i, b: t_group(i, b, False))
                sp.wait_ge(S("t_st_fa"), upto(16 * (l + 1) * NG))
                sp.wait_ge(S("t_st_ga"), upto(16 * (l + 1) * NG))
                stage_end(sp)

                stage_begin(sp, l, 2)
                def by_group(dst, scr):
                    return [(dst[:, j].rearrange("p (g n) -> p g n", g=NG), scr[:, :, j].rearrange("g p n -> p g n")) for j in (0, 1)]
                for dst, src in by_group(F["fa"], fa_scr) + [(F["cc"][:], ins["chan_cos"]), (F["cs"][:], ins["chan_sin"])]:
                    sp.dma_start(dst, src).then_inc(S("f_in"), 16)
                for dst, src in ((F["ct"], ins["seq_cos"][0]), (F["st"], ins["seq_sin"][0]), (F["sr"], ins["sign_row"]),
                                 (F["scol"], ins["sign_col"]), (F["pc"], ins["prompt_cos"]), (F["ps"], ins["prompt_sin"])):
                    sp.dma_start(dst[:], src).then_inc(S("f_tab"), 16)
                for dst, src in by_group(F["sga"], sga_scr):
                    sp.dma_start(dst, src).then_inc(S("f_sga"), 16)
                sp.wait_ge(S("f_sd"), upto(l * 4 + 2))
                for dst, src in ((F["ct"], ins["seq_cos"][1]), (F["st"], ins["seq_sin"][1])):
                    sp.dma_start(dst[:], src).then_inc(S("f_tab2"), 16)
                for j in (0, 1):
                    sp.wait_ge(S("cv_y"), l * 2 + j + 1)
                    sp.dma_start(yt_scr[:, 2 + j, :], F["cy"][:]).then_inc(S("cv_st"), 16)
                sp.wait_ge(S("f_ya"), l + 1)
                sp.dma_start(yt_scr[:, 0:2, :], F["ya"][:]).then_inc(S("f_st"), 16)
                sp.wait_ge(S("f_st"), 16 * (l + 1))
                sp.wait_ge(S("cv_st"), 32 * (l + 1))
                stage_end(sp)

                stage_begin(sp, l, 3)
                x_load(sp, "n_", N, l, 0)
                for t in range(PAST // P):
                    sp.dma_start(CACHED[t][:], ins["cache_k"][l, t * P:(t + 1) * P, :]).then_inc(S(f"n_ck{t}"), 16)
                weights_sp(sp, "n_", l, ins["w_in_n"], N["wraw"])
                x_load(sp, "n_", N, l, 1)

                def k_store(fill, col, f):
                    sp.wait_ge(S("n_flo"), fill + 1)
                    sp.dma_start(k_scr[:, 4 * f:4 * f + 4, bass.ds(col, P)], N[f"kst{f}"][:]).then_inc(S(f"n_kst{f}"), 16)

                for t in range(PAST // P):
                    for f in (0, 1):
                        k_store(l * 80 + 2 * t + f, t * P, f)

                def n_group(i, b, nxt=True, new=False):
                    for s in (0, 1):
                        tt = 2 * i + s
                        n = l * TILES + tt
                        sp.wait_ge(S("n_rope"), upto(l * TILES * 4 + 4 * tt))
                        sp.dma_start(N["rope"][:], ins["rope"][bass.ds(tt * P, P)]).then_inc(S("n_tab"), 16)
                        sp.wait_ge(S("n_vs"), n + 1)
                        sp.dma_start(v_scr[bass.ds(tt * P, P), :], N["vs"][:]).then_inc(S("n_vst"), 16)
                        if s == 1 and not (isinstance(i, int) and i + 2 >= NG):
                            x_load(sp, "n_", N, l, i + 2)
                        if new:
                            sp.dma_start(new_v[l, s * P:(s + 1) * P, :], N["vs"][:]).then_inc(S("n_newv"), 16)
                        for f in (0, 1):
                            sp.wait_ge(S("n_flo"), l * 80 + 8 + 4 * tt + f + 1)
                            sp.dma_start(q_scr[bass.ds(tt, 1), :, 4 * f:4 * f + 4].rearrange("t p j c n -> p (t j) c n"), N[f"qst{f}"][:]).then_inc(S(f"n_qst{f}"), 16)
                        sp.wait_ge(S("n_gs"), n + 1)
                        sp.dma_start(sgc_scr[bass.ds(tt * P, P), :], N["gs"][:]).then_inc(S("n_gst"), 16)
                        if new:
                            sp.wait_ge(S("n_dup"), upto(l * 40 + 4 + 2 * tt + 2))
                            sp.dma_start(new_k[l, s * P:(s + 1) * P, :].rearrange("p (j d) -> p j d", j=8), N["dup"][:, :, 0, :]).then_inc(S("n_newk"), 16)
                        for f in (0, 1):
                            k_store(l * 80 + 8 + 4 * tt + 2 + f, tt * P + PAST, f)
                groups(sp, n_group, n_group, lambda i, b: n_group(i, b, False, True))
                sp.wait_ge(S("n_vst"), 16 * TILES * (l + 1))
                sp.wait_ge(S("n_gst"), 16 * TILES * (l + 1))
                for f in (0, 1):
                    sp.wait_ge(S(f"n_qst{f}"), 16 * TILES * (l + 1))
                    sp.wait_ge(S(f"n_kst{f}"), 16 * 22 * (l + 1))
                sp.wait_ge(S("n_newv"), 32 * (l + 1))
                sp.wait_ge(S("n_newk"), 32 * (l + 1))
                stage_end(sp)

                stage_begin(sp, l, 4)
                U = l * 64

                def head_load(h):
                    hb = h % 2
                    if h >= 2:
                        sp.wait_ge(S("a_o"), upto(U + 16 * (h - 1)))
                    sp.dma_start(A[f"kt{hb}"][:].bitcast(F32), k_scr[:, 2 * h:2 * h + 2, 0:KEYS]).then_inc(S(f"a_k{hb}"), 16)
                    sp.dma_start(A[f"v{hb}"][:, 0:PAST // P, :], ins["cache_v"][l, :, h * P:(h + 1) * P].rearrange("(t p) d -> p t d", p=P)).then_inc(S(f"a_v{hb}"), 16)
                    sp.dma_start(A[f"v{hb}"][:, PAST // P:, :], v_scr[0:NS, h * P:(h + 1) * P].rearrange("(t p) d -> p t d", p=P)).then_inc(S(f"a_v{hb}"), 16)

                def q_load(h, t, b):
                    if not (isinstance(t, int) and h == 0 and t < 2):
                        sp.wait_ge(S("a_qk"), upto(4 * (U + 16 * h + t - 1)))
                    sp.dma_start(A[f"q{b}"][:].bitcast(F32), q_scr[bass.ds(t, 1), :, 2 * h:2 * h + 2].rearrange("t p j c n -> p (t j) c n")).then_inc(S(f"a_q{b}"), 16)

                def o_store(h, t, b):
                    sp.wait_ge(S("a_os"), U + 16 * h + t + 1)
                    sp.dma_start(o_scr[bass.ds(t * P, P), h * P:(h + 1) * P], A[f"os{b}"][:]).then_inc(S(f"a_st{b}"), 16)

                head_load(0)
                q_load(0, 0, 0)
                head_load(1)
                weights_sp(sp, "o_", l, ins["w_out"], O["wraw"])
                for h in range(HEADS):
                    for b in (0, 1):
                        q_load(h, 1 + b, 1 - b)
                        if h:
                            o_store(h - 1, 14 + b, b)
                    if 1 <= h < HEADS - 1:
                        head_load(h + 1)

                    def pair(m):
                        q_load(h, 2 * m + 1, 1)
                        o_store(h, 2 * m - 2, 0)
                        q_load(h, 2 * m + 2, 0)
                        o_store(h, 2 * m - 1, 1)
                    head_pairs(sp, h, pair, HEAD_TILES // 2 - 1)
                    q_load(h, 15, 1)
                    o_store(h, 12, 0)
                    if h < HEADS - 1:
                        q_load(h + 1, 0, 0)
                    o_store(h, 13, 1)
                o_store(HEADS - 1, 14, 0)
                o_store(HEADS - 1, 15, 1)
                for b in (0, 1):
                    sp.wait_ge(S(f"a_st{b}"), 16 * 32 * (l + 1))
                sp.wait_ge(S("a_o"), upto(U + 64))
                sp.wait_ge(S("a_os"), upto(U + 64))
                sp.dma_start(B["kt"][:].bitcast(F32), k_scr[:, :, KEYS:KEYS + NP]).then_inc(S("b_kv"), 16)
                sp.dma_start(B["v"][:], v_scr[NS:NTOK, :].rearrange("(t p) d -> p t d", p=P)).then_inc(S("b_kv"), 16)
                for t in (0, 1):
                    sp.wait_ge(S("b_qk"), upto(2 * l + t))
                    sp.dma_start(B["q"][:].bitcast(F32), q_scr[NS // P + t]).then_inc(S("b_q"), 16)
                    sp.wait_ge(S("b_os"), 2 * l + t + 1)
                    sp.dma_start(o_scr[NS + t * P:NS + (t + 1) * P, :], B["os"][:]).then_inc(S("b_st"), 16)
                sp.wait_ge(S("b_st"), 32 * (l + 1))
                stage_end(sp)

                stage_begin(sp, l, 5)
                sp.dma_start(O["subln"][:], ins["subln_g"][l:l + 1].partition_broadcast(P)).then_inc(S("o_c"), 16)
                sp.dma_start(O["fg"][:], ins["final_g"].partition_broadcast(P)).then_inc(S("o_c"), 16)
                sp.dma_start(O["gate_bias"][:], ins["b_mod_row"][l:l + 1, 2 * D:].partition_broadcast(P)).then_inc(S("o_g"), 16)
                for g in (0, 1):
                    sp.dma_start(O["gate"][:, g, :], gate_scr[g:g + 1].partition_broadcast(P)).then_inc(S("o_g"), 16)

                def load_attention(t, b):
                    r = bass.ds(t * P, P)
                    if not (isinstance(t, int) and t < 2):
                        sp.wait_ge(S("o_gated"), l * TILES + t - 1)
                    for dst, src in ((O[f"o{b}"][:], o_scr[r, :]), (O[f"g{b}"][:], sgc_scr[r, :])):
                        sp.dma_start(dst, src).then_inc(S(f"o_og{b}"), 16)

                def load_mixed(t, b):
                    r = bass.ds(t * P, P)
                    sp.dma_start(O[f"yf{b}"][:, 0:4, :], yt_scr[:, :, r]).then_inc(S(f"o_yt{b}"), 16)

                def load_x(t, b):
                    r = bass.ds(t * P, P)
                    if not (isinstance(t, int) and t < 2):
                        sp.wait_ge(S("o_xn"), l * TILES + t - 1)
                    sp.dma_start(O[f"x{b}"][:], (ins["x_all"] if l == 0 else x_scr)[r, :]).then_inc(S(f"o_x{b}"), 16)

                def store(t, b):
                    r = bass.ds(t * P, P)
                    if l == DEPTH - 1:
                        sp.wait_ge(S("o_y"), t + 1)
                        sp.dma_start(y_all[r, :], O[f"y{b}"][:]).then_inc(S(f"o_st{b}"), 16)
                    else:
                        sp.wait_ge(S("o_xn"), l * TILES + t + 1)
                        sp.dma_start(x_scr[r, :], O[f"xn{b}"][:]).then_inc(S(f"o_st{b}"), 16)

                for t in (0, 1):
                    load_attention(t, t)
                    load_mixed(t, t)
                load_x(0, 0)
                load_attention(2, 0)

                def step(t, b, m):
                    if isinstance(t, int) and near(t, 2):
                        sp.wait_ge(S("o_lo"), l * TILES + t + 1)
                    if near(t, 3):
                        load_attention(t + 3, 1 - b)
                    if near(t, 2):
                        load_mixed(t + 2, b)
                    if near(t, 1):
                        load_x(t + 1, 1 - b)
                    if near(t, -1):
                        store(t - 1, 1 - b)
                out_steps(sp, step)
                for b in (0, 1):
                    sp.wait_ge(S(f"o_st{b}"), upto(16 * (l + 1) * TILES // 2))
                stage_end(sp)

        @block.tensor
        def _(pe):
            pe.wait_ge(S("consts"), 16 * 5)
            pe.wait_ge(S("ones_set"), 3)
            for l in range(DEPTH):
                stage_begin(pe, l, 0)
                pe.wait_ge(S("cond_act"), 1)
                for k in range(KT):
                    pe.wait_ge(S(f"mod_w{k % 3}"), 16 * (l * ((KT - k % 3 + 2) // 3) + k // 3 + 1))
                    for m in range(6):
                        last = nc.tensor.matmul(psum[0:2, m, :], cond_act[:, k, :], M[f"w{k % 3}"][:, m * 512:(m + 1) * 512],
                                                start=(k == 0), stop=(k == KT - 1))
                    last.then_inc(S("mod_mm"), 1)
                pe.wait_ge(S("mod_row"), l + 1)
                for m in range(16):
                    last = nc.tensor.transpose(psum[:, 6, 2 * m:2 * m + 2], M["row"][0:2, m * P:(m + 1) * P], id_sb[0:2, 0:2])
                last.then_inc(S("mod_col"), 1)
                stage_end(pe)

                stage_begin(pe, l, 1)
                for q in range(4):
                    fill_pe(pe, "t_", T, l, 0, q)
                pe.wait_ge(S("t_wl"), (l + 1) * PIECES)

                def t_group(i, b, nxt=True):
                    pe.wait_ge(S("t_lo"), 4 * (l * NG + i + 1))
                    for m, (w, j) in enumerate(T_ORDER):
                        c = T_COLUMN[w] + j * P
                        first = isinstance(i, int) and i == 0
                        if m >= T_BANKS or not first:
                            o = (m - T_BANKS) % MT
                            back = l * NG + i - (m < T_BANKS)
                            if o in T_ACT:
                                pe.wait_ge(S("t_act"), len(T_ACT) * back + T_ACT.index(o) + 1)
                            else:
                                pe.wait_ge(S("t_dve"), len(T_DVE) * back + T_DVE.index(o) + 1)
                        split_products(psum[:, m % T_BANKS, 0:G],
                                       [((T["wh"][:, k, c:c + P], T["wl"][:, k, c:c + P]), (T[f"hh{b}"][:, k, :], T[f"hl{b}"][:, k, :]))
                                        for k in range(KT)]).then_inc(S("t_mm"), 1)
                        if nxt and m in T_FILL_AFTER:
                            fill_pe(pe, "t_", T, l, i + 1, T_FILL_AFTER[m])
                groups(pe, t_group, t_group, lambda i, b: t_group(i, b, False))
                stage_end(pe)

                stage_begin(pe, l, 2)
                pe.wait_ge(S("f_in"), 64 * (l + 1))
                pe.wait_ge(S("f_fold"), l + 1)
                for t in range(8):
                    pe.wait_ge(S("f_pq"), upto(l * 11 + t - 1 if t >= 2 else 0))
                    for part, (seq, tab) in enumerate(((F["fe"], F["cc"]), (F["fo"], F["cs"]))):
                        for j in (0, 1):
                            last = nc.tensor.matmul(psum[:, t % 2, part * FW:(part + 1) * FW], seq[:, j, t * P:(t + 1) * P], tab[:, j, :], start=(j == 0), stop=(j == 1))
                    last.then_inc(S("f_ch"), 1)
                for j in (0, 1):
                    last = nc.tensor.matmul(psum[0:1, 2, 0:FW], F["fe"][:, j, NH:NH + 1], F["cc"][:, j, :], start=(j == 0), stop=(j == 1))
                last.then_inc(S("f_ch"), 1)
                for t in (0, 1):
                    for part, tab in enumerate((F["cc"], F["cs"])):
                        for j in (0, 1):
                            last = nc.tensor.matmul(psum[:, 3 + t, part * FW:(part + 1) * FW], F["fa"][:, j, NS + t * P:NS + (t + 1) * P], tab[:, j, :], start=(j == 0), stop=(j == 1))
                    last.then_inc(S("f_ch"), 1)
                pe.wait_ge(S("f_tab"), 96 * (l + 1))
                pe.wait_ge(S("f_pq"), upto(l * 11 + 9))
                n = l * 4
                for kc in (0, 1):
                    if kc:
                        pe.wait_ge(S("f_tab2"), 32 * (l + 1))
                    for ct in (0, 1):
                        c = ct * P
                        pe.wait_ge(S("f_out"), upto(n - 1 if 2 * kc + ct >= 2 else 0))
                        cb, sb_ = (5, 6) if ct == 0 else (7, 2)
                        for t in range(8):
                            nc.tensor.matmul(psum[:, cb, :], F["pq"][:, t, c:c + P], F["ct"][:, t, :], start=(t == 0), stop=False)
                        nc.tensor.matmul(psum[:, cb, :], F["plast"][0:1, c:c + P], F["sr"][0:1, :], start=False, stop=True)
                        for t in range(8):
                            last = nc.tensor.matmul(psum[:, sb_, :], F["pq"][:, t, FW + c:FW + c + P], F["st"][:, t, :], start=(t == 0), stop=(t == 7))
                        last.then_inc(S("f_sd"), 1)
                        n += 1
                for ct in (0, 1):
                    c = ct * P
                    for t in range(8):
                        nc.tensor.matmul(psum[:, 0, ct:ct + 1], F["pq"][:, t, c:c + P], F["scol"][:, 0:1], start=(t == 0), stop=False)
                    last = nc.tensor.matmul(psum[:, 0, ct:ct + 1], F["plast"][0:1, c:c + P], ones[0:1, 0:1], start=False, stop=True)
                last.then_inc(S("f_nyq"), 1)
                pe.wait_ge(S("f_pq"), upto(l * 11 + 11))
                for ct in (0, 1):
                    c = ct * P
                    for t in (0, 1):
                        nc.tensor.matmul(psum[:, 1, ct * NP:(ct + 1) * NP], F["pqp"][:, t, c:c + P], F["pc"][:, t, :], start=(t == 0), stop=False)
                        last = nc.tensor.matmul(psum[:, 1, ct * NP:(ct + 1) * NP], F["pqp"][:, t, FW + c:FW + c + P], F["ps"][:, t, :], start=False, stop=(t == 1))
                last.then_inc(S("f_nyq"), 1)
                stage_end(pe)

                stage_begin(pe, l, 3)
                for q in range(4):
                    fill_pe(pe, "n_", N, l, 0, q)

                def dup_fill(n, dups, f):
                    pe.wait_ge(S("n_dup"), upto(dups))
                    if not (isinstance(n, int) and n < 2):
                        pe.wait_ge(S("n_fhi"), upto(n - 1))
                        pe.wait_ge(S("n_flo"), upto(n - 1))
                    for j in range(4):
                        last = nc.tensor.transpose(psum[:, 4 + f, j * P:(j + 1) * P], N["dup"][:, 4 * f + j].rearrange("p a d -> p (a d)"), id_sb[:])
                    last.then_inc(S("n_ftr"), 1)

                for t in range(PAST // P):
                    for f in (0, 1):
                        dup_fill(l * 80 + 2 * t + f, l * 40 + t + 1, f)
                pe.wait_ge(S("n_wl"), (l + 1) * PIECES)

                def n_group(i, b, nxt=True):
                    pe.wait_ge(S("n_lo"), 4 * (l * NG + i + 1))
                    first = isinstance(i, int) and i == 0
                    for s in (0, 1):
                        tt = 2 * i + s
                        for n in range(4):
                            if s or not first:
                                if n < 2:
                                    pe.wait_ge(S("n_rope"), upto(4 * (l * TILES + tt - 1) + 2 * n + 2))
                                else:
                                    pe.wait_ge(S("n_vs" if n == 2 else "n_gs"), upto(l * TILES + tt))
                            split_products(psum[:, n, :],
                                           [((N[f"hh{b}"][:, k, s * P:(s + 1) * P], N[f"hl{b}"][:, k, s * P:(s + 1) * P]),
                                             (N["wh"][:, k, n * AW:(n + 1) * AW], N["wl"][:, k, n * AW:(n + 1) * AW])) for k in range(KT)]).then_inc(S("n_mm"), 1)
                            if n >= 2:
                                for f in (0, 1):
                                    dup_fill(l * 80 + 8 + 4 * tt + 2 * (n - 2) + f, l * 40 + 4 + 2 * tt + n - 1, f)
                            if nxt and 4 * s + n in N_FILL_AFTER:
                                fill_pe(pe, "n_", N, l, i + 1, N_FILL_AFTER[4 * s + n])
                groups(pe, n_group, n_group, lambda i, b: n_group(i, b, False))
                stage_end(pe)

                stage_begin(pe, l, 4)
                U = l * 64

                def scores(h, t, b, part):
                    half, kp = part // 2, part % 2
                    u = U + 16 * h + t
                    if part == 0:
                        pe.wait_ge(S(f"a_q{b}"), 16 * (l * 32 + (8 * h + (t - b) // 2 if isinstance(t, int) else 8 * h + t_pair[0]) + 1))
                        if isinstance(t, int) and t == 0:
                            pe.wait_ge(S(f"a_k{h % 2}"), 16 * (2 * l + h // 2 + 1))
                    if not (isinstance(t, int) and 16 * h + t == 0 and part < 2):
                        pe.wait_ge(S("a_exp"), upto(4 * u + part - 1))
                    q = A[f"q{b}"]
                    kt = A[f"kt{h % 2}"]
                    for bank in ((0, 1, 2), (3, 4))[kp]:
                        keys = kt[:, half, bank * 512:(bank + 1) * 512]
                        nc.tensor.matmul(psum[:, bank, :], q[:, half, 0, :], keys, start=True, stop=False)
                        last = nc.tensor.matmul(psum[:, bank, :], q[:, half, 1, :], keys, start=False, stop=True)
                    last.then_inc(S("a_qk"), 1)

                def turn(u, b, f):
                    if f == 0:
                        pe.wait_ge(S("a_dA"), u + 1)
                    if f == 3:
                        pe.wait_ge(S("a_dB"), u + 1)
                    if f >= 2:
                        if f % 2 == 0:
                            pe.wait_ge(S("a_tevS"), 3 * u + f // 2)
                        else:
                            pe.wait_ge(S("a_tevV"), 2 * u + 1)
                    elif not (isinstance(u, int) and u == 0):
                        if f == 0:
                            pe.wait_ge(S("a_tevV"), 2 * u)
                        else:
                            pe.wait_ge(S("a_tevS"), 3 * u)
                    for j in range(4):
                        kt_ = 4 * f + j
                        last = nc.tensor.transpose(psum[:, 5 + (b + f) % 2, j * P:(j + 1) * P], A[f"d{b}"][:, kt_ * P:(kt_ + 1) * P], id_sb[:])
                    last.then_inc(S("a_tr"), 1)

                def values(h, u, f):
                    if f == 0:
                        if not (isinstance(u, int) and u == 0):
                            pe.wait_ge(S("a_os"), upto(u))
                        pe.wait_ge(S(f"a_v{h % 2}"), 32 * (2 * l + h // 2 + 1))
                    if f % 2 == 0:
                        pe.wait_ge(S("a_tevS"), 3 * u + f // 2 + 1)
                    else:
                        pe.wait_ge(S("a_tevV"), 2 * u + f // 2 + 1)
                    for j in range(4):
                        last = nc.tensor.matmul(psum[:, 7, 0:P], A["dt"][:, f, j * P:(j + 1) * P], A[f"v{h % 2}"][:, 4 * f + j, :],
                                                start=(f == 0 and j == 0), stop=(f == 4 and j == 3))
                    if f == 4:
                        last.then_inc(S("a_o"), 1)

                t_pair = [0]

                def unit(h, t, b, prev):
                    for what, n in A_ORDER:
                        if what == "q":
                            scores(h, t, b, n)
                        elif prev is None:
                            continue
                        elif what == "t":
                            turn(prev[1], b, n)
                        else:
                            values(prev[0], prev[1], n)

                for h in range(HEADS):
                    for b in (0, 1):
                        t_pair[0] = 0
                        unit(h, b, b, (h - 1, U + 16 * h - 2 + b) if h else None)

                    def pair(m):
                        t_pair[0] = m
                        for b in (0, 1):
                            unit(h, 2 * m + b, b, (h, U + 16 * h + 2 * m - 2 + b))
                    head_pairs(pe, h, pair)
                for b in (0, 1):
                    for f in range(5):
                        turn(U + 62 + b, b, f)
                        if f:
                            values(HEADS - 1, U + 62 + b, f - 1)
                    values(HEADS - 1, U + 62 + b, 4)
                pe.wait_ge(S("b_kv"), 32 * (l + 1))
                pe.wait_ge(S("a_os"), upto(U + 64))
                for t in (0, 1):
                    n = 2 * l + t
                    pe.wait_ge(S("b_q"), 16 * (n + 1))
                    pe.wait_ge(S("b_exp"), upto(n))
                    for j in range(8):
                        out = psum[:, j // 2, (j % 2) * NP:(j % 2 + 1) * NP]
                        nc.tensor.matmul(out, B["q"][:, j, 0, :], B["kt"][:, j, :], start=True, stop=False)
                        last = nc.tensor.matmul(out, B["q"][:, j, 1, :], B["kt"][:, j, :], start=False, stop=True)
                    last.then_inc(S("b_qk"), 1)
                    pe.wait_ge(S("b_d"), n + 1)
                    for h in range(HEADS):
                        for k in (0, 1):
                            j = 2 * h + k
                            last = nc.tensor.transpose(psum[:, 4 + j // 4, (j % 4) * P:(j % 4 + 1) * P], B["d"][:, h, k * P:(k + 1) * P], id_sb[:])
                    last.then_inc(S("b_tr"), 1)
                    pe.wait_ge(S("b_dt"), n + 1)
                    for h in range(HEADS):
                        for k in (0, 1):
                            last = nc.tensor.matmul(psum[:, 6, h * P:(h + 1) * P], B["dt"][:, 2 * h + k, :], B["v"][:, k, h * P:(h + 1) * P], start=(k == 0), stop=(k == 1))
                    last.then_inc(S("b_o"), 1)
                stage_end(pe)

                stage_begin(pe, l, 5)
                pe.wait_ge(S("o_wl"), (l + 1) * KT)

                def turn(t, b):
                    n = l * TILES + t
                    pe.wait_ge(S("o_gated"), n + 1)
                    if not (isinstance(t, int) and t < 2):
                        pe.wait_ge(S("o_yf"), n - 1)
                    for j in range(4):
                        last = nc.tensor.transpose(psum[:, 6 + b, j * P:(j + 1) * P], O[f"gated{b}"][:, j * P:(j + 1) * P], id_sb[:])
                    last.then_inc(S("o_tr"), 1)

                def products(t, b):
                    n = l * TILES + t
                    pe.wait_ge(S("o_lo"), n + 1)
                    for c in (0, 1):
                        if not (isinstance(t, int) and t < 2):
                            pe.wait_ge(S("o_mg"), 2 * (n - 2) + c + 1)
                        split_products(psum[:, 2 * b + c, :],
                                       [((O[f"yh{b}"][:, k, :], O[f"yl{b}"][:, k, :]), (O["wh"][:, k, c * 512:(c + 1) * 512], O["wl"][:, k, c * 512:(c + 1) * 512]))
                                        for k in range(KT)]).then_inc(S("o_mm"), 1)

                turn(0, 0)

                def step(t, b, m):
                    if near(t, 1):
                        turn(t + 1, 1 - b)
                    if near(t, 0):
                        products(t, b)
                out_steps(pe, step)
                stage_end(pe)

        @block.scalar
        def _(act):
            act.wait_ge(S("consts"), 16 * 5)
            nc.scalar.activation(cond_act[:], cond_in[:], ACT.Silu).then_inc(S("cond_act"), 1)
            for l in range(DEPTH):
                stage_begin(act, l, 0)
                act.wait_ge(S("lam_sum"), l + 1)
                nc.scalar.activation(lam_exp[:], lam_sum[:], ACT.Exp).then_inc(S("lam_exp"), 1)
                act.wait_ge(S("mod_mm"), KT * (l + 1))
                nc.scalar.activation(M["row"][0:2, :].rearrange("p (a b) -> p a b", a=6), psum[0:2, 0:6, :], ACT.Copy).then_inc(S("mod_row"), 1)
                weights_act(act, "t_", l, T)
                stage_end(act)

                stage_begin(act, l, 1)
                norm_act(act, "t_", T, l, 0)
                for q in range(4):
                    fill_act(act, "t_", T, l, 0, q)

                def t_group(i, b, nxt=True):
                    if nxt:
                        norm_act(act, "t_", T, l, i + 1)
                    gi = l * NG + i
                    for m, (w, j) in enumerate(T_ORDER):
                        if m in T_ACT:
                            act.wait_ge(S("t_mm"), MT * gi + m + 1)
                            src = psum[:, m % T_BANKS, 0:G]
                            if w in ("fa", "ga"):
                                if j == 0:
                                    act.wait_ge(S("t_st_" + w), upto(16 * gi))
                                ins_ = nc.scalar.activation(T[w][:, j, :], src, ACT.Copy if w == "fa" else ACT.Silu)
                            elif w == "cg":
                                act.wait_ge(S("t_dve"), upto(4 * gi + (1 if j else 0)))
                                ins_ = nc.scalar.activation(T["cg"][:], src, ACT.Copy)
                            else:
                                act.wait_ge(S("t_dve"), upto(4 * gi + (2 if j else 0)))
                                ins_ = nc.scalar.activation(T["gb"][:], src, ACT.Silu)
                            ins_.then_inc(S("t_act"), 1)
                        if nxt and m in T_FILL_AFTER:
                            fill_act(act, "t_", T, l, i + 1, T_FILL_AFTER[m])
                groups(act, t_group, t_group, lambda i, b: t_group(i, b, False))
                stage_end(act)

                stage_begin(act, l, 2)
                for t in range(8):
                    act.wait_ge(S("f_ch"), l * 11 + t + 1)
                    nc.scalar.activation(F["pq"][:, t, :], psum[:, t % 2, :], ACT.Copy).then_inc(S("f_pq"), 1)
                act.wait_ge(S("f_ch"), upto(l * 11 + 9))
                nc.scalar.activation(F["plast"][0:1, :], psum[0:1, 2, 0:FW], ACT.Copy).then_inc(S("f_pq"), 1)
                for t in (0, 1):
                    act.wait_ge(S("f_ch"), upto(l * 11 + 10 + t))
                    nc.scalar.activation(F["pqp"][:, t, :], psum[:, 3 + t, :], ACT.Copy).then_inc(S("f_pq"), 1)
                for j in (0, 1):
                    act.wait_ge(S("cv_st"), upto(16 * (2 * l + j)))
                    nc.scalar.activation(F["cy"][:], z[:, j, :], ACT.Identity, bias=conv_sb[:, l, j, 3:4], scale=conv_sb[:, l, j, 1:2]).then_inc(S("cv_mid"), 1)
                for n in range(4):
                    act.wait_ge(S("f_sd"), l * 4 + n + 1)
                    act.wait_ge(S("f_out"), upto(l * 4 + n - 1 if n >= 2 else 0))
                    nc.scalar.activation(F[f"sq{n % 2}"][:], psum[:, 6 if n % 2 == 0 else 2, :], ACT.Copy).then_inc(S("f_sq"), 1)
                stage_end(act)

                stage_begin(act, l, 3)
                for q in range(4):
                    fill_act(act, "n_", N, l, 0, q)
                weights_act(act, "n_", l, N)

                def dup_hi(n, kind, stores, f):
                    act.wait_ge(S("n_ftr"), n + 1)
                    act.wait_ge(S(f"n_{kind}{f}"), upto(16 * stores))
                    src = psum[:, 4 + f, :].rearrange("p (j n) -> p j n", j=4)
                    dst = N[f"qst{f}"][:, :, 0, :] if kind == "qst" else N[f"kst{f}"][:]
                    nc.scalar.activation(dst.bitcast(F32R), src, ACT.Copy).then_inc(S("n_fhi"), 1)

                for t in range(PAST // P):
                    for f in (0, 1):
                        dup_hi(l * 80 + 2 * t + f, "kst", l * 22 + t, f)

                def n_group(i, b, nxt=True):
                    for s in (0, 1):
                        tt = 2 * i + s
                        nt = l * TILES + tt
                        for n in range(4):
                            if n == 2:
                                act.wait_ge(S("n_mm"), upto(4 * nt + 3))
                                act.wait_ge(S("n_vst"), upto(16 * nt))
                                if isinstance(i, int) and i == NG - 1:
                                    act.wait_ge(S("n_newv"), upto(16 * (2 * l + s)))
                                nc.scalar.activation(N["vs"][:], psum[:, 2, :], ACT.Copy).then_inc(S("n_vs"), 1)
                                for f in (0, 1):
                                    dup_hi(l * 80 + 8 + 4 * tt + f, "qst", nt, f)
                            if n == 3:
                                act.wait_ge(S("n_mm"), upto(4 * nt + 4))
                                act.wait_ge(S("n_gst"), upto(16 * nt))
                                nc.scalar.activation(N["gs"][:], psum[:, 3, :], ACT.Silu).then_inc(S("n_gs"), 1)
                                for f in (0, 1):
                                    dup_hi(l * 80 + 8 + 4 * tt + 2 + f, "kst", l * 22 + 4 + tt, f)
                            if nxt and 4 * s + n in N_FILL_AFTER:
                                fill_act(act, "n_", N, l, i + 1, N_FILL_AFTER[4 * s + n])
                groups(act, n_group, n_group, lambda i, b: n_group(i, b, False))
                stage_end(act)

                stage_begin(act, l, 4)
                U = l * 64

                def exps(u, b, part):
                    half, kp = part // 2, part % 2
                    st = A[f"s{b}"]
                    act.wait_ge(S("a_nb"), 4 * u + part + 1)
                    if part == 0 and not (isinstance(u, int) and u < 2):
                        act.wait_ge(S("a_dA"), upto(u - 1))
                        act.wait_ge(S("a_dB"), upto(u - 1))
                    keys = slice(0, KEYS_A) if kp == 0 else slice(KEYS_A, KEYS)
                    nc.scalar.activation(A[f"e{b}"][:, half, keys].rearrange("p (o w) -> p o w", w=512), psum[:, 3 * kp:5 if kp else 3, :],
                                         ACT.Exp, bias=st[:, 4 + part:5 + part], scale=SCALE, accum_out=st[:, 8 + part:9 + part]).then_inc(S("a_exp"), 1)
                    if kp == 1:
                        nc.scalar.activation(st[:, 12 + half:13 + half], st[:, part - 1:part], ACT.Exp, bias=st[:, 4 + part:5 + part],
                                             scale=SCALE).then_inc(S("a_al"), 1)

                def turn_act(u, b, f):
                    act.wait_ge(S("a_tr"), 5 * u + f + 1)
                    nc.scalar.activation(A["dt"][:, f, :], psum[:, 5 + (b + f) % 2, :], ACT.Copy).then_inc(S("a_tevS"), 1)

                def output(u, b, stored):
                    act.wait_ge(S("a_o"), u + 1)
                    act.wait_ge(S(f"a_st{b}"), upto(16 * stored))
                    nc.scalar.activation(A[f"os{b}"][:], psum[:, 7, 0:P], ACT.Identity, scale=A[f"s{b}"][:, 20:21]).then_inc(S("a_os"), 1)

                def unit(u, b, prev):
                    if prev is not None:
                        turn_act(prev, b, 0)
                    exps(u, b, 0)
                    if prev is not None:
                        turn_act(prev, b, 2)
                    exps(u, b, 1)
                    if prev is not None:
                        turn_act(prev, b, 4)
                    exps(u, b, 2)
                    exps(u, b, 3)

                for h in range(HEADS):
                    u0 = U + 16 * h
                    for b in (0, 1):
                        if h:
                            output(u0 - 3 + b, 1 - b, u0 // 2 - 2 + b)
                        unit(u0 + b, b, u0 - 2 + b if h else None)
                        for k in W_OUT_SLOTS[h][b]:
                            act.wait_ge(S(f"o_w{k // 2}"), 16 * (l + 1))
                            nc.scalar.activation(O["wh"][:, k, :], O["wraw"][:, k, :], ACT.Copy).then_inc(S("o_wh"), 1)

                    def pair(m):
                        for b in (0, 1):
                            if not (isinstance(m, int) and h == 0 and 2 * m + b < 3):
                                output(u0 + 2 * m - 3 + b, 1 - b, u0 // 2 + m - 2 + b)
                            unit(u0 + 2 * m + b, b, u0 + 2 * m - 2 + b)
                    head_pairs(act, h, pair)
                for b in (0, 1):
                    output(U + 61 + b, 1 - b, U // 2 + 30 + b)
                    for f in (0, 2, 4):
                        turn_act(U + 62 + b, b, f)
                output(U + 63, 1, U // 2 + 31)
                for t in (0, 1):
                    n = 2 * l + t
                    act.wait_ge(S("b_nb"), n + 1)
                    act.wait_ge(S("b_d"), upto(n))
                    for j in range(8):
                        last = nc.scalar.activation(B["e"][:, j, :], psum[:, j // 2, (j % 2) * NP:(j % 2 + 1) * NP], ACT.Exp,
                                                    bias=B["nb"][:, j:j + 1], scale=SCALE, accum_out=B["ls"][:, j:j + 1])
                    last.then_inc(S("b_exp"), 1)
                    act.wait_ge(S("b_tr"), n + 1)
                    nc.scalar.activation(B["dt"][:].rearrange("p (a b) n -> p a (b n)", a=2), psum[:, 4:6, :], ACT.Copy).then_inc(S("b_dt"), 1)
                stage_end(act)

                stage_begin(act, l, 5)
                def norm(t, b, half):
                    n = l * TILES + t
                    act.wait_ge(S(f"o_og{b}"), 32 * (l * TILES // 2 + half + 1))
                    if not (isinstance(t, int) and t < 2):
                        act.wait_ge(S("o_ms"), n - 1)
                    act.wait_ge(S("o_sq"), upto(n))
                    for h in range(HEADS):
                        last = nc.scalar.activation(O["junk"][:, h * P:(h + 1) * P], O[f"o{b}"][:, h * P:(h + 1) * P], ACT.Square,
                                                    accum_out=O[f"sm{b}"][:, h:h + 1])
                    last.then_inc(S("o_sq"), 1)

                def hi(t, b, half):
                    n = l * TILES + t
                    act.wait_ge(S("o_tr"), n + 1)
                    if not (isinstance(t, int) and t < 2):
                        act.wait_ge(S("o_lo"), n - 1)
                    nc.scalar.activation(O[f"yf{b}"][:, 4:8, :].rearrange("p a n -> p (a n)"), psum[:, 6 + b, :], ACT.Copy).then_inc(S("o_yf"), 1)
                    act.wait_ge(S("o_yf"), n + 1)
                    act.wait_ge(S(f"o_yt{b}"), 16 * (l * TILES // 2 + half + 1))
                    if not (isinstance(t, int) and t < 2):
                        act.wait_ge(S("o_mm"), 2 * (n - 1))
                    nc.scalar.activation(O[f"yh{b}"][:], O[f"yf{b}"][:], ACT.Copy).then_inc(S("o_hi"), 1)

                def final_square(t, b):
                    act.wait_ge(S("o_xn"), l * TILES + t + 1)
                    act.wait_ge(S("o_fsq"), upto(t))
                    nc.scalar.activation(O["junk2"][:], O[f"xn{b}"][:], ACT.Square, accum_out=O[f"sm{b}"][:, 12:13]).then_inc(S("o_fsq"), 1)

                norm(0, 0, 0)
                norm(1, 1, 0)
                hi(0, 0, 0)

                def step(t, b, m):
                    if near(t, 1):
                        hi(t + 1, 1 - b, m + b)
                    if near(t, 2):
                        norm(t + 2, b, m + 1)
                    if near(t, -1) and l == DEPTH - 1:
                        final_square(t - 1, 1 - b)
                out_steps(act, step)
                stage_end(act)

        @block.vector
        def _(dve):
            chain = [0]

            def linked(instruction):
                chain[0] += 1
                instruction.then_inc(S("dve_chain"), 1)
                dve.wait_ge(S("dve_chain"), chain[0])

            nc.vector.memset(ones[:], 1.0).then_inc(S("ones_set"), 1)
            nc.vector.memset(neg_half[:], -0.5).then_inc(S("ones_set"), 1)
            nc.vector.memset(lam_sum[:], 0.0).then_inc(S("ones_set"), 1)
            dve.wait_ge(S("consts"), 16 * 5)
            for l in range(DEPTH):
                stage_begin(dve, l, 0)
                dve.wait_ge(S("lam_in"), 16 * (l + 1))
                linked(nc.vector.tensor_tensor(lam_pr[:], lam_in[:, 0::2, :], lam_in[:, 1::2, :], ALU.mult))
                nc.vector.tensor_reduce(lam_sum[:], lam_pr[:], AX_X, ALU.add).then_inc(S("lam_sum"), 1)
                dve.wait_ge(S("lam_exp"), l + 1)
                lam_init = 0.8 - 0.6 * math.exp(-0.3 * l)
                linked(nc.vector.scalar_tensor_tensor(lam[:], lam_exp[:, 0:1], lam_init, lam_exp[:, 1:2], ALU.add, ALU.subtract))
                dve.wait_ge(S("mod_col"), l + 1)
                linked(nc.vector.tensor_tensor(mod[:], psum[:, 6, 0:32].rearrange("p (m g) -> p m g", g=2),
                                               bmod_sb[:, l, 0:16].unsqueeze(2).broadcast_to([P, 16, 2]), ALU.add))
                linked(nc.vector.tensor_scalar(one_scale[:], mod[:, 8:16, :], 1.0, None, ALU.add))
                linked(nc.vector.tensor_tensor(one_scale[:], one_scale[:], ng_sb[:, l].unsqueeze(2).broadcast_to([P, KT, 2]), ALU.mult))
                weights_dve(dve, "t_", l, T)
                stage_end(dve)

                stage_begin(dve, l, 1)
                norm_dve(dve, "t_", T, l, 0, True)
                for q in range(4):
                    fill_dve(dve, "t_", T, l, 0, 0, q, MT)

                def t_group(i, b, nxt=True):
                    if nxt:
                        norm_dve(dve, "t_", T, l, i + 1, True)
                    gi = l * NG + i
                    for m, (w, j) in enumerate(T_ORDER):
                        if m in T_DVE:
                            dve.wait_ge(S("t_mm"), MT * gi + m + 1)
                            dve.wait_ge(S("t_act"), len(T_ACT) * gi + T_ACT.index(m - 1) + 1)
                            dst, other = (z, T["cg"]) if w == "hc" else (bgs, T["gb"])
                            nc.vector.tensor_tensor(dst[:, j, bass.ds(i * G, G)], psum[:, m % T_BANKS, 0:G], other[:], ALU.mult).then_inc(S("t_dve"), 1)
                        if nxt and m in T_FILL_AFTER:
                            fill_dve(dve, "t_", T, l, i + 1, 1 - b, T_FILL_AFTER[m], MT)
                groups(dve, t_group, t_group, lambda i, b: t_group(i, b, False))
                stage_end(dve)

                stage_begin(dve, l, 2)
                dve.wait_ge(S("f_in"), 64 * (l + 1))
                fa, fe, fo, ya, sga = F["fa"], F["fe"], F["fo"], F["ya"], F["sga"]
                for j in (0, 1):
                    nc.vector.tensor_tensor(fe[:, j, 1:NH], fa[:, j, 1:NH], fa[:, j, NS - 1:NH:-1], ALU.add)
                    nc.vector.tensor_tensor(fo[:, j, 1:NH], fa[:, j, 1:NH], fa[:, j, NS - 1:NH:-1], ALU.subtract)
                nc.vector.tensor_copy(fe[:, :, 0:NH + 1:NH], fa[:, :, 0:NH + 1:NH])
                nc.vector.memset(fo[:, :, 0:1], 0.0).then_inc(S("f_fold"), 1)
                for j in (0, 1):
                    dve.wait_ge(S("cv_mid"), 2 * l + j + 1)
                    cy = F["cy"]
                    for tap, to, frm in ((0, 1, 0), (2, 0, 1)):
                        for a, b in ((0, NS), (NS, NTOK)):
                            ins_ = nc.vector.scalar_tensor_tensor(cy[:, a + to:b - frm], z[:, j, a + frm:b - to], conv_sb[:, l, j, tap:tap + 1],
                                                                  cy[:, a + to:b - frm], ALU.mult, ALU.add)
                        linked(ins_)
                    nc.vector.tensor_tensor(cy[:], cy[:], bgs[:, j, :], ALU.mult).then_inc(S("cv_y"), 1)
                for n in range(4):
                    kc, ct = n // 2, n % 2
                    dve.wait_ge(S("f_sq"), l * 4 + n + 1)
                    cb = psum[:, 5 if ct == 0 else 7, :]
                    sq = F[f"sq{n % 2}"]
                    a = kc * 512
                    nc.vector.tensor_tensor(ya[:, ct, a:a + 512], cb, sq[:], ALU.subtract)
                    o = 1 if kc == 0 else 0
                    top = NS - a - o
                    nc.vector.tensor_tensor(ya[:, ct, top:top - (512 - o):-1], cb[:, o:512], sq[:, o:512], ALU.add).then_inc(S("f_out"), 1)
                dve.wait_ge(S("f_nyq"), 2 * (l + 1))
                nc.vector.tensor_copy(ya[:, :, NH:NH + 1], psum[:, 0, 0:2].unsqueeze(2))
                linked(nc.vector.tensor_copy(ya[:, :, NS:NTOK], psum[:, 1, :].rearrange("p (a b) -> p a b", a=2)))
                dve.wait_ge(S("f_sga"), 32 * (l + 1))
                nc.vector.tensor_tensor(ya[:], ya[:], sga[:], ALU.mult).then_inc(S("f_ya"), 1)
                stage_end(dve)

                stage_begin(dve, l, 3)
                norm_dve(dve, "n_", N, l, 0, False)
                for q in range(4):
                    fill_dve(dve, "n_", N, l, 0, 0, q, 8)
                weights_dve(dve, "n_", l, N)

                def dup_lo(n, kind, f):
                    dve.wait_ge(S("n_fhi"), n + 1)
                    if kind == "qst":
                        src = psum[:, 4 + f, :].rearrange("p (j n) -> p j n", j=4)
                        ins_ = nc.vector.tensor_tensor(N[f"qst{f}"][:, :, 1, :].bitcast(F32R), src, N[f"qst{f}"][:, :, 0, :], ALU.subtract)
                    else:
                        src = psum[HD:P, 4 + f, :].rearrange("p (j n) -> p j n", j=4)
                        ins_ = nc.vector.tensor_tensor(N[f"kst{f}"][HD:P].bitcast(F32R), src, N[f"kst{f}"][HD:P], ALU.subtract)
                    ins_.then_inc(S("n_flo"), 1)
                    return ins_

                for t in range(PAST // P):
                    for f in (0, 1):
                        dup_lo(l * 80 + 2 * t + f, "kst", f)

                def rope(tt, n):
                    nt = l * TILES + tt
                    dve.wait_ge(S("n_mm"), 4 * nt + n + 1)
                    dve.wait_ge(S("n_tab"), 16 * (nt + 1))
                    dve.wait_ge(S("n_dup"), upto(l * 40 + 4 + 2 * tt + n))
                    cos = N["rope"][:, 0].unsqueeze(1).broadcast_to([P, 8, HD])
                    nc.vector.tensor_tensor(N["m1"][:].rearrange("p (j d) -> p j d", j=8), psum[:, n, :].rearrange("p (j d) -> p j d", j=8), cos, ALU.mult).then_inc(S("n_rope"), 1)
                    src = psum[:, n, :].rearrange("p (j r a w) -> p j r a w", j=8, r=2, a=2)
                    dst = N["m2"][:].rearrange("p (j r a w) -> p j r a w", j=8, r=2, a=2)
                    sin = N["rope"][:, 1].rearrange("p (r a w) -> p r a w", r=2, a=2)
                    for a in (0, 1):
                        ins_ = nc.vector.tensor_tensor(dst[:, :, :, a, :], src[:, :, :, 1 - a, :], sin[:, :, a, :].unsqueeze(1).broadcast_to([P, 8, 2, 16]), ALU.mult)
                    ins_.then_inc(S("n_rope"), 1)

                def n_group(i, b, nxt=True):
                    if nxt:
                        norm_dve(dve, "n_", N, l, i + 1, False)
                    for s in (0, 1):
                        tt = 2 * i + s
                        for n in range(4):
                            if n < 2:
                                rope(tt, n)
                            if n == 2:
                                for f in (0, 1):
                                    dup_lo(l * 80 + 8 + 4 * tt + f, "qst", f)
                            if n == 3:
                                for f in (0, 1):
                                    dup_lo(l * 80 + 8 + 4 * tt + 2 + f, "kst", f)
                            if nxt and 4 * s + n in N_FILL_AFTER:
                                fill_dve(dve, "n_", N, l, i + 1, 1 - b, N_FILL_AFTER[4 * s + n], 8)
                groups(dve, n_group, n_group, lambda i, b: n_group(i, b, False))
                stage_end(dve)

                stage_begin(dve, l, 4)
                U = l * 64

                def maxima(u, b, part):
                    half, kp = part // 2, part % 2
                    st = A[f"s{b}"]
                    dve.wait_ge(S("a_qk"), 4 * u + part + 1)
                    if part == 0 and not (isinstance(u, int) and u < 2):
                        dve.wait_ge(S("a_dB"), upto(u - 1))
                    nc.vector.tensor_reduce(st[:, part:part + 1], psum[:, 3 * kp:5 if kp else 3, :], mybir.AxisListType.XY,
                                            ALU.max).then_inc(S("a_mx"), 1)
                    dve.wait_ge(S("a_mx"), 4 * u + part + 1)
                    if kp == 0:
                        nc.vector.tensor_scalar(st[:, 4 + part:5 + part], st[:, part:part + 1], -SCALE, None, ALU.mult).then_inc(S("a_nb"), 1)
                    else:
                        nc.vector.tensor_scalar(st[:, 4 + part:5 + part], st[:, part:part + 1], st[:, part - 1:part], -SCALE, ALU.max, ALU.mult).then_inc(S("a_nb"), 1)

                SMALL = 3

                def small(u, n, ins_):
                    ins_.then_inc(S("a_sm"), 1)
                    dve.wait_ge(S("a_sm"), SMALL * u + n + 1)

                def factors(u, b):
                    st = A[f"s{b}"]
                    c = lambda i, w=1: st[:, i:i + w]
                    dve.wait_ge(S("a_exp"), upto(4 * u + 4))
                    dve.wait_ge(S("a_al"), upto(2 * u + 2))
                    if not (isinstance(u, int) and u < 2):
                        dve.wait_ge(S("a_os"), upto(u - 1))
                    for half in (0, 1):
                        ins_ = nc.vector.scalar_tensor_tensor(c(14 + half), c(8 + 2 * half), c(12 + half), c(9 + 2 * half), ALU.mult, ALU.add)
                    small(u, 0, ins_)
                    small(u, 1, nc.vector.reciprocal(c(16, 2), c(14, 2)))
                    nc.vector.tensor_scalar(c(20), c(16), -1.0, None, ALU.mult)
                    small(u, 2, nc.vector.scalar_tensor_tensor(c(18), c(14), lam[:, 0:1], c(17), ALU.mult, ALU.mult))
                    nc.vector.tensor_scalar(c(19), c(18), c(13), None, ALU.mult).then_inc(S("a_c"), 1)

                def combine(u, b):
                    e = A[f"e{b}"]
                    dve.wait_ge(S("a_c"), u + 1)
                    dve.wait_ge(S("a_e1"), u + 1)
                    if not (isinstance(u, int) and u < 2):
                        dve.wait_ge(S("a_tr"), upto(5 * (u - 1)))
                    nc.vector.scalar_tensor_tensor(A[f"d{b}"][:, 0:KEYS_A], e[:, 1, 0:KEYS_A], A[f"s{b}"][:, 19:20], e[:, 0, 0:KEYS_A],
                                                   ALU.mult, ALU.subtract).then_inc(S("a_dA"), 1)

                def turn_dve(u, b, f):
                    dve.wait_ge(S("a_tr"), 5 * u + f + 1)
                    nc.vector.tensor_copy(A["dt"][:, f, :], psum[:, 5 + (b + f) % 2, :]).then_inc(S("a_tevV"), 1)

                def unit(u, b, first=False):
                    lone = first and b == 0
                    maxima(u, b, 0)
                    if not first:
                        turn_dve(u - 2, b, 1)
                    if not lone:
                        factors(u - 1, 1 - b)
                    maxima(u, b, 1)
                    if not first:
                        turn_dve(u - 2, b, 3)
                    maxima(u, b, 2)
                    if not lone:
                        combine(u - 1, 1 - b)
                    maxima(u, b, 3)

                for h in range(HEADS):
                    u0 = U + 16 * h
                    for b in (0, 1):
                        unit(u0 + b, b, h == 0)

                    def pair(m):
                        for b in (0, 1):
                            unit(u0 + 2 * m + b, b)
                    head_pairs(dve, h, pair)
                factors(U + 63, 1)
                turn_dve(U + 62, 0, 1)
                turn_dve(U + 62, 0, 3)
                combine(U + 63, 1)
                turn_dve(U + 63, 1, 1)
                turn_dve(U + 63, 1, 3)
                for t in (0, 1):
                    n = 2 * l + t
                    dve.wait_ge(S("b_qk"), n + 1)
                    linked(nc.vector.tensor_reduce(B["mx"][:], psum[:, 0:4, :].rearrange("p a (b n) -> p (a b) n", b=2), AX_X, ALU.max))
                    nc.vector.tensor_scalar(B["nb"][:], B["mx"][:], -SCALE, None, ALU.mult).then_inc(S("b_nb"), 1)
                    dve.wait_ge(S("b_exp"), n + 1)
                    linked(nc.vector.reciprocal(B["rl"][:], B["ls"][:]))
                    linked(nc.vector.tensor_scalar(B["nr"][:], B["rl"][:, 0::2], -1.0, None, ALU.mult))
                    linked(nc.vector.scalar_tensor_tensor(B["c"][:], B["ls"][:, 0::2], lam[:, 0:1], B["rl"][:, 1::2], ALU.mult, ALU.mult))
                    dve.wait_ge(S("b_tr"), upto(n))
                    for h in range(HEADS):
                        last = nc.vector.scalar_tensor_tensor(B["d"][:, h, :], B["e"][:, 2 * h + 1, :], B["c"][:, h:h + 1], B["e"][:, 2 * h, :], ALU.mult, ALU.subtract)
                    last.then_inc(S("b_d"), 1)
                    dve.wait_ge(S("b_o"), n + 1)
                    dve.wait_ge(S("b_st"), upto(16 * n))
                    nc.vector.tensor_tensor(B["os"][:].rearrange("p (h d) -> p h d", h=HEADS), psum[:, 6, :].rearrange("p (h d) -> p h d", h=HEADS),
                                            B["nr"][:].unsqueeze(2).broadcast_to([P, HEADS, P]), ALU.mult).then_inc(S("b_os"), 1)
                stage_end(dve)

                stage_begin(dve, l, 5)
                dve.wait_ge(S("o_c"), 32 * (l + 1))
                linked(nc.vector.tensor_scalar(O["subln"][:], O["subln"][:], 1.0 - lam_init, None, ALU.mult))

                def scale(t, b):
                    n = l * TILES + t
                    sm = O[f"sm{b}"]
                    dve.wait_ge(S("o_sq"), n + 1)
                    nc.vector.tensor_scalar(sm[:, 4:8], sm[:, 0:4], 1.0 / P, EPS, ALU.mult, ALU.add).then_inc(S("o_ms"), 1)
                    dve.wait_ge(S("o_rs"), n + 1)
                    hv = lambda x: x[:].rearrange("p (h d) -> p h d", h=HEADS)
                    nc.vector.tensor_tensor(hv(O["on"]), hv(O[f"o{b}"]), sm[:, 8:12].unsqueeze(2).broadcast_to([P, HEADS, P]), ALU.mult).then_inc(S("o_y1"), 1)
                    dve.wait_ge(S("o_y1"), n + 1)
                    nc.vector.tensor_tensor(hv(O["on2"]), hv(O["on"]), O["subln"][:].unsqueeze(1).broadcast_to([P, HEADS, P]), ALU.mult).then_inc(S("o_y2"), 1)
                    dve.wait_ge(S("o_y2"), n + 1)
                    if not (isinstance(t, int) and t < 2):
                        dve.wait_ge(S("o_tr"), n - 1)
                    nc.vector.tensor_tensor(O[f"gated{b}"][:], O["on2"][:], O[f"g{b}"][:], ALU.mult).then_inc(S("o_gated"), 1)

                def lo(t, b):
                    dve.wait_ge(S("o_hi"), l * TILES + t + 1)
                    nc.vector.tensor_tensor(O[f"yl{b}"][:], O[f"yf{b}"][:], O[f"yh{b}"][:].bitcast(F32), ALU.subtract).then_inc(S("o_lo"), 1)

                def mod_gate(t, b, g):
                    n = l * TILES + t
                    if not (isinstance(t, int) and t < 2):
                        dve.wait_ge(S("o_xn"), n - 1)
                    for c in (0, 1):
                        dve.wait_ge(S("o_mm"), 2 * n + c + 1)
                        nc.vector.tensor_tensor(O[f"t{b}"][:, c * 512:(c + 1) * 512], psum[:, 2 * b + c, :], O["gate"][:, g, c * 512:(c + 1) * 512], ALU.mult).then_inc(S("o_mg"), 1)

                def final_norm(t, b, half):
                    sm = O[f"sm{b}"]
                    dve.wait_ge(S("o_fsq"), t + 1)
                    nc.vector.tensor_scalar(sm[:, 13:14], sm[:, 12:13], 1.0 / D, EPS, ALU.mult, ALU.add).then_inc(S("o_fms"), 1)
                    dve.wait_ge(S("o_frs"), t + 1)
                    dve.wait_ge(S(f"o_st{b}"), upto(16 * (l * TILES // 2 + half)))
                    nc.vector.scalar_tensor_tensor(O[f"y{b}"][:], O[f"xn{b}"][:], sm[:, 14:15], O["fg"][:], ALU.mult, ALU.mult).then_inc(S("o_y"), 1)

                scale(0, 0)
                scale(1, 1)
                lo(0, 0)
                dve.wait_ge(S("o_g"), 48 * (l + 1))
                linked(nc.vector.tensor_tensor(O["gate"][:], O["gate"][:], O["gate_bias"][:].unsqueeze(1).broadcast_to([P, 2, D]), ALU.add))

                def step(t, b, m):
                    if near(t, -1):
                        mod_gate(t - 1, 1 - b, 1 if isinstance(t, int) and (t - 1) * P >= NS else 0)
                    if near(t, 1):
                        lo(t + 1, 1 - b)
                    if near(t, 2):
                        scale(t + 2, b)
                    if near(t, -1) and l == DEPTH - 1:
                        final_norm(t - 1, 1 - b, m - 1 + b)
                out_steps(dve, step)
                stage_end(dve)

        @block.gpsimd
        def _(pool):
            pool.wait_ge(S("ones_set"), 3)
            for l in range(DEPTH):
                stage_begin(pool, l, 0)
                stage_end(pool)

                stage_begin(pool, l, 1)
                norm_pool(pool, "t_", l, 0)
                for q in range(4):
                    fill_pool(pool, "t_", T, l, 0, 0, q, MT)

                def t_group(i, b, nxt=True):
                    if nxt:
                        norm_pool(pool, "t_", l, i + 1)
                        for q in range(4):
                            fill_pool(pool, "t_", T, l, i + 1, 1 - b, q, MT)
                groups(pool, t_group, t_group, lambda i, b: t_group(i, b, False))
                stage_end(pool)

                stage_begin(pool, l, 2)
                stage_end(pool)

                stage_begin(pool, l, 3)
                for q in range(4):
                    fill_pool(pool, "n_", N, l, 0, 0, q, 8)
                dup = N["dup"]
                for t in range(PAST // P):
                    pool.wait_ge(S(f"n_ck{t}"), 16 * (l + 1))
                    pool.wait_ge(S("n_ftr"), upto(l * 80 + 2 * t))
                    for a in (0, 1):
                        ins_ = nc.gpsimd.tensor_copy(dup[:, :, a, :], CACHED[t][:].rearrange("p (j d) -> p j d", j=8))
                    ins_.then_inc(S("n_dup"), 1)

                def n_group(i, b, nxt=True):
                    for s in (0, 1):
                        tt = 2 * i + s
                        for n in range(4):
                            if nxt and 4 * s + n in N_FILL_AFTER:
                                fill_pool(pool, "n_", N, l, i + 1, 1 - b, N_FILL_AFTER[4 * s + n], 8)
                            if n < 2:
                                pool.wait_ge(S("n_rope"), upto(4 * (l * TILES + tt) + 2 * n + 2))
                                pool.wait_ge(S("n_ftr"), upto(l * 80 + 8 + 4 * tt + 2 * n))
                                if isinstance(i, int) and i == NG - 1:
                                    pool.wait_ge(S("n_newk"), upto(16 * (2 * l + s)))
                                for a in (0, 1):
                                    ins_ = nc.gpsimd.tensor_tensor(dup[:, :, a, :], N["m1"][:].rearrange("p (j d) -> p j d", j=8),
                                                                   N["m2"][:].rearrange("p (j d) -> p j d", j=8), ALU.add)
                                ins_.then_inc(S("n_dup"), 1)
                groups(pool, n_group, n_group, lambda i, b: n_group(i, b, False))
                stage_end(pool)

                stage_begin(pool, l, 4)
                U = l * 64

                def combine(u, b):
                    e = A[f"e{b}"]
                    st = A[f"s{b}"]
                    pool.wait_ge(S("a_c"), u + 1)
                    e1 = e[:, 0, 0:KEYS_A]
                    nc.gpsimd.tensor_tensor(e1, e1, st[:, 12:13].broadcast_to([P, KEYS_A]), ALU.mult).then_inc(S("a_e1"), 1)
                    e2 = e[:, 1, KEYS_A:KEYS]
                    nc.gpsimd.tensor_tensor(e2, e2, st[:, 18:19].broadcast_to([P, KEYS - KEYS_A]), ALU.mult).then_inc(S("a_e2"), 1)
                    pool.wait_ge(S("a_e2"), u + 1)
                    if not (isinstance(u, int) and u < 2):
                        pool.wait_ge(S("a_tr"), upto(5 * (u - 1)))
                    nc.gpsimd.tensor_tensor(A[f"d{b}"][:, KEYS_A:KEYS], e2, e[:, 0, KEYS_A:KEYS], ALU.subtract).then_inc(S("a_dB"), 1)

                for h in range(HEADS):
                    u0 = U + 16 * h
                    for b in (0, 1):
                        if h or b:
                            combine(u0 + b - 1, 1 - b)
                        for k in W_OUT_SLOTS[h][b]:
                            pool.wait_ge(S("o_wh"), l * KT + k + 1)
                            nc.gpsimd.tensor_tensor(O["wl"][:, k, :], O["wraw"][:, k, :], O["wh"][:, k, :].bitcast(F32),
                                                    ALU.subtract).then_inc(S("o_wl"), 1)

                    def pair(m):
                        for b in (0, 1):
                            combine(u0 + 2 * m + b - 1, 1 - b)
                    head_pairs(pool, h, pair)
                combine(U + 63, 1)
                stage_end(pool)

                stage_begin(pool, l, 5)

                def rstd_heads(t, b):
                    sm = O[f"sm{b}"]
                    pool.wait_ge(S("o_ms"), l * TILES + t + 1)
                    nc.gpsimd.tensor_tensor(sm[:, 8:12], sm[:, 4:8], neg_half[:], ALU.pow).then_inc(S("o_rs"), 1)

                def residual(t, b, half):
                    n = l * TILES + t
                    pool.wait_ge(S("o_mg"), 2 * n + 2)
                    pool.wait_ge(S(f"o_x{b}"), 16 * (l * TILES // 2 + half + 1))
                    if not (isinstance(t, int) and t < 2):
                        if l < DEPTH - 1:
                            pool.wait_ge(S(f"o_st{b}"), 16 * (l * TILES // 2 + half))
                        else:
                            pool.wait_ge(S("o_y"), t - 1)
                    nc.gpsimd.tensor_tensor(O[f"xn{b}"][:], O[f"t{b}"][:], O[f"x{b}"][:], ALU.add).then_inc(S("o_xn"), 1)

                def final_rstd(t, b):
                    sm = O[f"sm{b}"]
                    pool.wait_ge(S("o_fms"), t + 1)
                    nc.gpsimd.tensor_tensor(sm[:, 14:15], sm[:, 13:14], neg_half[:, 0:1], ALU.pow).then_inc(S("o_frs"), 1)

                rstd_heads(0, 0)
                rstd_heads(1, 1)

                def step(t, b, m):
                    if near(t, -1):
                        residual(t - 1, 1 - b, m - 1 + b)
                    if near(t, 2):
                        rstd_heads(t + 2, b)
                    if near(t, -1) and l == DEPTH - 1:
                        final_rstd(t - 1, 1 - b)
                out_steps(pool, step)
                stage_end(pool)


def _tables():
    f32 = np.float32
    t = {}
    c = np.arange(FW)
    ang = 2 * np.pi * ((c[:, None] * c[None, :]) % FW) / FW
    norm = 1.0 / math.sqrt(NS * FW)
    lay = lambda a: np.ascontiguousarray(a.reshape(-1, P, a.shape[1]).transpose(1, 0, 2))
    t["chan_cos"] = lay((np.cos(ang) * norm).astype(f32))
    t["chan_sin"] = lay((np.sin(ang) * norm).astype(f32))
    n = np.arange(NH)
    ang = 2 * np.pi * ((n[:, None] * n[None, :]) % NS) / NS
    for name, tab in (("seq_cos", np.cos(ang)), ("seq_sin", np.sin(ang))):
        tab = tab.astype(f32).reshape(8, P, 2, 512)
        t[name] = np.ascontiguousarray(tab.transpose(2, 1, 0, 3))
    sign = np.where(np.arange(512) % 2, -1.0, 1.0).astype(f32)
    t["sign_row"] = sign[None, :]
    t["sign_col"] = np.ascontiguousarray(sign[:P, None])
    n = np.arange(NP)
    ang = 2 * np.pi * ((n[:, None] * n[None, :]) % NP) / NP
    up = math.sqrt(NS / NP)
    t["prompt_cos"] = lay((np.cos(ang) * up).astype(f32))
    t["prompt_sin"] = lay((-np.sin(ang) * up).astype(f32))
    t["ident"] = np.eye(P, dtype=f32)
    half = HD // 2
    inv = (f32(1.0) / (f32(10000.0) ** (np.arange(0, half, 2, dtype=f32) / f32(half)))).astype(f32)
    tok = np.arange(NS)
    rope = np.zeros((NTOK, 2, HD), f32)
    rope[NS:, 0] = 1.0
    for a, pos in enumerate((tok // GRID_W, tok % GRID_W)):
        ang = (pos.astype(f32)[:, None] * inv[None, :]).astype(f32).astype(np.float64)
        w = half // 2
        for b in (0, 1):
            col = a * half + b * w
            rope[:NS, 0, col:col + w] = np.cos(ang)
            rope[:NS, 1, col:col + w] = np.sin(ang) * (-1.0 if b == 0 else 1.0)
    t["rope"] = rope
    return t


def kernel(x_prompt, x_sample, cache_k, cache_v, c, c_ctx, norm_g, w_mod, b_mod, w_in, conv_w, conv_b, lam_vec,
           subln_g, w_out, final_g):
    import concourse.bacc as _bacc
    from concourse.bass_utils import run_bass_kernel_spmd as _run

    a = lambda x: np.ascontiguousarray(np.asarray(x))
    arrays = {
        "x_all": a(np.concatenate([np.asarray(x_sample)[0], np.asarray(x_prompt)[0]])),
        "cond": a(np.stack([np.asarray(c)[0], np.asarray(c_ctx)]).reshape(2, KT, P).transpose(2, 1, 0)),
        "b_mod": a(np.asarray(b_mod).reshape(DEPTH, 24, P).transpose(2, 0, 1)),
        "norm_g": a(np.asarray(norm_g).reshape(DEPTH, KT, P).transpose(2, 0, 1)),
        "b_mod_row": a(b_mod),
        "w_mod": a(w_mod),
        "w_in_t": a(np.asarray(w_in)[:, :, :WT]),
        "w_in_n": a(np.asarray(w_in)[:, :, WT:]),
        "conv_wb": a(np.concatenate([np.asarray(conv_w), np.asarray(conv_b)[:, None]], 1).reshape(DEPTH, 4, 2, P).transpose(3, 0, 2, 1)),
        "lam_vec": a(lam_vec),
        "subln_g": a(subln_g),
        "w_out": a(w_out),
        "final_g": a(np.asarray(final_g)[None]),
        "cache_k": a(np.asarray(cache_k)[0].reshape(DEPTH, PAST, AW)),
        "cache_v": a(np.asarray(cache_v)[0].reshape(DEPTH, PAST, AW)),
        **_tables(),
    }
    nc = _bacc.Bacc("TRN2", target_bir_lowering=False, num_devices=1)
    ins = {n: nc.dram_tensor(n, v.shape, F32, kind="ExternalInput").ap() for n, v in arrays.items()}
    y_all = nc.dram_tensor("y_all", (NTOK, D), F32, kind="ExternalOutput").ap()
    new_k = nc.dram_tensor("new_k", (DEPTH, NP, AW), F32, kind="ExternalOutput").ap()
    new_v = nc.dram_tensor("new_v", (DEPTH, NP, AW), F32, kind="ExternalOutput").ap()
    backbone(nc, ins, y_all, new_k, new_v)
    r = _run(nc, [arrays], core_ids=[0]).results[0]
    y = r["y_all"]
    return (y[NS:].reshape(1, NP, D), y[:NS].reshape(1, NS, D), r["new_k"].reshape(1, DEPTH, NP, HEADS, QKW),
            r["new_v"].reshape(1, DEPTH, NP, HEADS, QKW))
```

```python
from contextlib import ExitStack
import math

import numpy as np

import concourse.bass as bass
from concourse import mybir

F32 = mybir.dt.float32
F32R = mybir.dt.float32r
BF16 = mybir.dt.bfloat16
ACT = mybir.ActivationFunctionType
ALU = mybir.AluOpType
AX_X = mybir.AxisListType.X

P = 128
D = 1024
KT = D // P
DEPTH = 2
NS = 2048
NP = 256
NTOK = NS + NP
TILES = NTOK // P
PAST = 512
G = 256
NG = NTOK // G
HEADS = 4
HD = 64
QKW = 2 * HD
AW = HEADS * QKW
FW = 256
CW = 256
WT = 2 * FW + 4 * CW
WN = 4 * AW
MT = WT // P
KEYS = PAST + NS
KEYS_A = 3 * 512
KTILES = KEYS // P
HEAD_TILES = NS // P
EPS = 1e-6
NH = NS // 2
SCALE = HD ** -0.5
GRID_W = 64

T_ORDER = [("fa", 0), ("fa", 1), ("ga", 0), ("ga", 1), ("cg", 0), ("hc", 0), ("gb", 0), ("bg", 0),
           ("cg", 1), ("hc", 1), ("gb", 1), ("bg", 1)]
T_COLUMN = {"fa": 0, "ga": FW, "bg": 2 * FW, "cg": 2 * FW + CW, "hc": 2 * FW + 2 * CW, "gb": 2 * FW + 3 * CW}
T_ACT = [m for m, (w, _) in enumerate(T_ORDER) if w not in ("hc", "bg")]
T_DVE = [m for m, (w, _) in enumerate(T_ORDER) if w in ("hc", "bg")]
T_BANKS = 6
T_FILL_AFTER = {3: 0, 5: 1, 7: 2, 9: 3}
N_FILL_AFTER = {0: 0, 1: 1, 4: 2, 5: 3}


def dups_after(i, s, n):
    if isinstance(i, int) and i == 0:
        return [(n % 2, 0 if n >= 2 else 1)] if s == 1 else []
    return [(n - 2, 0)] if n >= 2 else []

A_ORDER = [("q", 0), ("t", 0), ("t", 1), ("q", 1), ("v", 0), ("t", 2), ("v", 1), ("t", 3), ("q", 2), ("t", 4),
           ("q", 3), ("v", 2), ("v", 3), ("v", 4)]

W_OUT_SLOTS = [[(), ()], [(0,), (1,)], [(2,), (3,)], [(4, 5), (6, 7)]]


def backbone(nc, ins, y_all, new_k, new_v):
    es = ExitStack()
    with es:
        def scratch(name, shape):
            return nc.dram_tensor(name, shape, F32, kind="Internal").ap()

        x_scr = scratch("x_scr", (NTOK, D))
        fa_scr = scratch("fa_scr", (NG, P, 2, G))
        sga_scr = scratch("sga_scr", (NG, P, 2, G))
        yt_scr = scratch("yt_scr", (P, 4, NTOK))
        q_scr = scratch("q_scr", (TILES, P, 8, 2, P))
        k_scr = scratch("k_scr", (P, 8, KEYS + NP))
        v_scr = scratch("v_scr", (NTOK, AW))
        sgc_scr = scratch("sgc_scr", (NTOK, AW))
        gate_scr = scratch("gate_scr", (2, D))
        o_scr = scratch("o_scr", (NTOK, AW))

        def keep(name, shape, dt=F32):
            return es.enter_context(nc.sbuf_tensor(name, shape, dt))

        id_sb = keep("id_sb", [P, P])
        ones = keep("ones", [P, P])
        cond_in = keep("cond_in", [P, KT, 2])
        cond_act = keep("cond_act", [P, KT, 2])
        mod = keep("mod", [P, 16, 2])
        bmod_sb = keep("bmod_sb", [P, DEPTH, 24])
        ng_sb = keep("ng_sb", [P, DEPTH, KT])
        one_scale = keep("one_scale", [P, KT, 2])
        sqsum = keep("sqsum", [P, 2])
        meansq = keep("meansq", [P, 2])
        rstd = keep("rstd", [P, TILES])
        neg_half = keep("neg_half", [P, 4])
        conv_sb = keep("conv_sb", [P, DEPTH, 2, 4])
        lam_in = keep("lam_in", [P, 4, HD])
        lam_pr = keep("lam_pr", [P, 2, HD])
        lam_sum = keep("lam_sum", [P, 2])
        lam_exp = keep("lam_exp", [P, 2])
        lam = keep("lam", [P, 1])

        def region(prefix, shapes):
            with ExitStack() as st:
                return {n: st.enter_context(nc.sbuf_tensor(prefix + n, s, d)) for n, s, d in shapes}

        def weight_buffers(stack, prefix, width):
            wh = stack.enter_context(nc.sbuf_tensor(prefix + "wh", [P, KT, width], F32R))
            wraw = region(prefix, [("wraw", [P, KT, width], F32)])["wraw"]
            wl = stack.enter_context(nc.sbuf_tensor(prefix + "wl", [P, KT, width], F32R))
            return {"wh": wh, "wraw": wraw, "wl": wl}

        norm_bufs = [("xt0", [P, D], F32), ("xt1", [P, D], F32), ("hf", [P, 2, 4, P], F32),
                     ("hh0", [P, KT, G], F32R), ("hl0", [P, KT, G], F32R),
                     ("hh1", [P, KT, G], F32R), ("hl1", [P, KT, G], F32R)]
        with ExitStack() as conv_stack:
            z = conv_stack.enter_context(nc.sbuf_tensor("conv_z", [P, 2, NTOK], F32))
            bgs = conv_stack.enter_context(nc.sbuf_tensor("conv_bgs", [P, 2, NTOK], F32))
            with ExitStack() as weights_stack:
                T_W = weight_buffers(weights_stack, "t_", WT)
                M = region("m_", [("w0", [P, 3 * D], F32), ("w1", [P, 3 * D], F32), ("w2", [P, 3 * D], F32),
                                  ("row", [2, 3 * D], F32)])
                T = region("t_", norm_bufs + [
                    ("junk", [P, D], BF16), ("fa", [P, 2, G], F32), ("ga", [P, 2, G], F32), ("cg", [P, G], F32), ("gb", [P, G], F32)])
                T.update(T_W)
            F = region("f_", [
                ("fa", [P, 2, NTOK], F32),
                ("sga", [P, 2, NTOK], F32), ("fe", [P, 2, NH + 1], F32), ("fo", [P, 2, NH], F32), ("pq", [P, 8, 2 * FW], F32),
                ("plast", [1, FW], F32), ("pqp", [P, 2, 2 * FW], F32),
                ("cc", [P, 2, FW], F32), ("cs", [P, 2, FW], F32),
                ("ct0", [P, 8, 512], F32), ("st0", [P, 8, 512], F32), ("ct1", [P, 8, 512], F32), ("st1", [P, 8, 512], F32),
                ("sr", [1, 512], F32), ("scol", [P, 1], F32), ("pc", [P, 2, NP], F32), ("ps", [P, 2, NP], F32),
                ("sq0", [P, 512], F32), ("sq1", [P, 512], F32), ("cy", [P, NTOK], F32)])
        with ExitStack() as weights_stack:
            N_W = weight_buffers(weights_stack, "n_", WN)
            N = {n: weights_stack.enter_context(nc.sbuf_tensor("n_" + n, shape, d)) for n, shape, d in norm_bufs[:-2]}
            CACHED_T = region("n_", [(f"cached{n}", [P, 4, P], F32) for n in range(2 * PAST // P)])
            N.update(region("n_", norm_bufs[-2:] + [
                ("rope", [P, 2, HD], F32), ("m1", [P, AW], F32), ("m2", [P, AW], F32),
                ("vs", [P, AW], F32), ("gs", [P, AW], F32),
                ("dup", [P, 8, 2, HD], F32), ("qst0", [P, 4, 2, P], F32), ("qst1", [P, 4, 2, P], F32),
                ("kst0", [P, 4, P], F32), ("kst1", [P, 4, P], F32)]))
            N.update(N_W)
            CACHED = [N["m1"], N["m2"], N["vs"], N["gs"]]
        with ExitStack() as weights_stack:
            O_W = weight_buffers(weights_stack, "o_", D)
            attn_stack = ExitStack()
            a_bufs = [
                ("kt0", [P, 2, KEYS], F32R), ("kt1", [P, 2, KEYS], F32R), ("v0", [P, KTILES, P], F32), ("v1", [P, KTILES, P], F32),
                ("q0", [P, 2, 2, P], F32R), ("q1", [P, 2, 2, P], F32R),
                ("os0", [P, P], F32), ("os1", [P, P], F32), ("s0", [P, 24], F32), ("s1", [P, 24], F32)]
            A = {n: attn_stack.enter_context(nc.sbuf_tensor("a_" + n, shape, d)) for n, shape, d in a_bufs}
            A.update(region("a_", [
                ("e0", [P, 2, KEYS], F32), ("e1", [P, 2, KEYS], F32), ("d0", [P, KEYS], F32), ("d1", [P, KEYS], F32),
                ("dt", [P, 5, 4 * P], F32)]))
            B = region("b_", [
                ("kt", [P, 8, NP], F32R), ("v", [P, 2, AW], F32), ("q0", [P, 8, 2, P], F32R), ("q1", [P, 8, 2, P], F32R),
                ("e0", [P, 8, NP], F32), ("e1", [P, 8, NP], F32), ("d0", [P, 4, NP], F32), ("d1", [P, 4, NP], F32),
                ("dt0", [P, 8, P], F32), ("dt1", [P, 8, P], F32), ("os0", [P, AW], F32), ("os1", [P, AW], F32),
                ("mx0", [P, 8], F32), ("nb0", [P, 8], F32), ("ls0", [P, 8], F32), ("rl0", [P, 8], F32), ("c0", [P, 4], F32), ("nr0", [P, 4], F32),
                ("mx1", [P, 8], F32), ("nb1", [P, 8], F32), ("ls1", [P, 8], F32), ("rl1", [P, 8], F32), ("c1", [P, 4], F32), ("nr1", [P, 4], F32)])
            attn_stack.close()
            O = region("o_", [
                ("subln", [P, P], F32), ("fg", [P, D], F32), ("gate", [P, 2, D], F32), ("gate_bias", [P, D], F32), ("junk", [P, D], BF16), ("junk2", [P, D], BF16),
                ("o0", [P, AW], F32), ("o1", [P, AW], F32), ("g0", [P, AW], F32), ("g1", [P, AW], F32),
                ("x0", [P, D], F32), ("x1", [P, D], F32), ("yf0", [P, KT, P], F32), ("yf1", [P, KT, P], F32),
                ("yh0", [P, KT, P], F32R), ("yh1", [P, KT, P], F32R), ("yl0", [P, KT, P], F32R), ("yl1", [P, KT, P], F32R),
                ("on", [P, AW], F32), ("on2", [P, AW], F32), ("gated0", [P, AW], F32), ("gated1", [P, AW], F32),
                ("t0", [P, D], F32), ("t1", [P, D], F32), ("xn0", [P, D], F32), ("xn1", [P, D], F32),
                ("y0", [P, D], F32), ("y1", [P, D], F32),
                ("sm0", [P, 16], F32), ("sm1", [P, 16], F32)])
            O.update(O_W)

        psum = es.enter_context(nc.psum_tensor("psum", [P, 8, 512], F32))

        sems = {}

        def S(name):
            if name not in sems:
                sems[name] = es.enter_context(nc.semaphore(name))
            return sems[name]

        def upto(value):
            if isinstance(value, int):
                return max(value, 0)
            assert value.min_val > 0
            return value

        STAGES = 6

        def stage_begin(eng, l, n):
            eng.wait_ge(S("stage_left"), upto(5 * (STAGES * l + n)))

        def stage_end(eng):
            eng.drain().then_inc(S("stage_left"), 1)

        def groups(eng, first, pair, last):
            first(0, 0)
            with eng.Fori(0, 3) as m:
                pair(2 * m + 1, 1)
                pair(2 * m + 2, 0)
            pair(7, 1)
            last(8, 0)

        def near(t, d):
            return not isinstance(t, int) or 0 <= t + d < TILES

        def out_steps(eng, step):
            def pair(m):
                step(2 * m, 0, m)
                step(2 * m + 1, 1, m)
            pair(0)
            pair(1)
            with eng.Fori(2, 7) as m:
                pair(m)
            pair(7)
            pair(8)
            step(TILES, 0, TILES // 2)

        def head_pairs(eng, h, body, last=HEAD_TILES // 2):
            first = 3 if h == 0 else 1
            for m in range(1, first):
                body(m)
            with eng.Fori(first, last) as m:
                body(m)


        def x_load(sp, p, R, l, i):
            for s in (0, 1):
                if not (isinstance(i, int) and i == 0):
                    sp.wait_ge(S(p + "tr"), upto(l * 4 * NG + 4 * (i - 1) + 2 * s + 2))
                src = ins["x_all"] if l == 0 else x_scr
                r0 = i * G + s * P
                sp.dma_start(R[f"xt{s}"][:], src[bass.ds(r0, P), :]).then_inc(S(p + f"x{s}"), 16)

        def norm_act(act, p, R, l, i):
            for s in (0, 1):
                act.wait_ge(S(p + f"x{s}"), 16 * (l * NG + i + 1))
                if s == 0:
                    act.wait_ge(S(p + "ms"), upto(l * NG + i))
                act.wait_ge(S(p + "sq"), upto(2 * (l * NG + i) + s))
                nc.scalar.activation(R["junk"][:], R[f"xt{s}"][:], ACT.Square, accum_out=sqsum[:, s:s + 1]).then_inc(S(p + "sq"), 1)

        def norm_pool(pool, p, l, i):
            pool.wait_ge(S(p + "ms"), l * NG + i + 1)
            nc.gpsimd.tensor_tensor(rstd[:, bass.ds(2 * i, 2)], meansq[:], neg_half[:, 0:2], ALU.pow).then_inc(S(p + "rs"), 1)

        def norm_dve(dve, p, R, l, i, stats):
            if stats:
                dve.wait_ge(S(p + "sq"), 2 * (l * NG + i + 1))
                dve.wait_ge(S(p + "rs"), upto(l * NG + i))
                nc.vector.tensor_scalar(meansq[:], sqsum[:], 1.0 / D, EPS, ALU.mult, ALU.add).then_inc(S(p + "ms"), 1)
                dve.wait_ge(S(p + "rs"), l * NG + i + 1)
            for s in (0, 1):
                dve.wait_ge(S(p + f"x{s}"), 16 * (l * NG + i + 1))
                xt = R[f"xt{s}"]
                nc.vector.tensor_scalar(xt[:], xt[:], rstd[:, bass.ds(2 * i + s, 1)], None, ALU.mult).then_inc(S(p + "xn"), 1)

        def fill_pe(pe, p, R, l, i, q):
            s, kh = q // 2, q % 2
            n = l * 4 * NG + 4 * i + q
            pe.wait_ge(S(p + "xn"), l * 2 * NG + 2 * i + s + 1)
            if not (isinstance(i, int) and i == 0 and q < 2):
                pe.wait_ge(S(p + "ev"), upto(n - 1))
            for kk in range(4):
                k = 4 * kh + kk
                last = nc.tensor.transpose(psum[:, 6 + q % 2, kk * P:(kk + 1) * P], R[f"xt{s}"][:, k * P:(k + 1) * P], id_sb[:])
            last.then_inc(S(p + "tr"), 1)

        def fill_act(act, p, R, l, i, q):
            kh = q % 2
            g = 1 if isinstance(i, int) and i == NG - 1 else 0
            n = l * 4 * NG + 4 * i + q
            act.wait_ge(S(p + "tr"), n + 1)
            if not (isinstance(i, int) and i == 0 and q < 2):
                act.wait_ge(S(p + "lo"), upto(n - 1))
            for kk in range(4):
                k = 4 * kh + kk
                last = nc.scalar.activation(R["hf"][:, q % 2, kk, :], psum[:, 6 + q % 2, kk * P:(kk + 1) * P], ACT.Identity,
                                            bias=mod[:, k, g:g + 1], scale=one_scale[:, k, g:g + 1])
            last.then_inc(S(p + "ev"), 1)

        def fill_dve(dve, p, R, l, i, b, q, mm_per_group):
            s, kh = q // 2, q % 2
            n = l * 4 * NG + 4 * i + q
            dve.wait_ge(S(p + "ev"), n + 1)
            if not (isinstance(i, int) and i == 0):
                dve.wait_ge(S(p + "mm"), upto(mm_per_group * (l * NG + i - 1)))
            if p == "n_" and isinstance(i, int) and i == 1:
                dve.wait_ge(S("n_cst"), 16 * 2 * (PAST // P) * (l + 1))
            nc.vector.tensor_copy(R[f"hh{b}"][:, 4 * kh:4 * kh + 4, s * P:(s + 1) * P], R["hf"][:, q % 2]).then_inc(S(p + "hi"), 1)

        def fill_pool(pool, p, R, l, i, b, q, mm_per_group):
            s, kh = q // 2, q % 2
            pool.wait_ge(S(p + "hi"), l * 4 * NG + 4 * i + q + 1)
            hi = R[f"hh{b}"][:, 4 * kh:4 * kh + 4, s * P:(s + 1) * P]
            nc.gpsimd.tensor_tensor(R[f"hl{b}"][:, 4 * kh:4 * kh + 4, s * P:(s + 1) * P], R["hf"][:, q % 2], hi.bitcast(F32),
                                    ALU.subtract).then_inc(S(p + "lo"), 1)

        PIECES = 4

        def loaded(p, l):
            return 16 * (3 * l + ("t_", "n_", "o_").index(p) + 1)

        def piece(w, c):
            return w[:, 2 * c:2 * c + 2, :]

        def weights_sp(sp, p, l, src, raw):
            for c in range(PIECES):
                sp.dma_start(piece(raw, c), src[l, 2 * c * P:(2 * c + 2) * P, :].rearrange("(k p) w -> p k w", p=P)).then_inc(S(f"piece{c}"), 16)

        def weights_act(act, p, l, R, behind=None):
            for c in range(PIECES):
                act.wait_ge(S(f"piece{c}"), loaded(p, l))
                nc.scalar.activation(piece(R["wh"], c), piece(R["wraw"], c), ACT.Copy).then_inc(S(p + "wh"), 1)
                if behind:
                    behind(c)

        def weights_dve(dve, p, l, R, behind=None):
            for c in range(PIECES):
                dve.wait_ge(S(p + "wh"), l * PIECES + c + 1)
                nc.vector.tensor_tensor(piece(R["wl"], c), piece(R["wraw"], c), piece(R["wh"], c).bitcast(F32), ALU.subtract).then_inc(S(p + "wl"), 1)
                if behind:
                    behind(c)

        def split_products(out, terms, inc=None):
            n = len(terms)
            for j, ((wh, wl), (xh, xl)) in enumerate(terms):
                nc.tensor.matmul(out, wh, xh, start=(j == 0), stop=False)
                nc.tensor.matmul(out, wh, xl, start=False, stop=False)
                last = nc.tensor.matmul(out, wl, xh, start=False, stop=(j == n - 1))
            return last

        block = es.enter_context(nc.Block())

        @block.sync
        def _(sp):
            for dst, name in ((id_sb[:], "ident"), (cond_in[:], "cond"), (bmod_sb[:], "b_mod"), (ng_sb[:], "norm_g"), (conv_sb[:], "conv_wb")):
                sp.dma_start(dst, ins[name]).then_inc(S("consts"), 16)
            for l in range(DEPTH):
                stage_begin(sp, l, 0)
                sp.dma_start(lam_in[:], ins["lam_vec"][l:l + 1].partition_broadcast(P)).then_inc(S("lam_in"), 16)
                for k in range(KT):
                    if k >= 3:
                        sp.wait_ge(S("mod_mm"), l * KT + k - 2)
                    sp.dma_start(M[f"w{k % 3}"][:], ins["w_mod"][l, k * P:(k + 1) * P, :]).then_inc(S(f"mod_w{k % 3}"), 16)
                weights_sp(sp, "t_", l, ins["w_in_t"], T["wraw"])
                sp.wait_ge(S("lam_in"), 16 * (l + 1))
                sp.wait_ge(S("mod_row"), l + 1)
                sp.dma_start(gate_scr, M["row"][0:2, 2 * D:3 * D]).then_inc(S("mod_gate"), 16)
                sp.wait_ge(S("mod_gate"), 16 * (l + 1))
                stage_end(sp)

                stage_begin(sp, l, 1)
                x_load(sp, "t_", T, l, 0)

                def t_group(i, b, nxt=True):
                    if nxt:
                        x_load(sp, "t_", T, l, i + 1)
                    for j, (w, scr) in enumerate((("fa", fa_scr), ("ga", sga_scr))):
                        sp.wait_ge(S("t_act"), upto(len(T_ACT) * (l * NG + i) + 2 * j + 2))
                        sp.dma_start(scr[bass.ds(i, 1)].rearrange("g p j n -> (g p) j n"), T[w][:]).then_inc(S("t_st_" + w), 16)
                groups(sp, t_group, t_group, lambda i, b: t_group(i, b, False))
                sp.wait_ge(S("t_st_fa"), upto(16 * (l + 1) * NG))
                sp.wait_ge(S("t_st_ga"), upto(16 * (l + 1) * NG))
                stage_end(sp)

                stage_begin(sp, l, 2)
                def by_group(dst, scr):
                    return [(dst[:, j].rearrange("p (g n) -> p g n", g=NG), scr[:, :, j].rearrange("g p n -> p g n")) for j in (0, 1)]
                for dst, src in by_group(F["fa"], fa_scr) + [(F["cc"][:], ins["chan_cos"]), (F["cs"][:], ins["chan_sin"])]:
                    sp.dma_start(dst, src).then_inc(S("f_in"), 16)
                for name, src in (("sr", "sign_row"), ("scol", "sign_col"), ("pc", "prompt_cos"), ("ps", "prompt_sin")):
                    sp.dma_start(F[name][:], ins[src]).then_inc(S("f_tab"), 16)
                for kc in (0, 1):
                    for name, src in (("ct", "seq_cos"), ("st", "seq_sin")):
                        sp.dma_start(F[f"{name}{kc}"][:], ins[src][kc]).then_inc(S(f"f_tab{kc}"), 16)
                    if kc == 0:
                        for dst, src in by_group(F["sga"], sga_scr):
                            sp.dma_start(dst, src).then_inc(S("f_sga"), 16)
                for j in (0, 1):
                    sp.wait_ge(S("cv_y"), l * 2 + j + 1)
                    sp.dma_start(yt_scr[:, 2 + j, :], F["cy"][:]).then_inc(S("cv_st"), 16)
                for j in (0, 1):
                    sp.wait_ge(S("f_ya"), 5 * l + 2 * j + 3)
                    sp.dma_start(yt_scr[:, j, :], F["fa"][:, j, :]).then_inc(S("f_st"), 16)
                sp.wait_ge(S("f_st"), 32 * (l + 1))
                sp.wait_ge(S("cv_st"), 32 * (l + 1))
                stage_end(sp)

                stage_begin(sp, l, 3)
                x_load(sp, "n_", N, l, 0)
                for t in range(PAST // P):
                    sp.dma_start(CACHED[t][:], ins["cache_k"][l, t * P:(t + 1) * P, :]).then_inc(S(f"n_ck{t}"), 16)
                weights_sp(sp, "n_", l, ins["w_in_n"], N["wraw"])
                x_load(sp, "n_", N, l, 1)

                for t in range(PAST // P):
                    for f in (0, 1):
                        sp.wait_ge(S("n_flo"), l * 80 + 2 * t + f + 1)
                        sp.dma_start(k_scr[:, 4 * f:4 * f + 4, t * P:(t + 1) * P], CACHED_T[f"cached{2 * t + f}"][:]).then_inc(S("n_cst"), 16)

                def k_store(fill, col, f):
                    sp.wait_ge(S("n_flo"), fill + 1)
                    sp.dma_start(k_scr[:, 4 * f:4 * f + 4, bass.ds(col, P)], N[f"kst{f}"][:]).then_inc(S(f"n_kst{f}"), 16)

                def rope_load(tt):
                    sp.wait_ge(S("n_rope"), upto(l * TILES * 4 + 4 * tt))
                    sp.dma_start(N["rope"][:], ins["rope"][bass.ds(tt * P, P)]).then_inc(S("n_tab"), 16)

                def q_store(tt):
                    for f in (0, 1):
                        sp.wait_ge(S("n_flo"), l * 80 + 8 + 4 * tt + f + 1)
                        sp.dma_start(q_scr[bass.ds(tt, 1), :, 4 * f:4 * f + 4].rearrange("t p j c n -> p (t j) c n"), N[f"qst{f}"][:]).then_inc(S(f"n_qst{f}"), 16)

                def gate_store(tt):
                    sp.wait_ge(S("n_gs"), l * TILES + tt + 1)
                    sp.dma_start(sgc_scr[bass.ds(tt * P, P), :], N["gs"][:]).then_inc(S("n_gst"), 16)

                def k_stores(tt):
                    for f in (0, 1):
                        k_store(l * 80 + 8 + 4 * tt + 2 + f, tt * P + PAST, f)

                def n_group(i, b, nxt=True, new=False):
                    for s in (0, 1):
                        tt = 2 * i + s
                        n = l * TILES + tt
                        early = isinstance(i, int) and i == 0
                        if not early or s == 0:
                            rope_load(tt)
                        if early and s == 1:
                            gate_store(0)
                            rope_load(1)
                            q_store(0)
                            k_stores(0)
                        sp.wait_ge(S("n_vs"), n + 1)
                        sp.dma_start(v_scr[bass.ds(tt * P, P), :], N["vs"][:]).then_inc(S("n_vst"), 16)
                        if s == 1 and not (isinstance(i, int) and i + 2 >= NG):
                            x_load(sp, "n_", N, l, i + 2)
                        if new:
                            sp.dma_start(new_v[l, s * P:(s + 1) * P, :], N["vs"][:]).then_inc(S("n_newv"), 16)
                        if early and s == 0:
                            continue
                        q_store(tt)
                        gate_store(tt)
                        if new:
                            sp.wait_ge(S("n_dup"), upto(l * 40 + 4 + 2 * tt + 2))
                            sp.dma_start(new_k[l, s * P:(s + 1) * P, :].rearrange("p (j d) -> p j d", j=8), N["dup"][:, :, 0, :]).then_inc(S("n_newk"), 16)
                        k_stores(tt)
                groups(sp, n_group, n_group, lambda i, b: n_group(i, b, False, True))
                sp.wait_ge(S("n_vst"), 16 * TILES * (l + 1))
                sp.wait_ge(S("n_gst"), 16 * TILES * (l + 1))
                for f in (0, 1):
                    sp.wait_ge(S(f"n_qst{f}"), 16 * TILES * (l + 1))
                    sp.wait_ge(S(f"n_kst{f}"), 16 * TILES * (l + 1))
                sp.wait_ge(S("n_newv"), 32 * (l + 1))
                sp.wait_ge(S("n_newk"), 32 * (l + 1))
                stage_end(sp)

                stage_begin(sp, l, 4)
                U = l * 64

                def head_load(h):
                    hb = h % 2
                    if h >= 2:
                        sp.wait_ge(S("a_o"), upto(U + 16 * (h - 1)))
                    sp.dma_start(A[f"kt{hb}"][:].bitcast(F32), k_scr[:, 2 * h:2 * h + 2, 0:KEYS]).then_inc(S(f"a_k{hb}"), 16)
                    sp.dma_start(A[f"v{hb}"][:, 0:PAST // P, :], ins["cache_v"][l, :, h * P:(h + 1) * P].rearrange("(t p) d -> p t d", p=P)).then_inc(S(f"a_v{hb}"), 16)
                    sp.dma_start(A[f"v{hb}"][:, PAST // P:, :], v_scr[0:NS, h * P:(h + 1) * P].rearrange("(t p) d -> p t d", p=P)).then_inc(S(f"a_v{hb}"), 16)

                def q_load(h, t, b):
                    if not (isinstance(t, int) and h == 0 and t < 2):
                        sp.wait_ge(S("a_qk"), upto(4 * (U + 16 * h + t - 1)))
                    sp.dma_start(A[f"q{b}"][:].bitcast(F32), q_scr[bass.ds(t, 1), :, 2 * h:2 * h + 2].rearrange("t p j c n -> p (t j) c n")).then_inc(S(f"a_q{b}"), 16)

                def o_store(h, t, b):
                    sp.wait_ge(S("a_os"), U + 16 * h + t + 1)
                    sp.dma_start(o_scr[bass.ds(t * P, P), h * P:(h + 1) * P], A[f"os{b}"][:]).then_inc(S(f"a_st{b}"), 16)

                sp.dma_start(B["kt"][:].bitcast(F32), k_scr[:, :, KEYS:KEYS + NP]).then_inc(S("b_k"), 16)
                for t in (0, 1):
                    sp.dma_start(B[f"q{t}"][:].bitcast(F32), q_scr[NS // P + t]).then_inc(S(f"b_q{t}"), 16)
                sp.dma_start(B["v"][:], v_scr[NS:NTOK, :].rearrange("(t p) d -> p t d", p=P)).then_inc(S("b_v"), 16)
                head_load(0)
                q_load(0, 0, 0)
                for t in (0, 1):
                    sp.wait_ge(S("b_os"), 2 * l + t + 1)
                    sp.dma_start(o_scr[NS + t * P:NS + (t + 1) * P, :], B[f"os{t}"][:]).then_inc(S("b_st"), 16)
                for h in range(HEADS):
                    for b in (0, 1):
                        q_load(h, 1 + b, 1 - b)
                        if h:
                            o_store(h - 1, 14 + b, b)
                    if h == 0:
                        weights_sp(sp, "o_", l, ins["w_out"], O["wraw"])
                    if h < HEADS - 1:
                        head_load(h + 1)

                    def pair(m):
                        q_load(h, 2 * m + 1, 1)
                        o_store(h, 2 * m - 2, 0)
                        q_load(h, 2 * m + 2, 0)
                        o_store(h, 2 * m - 1, 1)
                    head_pairs(sp, h, pair, HEAD_TILES // 2 - 1)
                    q_load(h, 15, 1)
                    o_store(h, 12, 0)
                    if h < HEADS - 1:
                        q_load(h + 1, 0, 0)
                    o_store(h, 13, 1)
                o_store(HEADS - 1, 14, 0)
                o_store(HEADS - 1, 15, 1)
                for b in (0, 1):
                    sp.wait_ge(S(f"a_st{b}"), 16 * 32 * (l + 1))
                sp.wait_ge(S("b_st"), 32 * (l + 1))
                stage_end(sp)

                stage_begin(sp, l, 5)
                sp.dma_start(O["subln"][:], ins["subln_g"][l:l + 1].partition_broadcast(P)).then_inc(S("o_c"), 16)
                sp.dma_start(O["fg"][:], ins["final_g"].partition_broadcast(P)).then_inc(S("o_c"), 16)
                sp.dma_start(O["gate_bias"][:], ins["b_mod_row"][l:l + 1, 2 * D:].partition_broadcast(P)).then_inc(S("o_g"), 16)
                for g in (0, 1):
                    sp.dma_start(O["gate"][:, g, :], gate_scr[g:g + 1].partition_broadcast(P)).then_inc(S("o_g"), 16)

                def load_attention(t, b):
                    r = bass.ds(t * P, P)
                    if not (isinstance(t, int) and t < 2):
                        sp.wait_ge(S("o_gated"), l * TILES + t - 1)
                    for dst, src in ((O[f"o{b}"][:], o_scr[r, :]), (O[f"g{b}"][:], sgc_scr[r, :])):
                        sp.dma_start(dst, src).then_inc(S(f"o_og{b}"), 16)

                def load_mixed(t, b):
                    r = bass.ds(t * P, P)
                    sp.dma_start(O[f"yf{b}"][:, 0:4, :], yt_scr[:, :, r]).then_inc(S(f"o_yt{b}"), 16)

                def load_x(t, b):
                    r = bass.ds(t * P, P)
                    if not (isinstance(t, int) and t < 2):
                        sp.wait_ge(S("o_xn"), l * TILES + t - 1)
                    sp.dma_start(O[f"x{b}"][:], (ins["x_all"] if l == 0 else x_scr)[r, :]).then_inc(S(f"o_x{b}"), 16)

                def store(t, b):
                    r = bass.ds(t * P, P)
                    if l == DEPTH - 1:
                        sp.wait_ge(S("o_y"), t + 1)
                        sp.dma_start(y_all[r, :], O[f"y{b}"][:]).then_inc(S(f"o_st{b}"), 16)
                    else:
                        sp.wait_ge(S("o_xn"), l * TILES + t + 1)
                        sp.dma_start(x_scr[r, :], O[f"xn{b}"][:]).then_inc(S(f"o_st{b}"), 16)

                for t in (0, 1):
                    load_attention(t, t)
                    load_mixed(t, t)
                load_x(0, 0)
                load_attention(2, 0)

                def step(t, b, m):
                    if isinstance(t, int) and near(t, 2):
                        sp.wait_ge(S("o_lo"), l * TILES + t + 1)
                    if near(t, 3):
                        load_attention(t + 3, 1 - b)
                    if near(t, 2):
                        load_mixed(t + 2, b)
                    if near(t, 1):
                        load_x(t + 1, 1 - b)
                    if near(t, -1):
                        store(t - 1, 1 - b)
                out_steps(sp, step)
                for b in (0, 1):
                    sp.wait_ge(S(f"o_st{b}"), upto(16 * (l + 1) * TILES // 2))
                stage_end(sp)

        @block.tensor
        def _(pe):
            pe.wait_ge(S("consts"), 16 * 5)
            pe.wait_ge(S("ones_set"), 3)
            for l in range(DEPTH):
                stage_begin(pe, l, 0)
                pe.wait_ge(S("cond_act"), 1)
                for k in range(KT):
                    pe.wait_ge(S(f"mod_w{k % 3}"), 16 * (l * ((KT - k % 3 + 2) // 3) + k // 3 + 1))
                    for m in range(6):
                        last = nc.tensor.matmul(psum[0:2, m, :], cond_act[:, k, :], M[f"w{k % 3}"][:, m * 512:(m + 1) * 512],
                                                start=(k == 0), stop=(k == KT - 1))
                    last.then_inc(S("mod_mm"), 1)
                pe.wait_ge(S("mod_row"), l + 1)
                for m in range(16):
                    last = nc.tensor.transpose(psum[:, 6, 2 * m:2 * m + 2], M["row"][0:2, m * P:(m + 1) * P], id_sb[0:2, 0:2])
                last.then_inc(S("mod_col"), 1)
                stage_end(pe)

                stage_begin(pe, l, 1)
                for q in range(4):
                    fill_pe(pe, "t_", T, l, 0, q)
                pe.wait_ge(S("t_wl"), (l + 1) * PIECES)

                def t_group(i, b, nxt=True):
                    pe.wait_ge(S("t_lo"), 4 * (l * NG + i + 1))
                    for m, (w, j) in enumerate(T_ORDER):
                        c = T_COLUMN[w] + j * P
                        first = isinstance(i, int) and i == 0
                        if m >= T_BANKS or not first:
                            o = (m - T_BANKS) % MT
                            back = l * NG + i - (m < T_BANKS)
                            if o in T_ACT:
                                pe.wait_ge(S("t_act"), len(T_ACT) * back + T_ACT.index(o) + 1)
                            else:
                                pe.wait_ge(S("t_dve"), len(T_DVE) * back + T_DVE.index(o) + 1)
                        split_products(psum[:, m % T_BANKS, 0:G],
                                       [((T["wh"][:, k, c:c + P], T["wl"][:, k, c:c + P]), (T[f"hh{b}"][:, k, :], T[f"hl{b}"][:, k, :]))
                                        for k in range(KT)]).then_inc(S("t_mm"), 1)
                        if nxt and m in T_FILL_AFTER:
                            fill_pe(pe, "t_", T, l, i + 1, T_FILL_AFTER[m])
                groups(pe, t_group, t_group, lambda i, b: t_group(i, b, False))
                stage_end(pe)

                stage_begin(pe, l, 2)
                pe.wait_ge(S("f_in"), 64 * (l + 1))
                pe.wait_ge(S("f_fold"), l + 1)
                for t in range(8):
                    pe.wait_ge(S("f_pq"), upto(l * 11 + t - 1 if t >= 2 else 0))
                    for part, (seq, tab) in enumerate(((F["fe"], F["cc"]), (F["fo"], F["cs"]))):
                        for j in (0, 1):
                            last = nc.tensor.matmul(psum[:, t % 2, part * FW:(part + 1) * FW], seq[:, j, t * P:(t + 1) * P], tab[:, j, :], start=(j == 0), stop=(j == 1))
                    last.then_inc(S("f_ch"), 1)
                for j in (0, 1):
                    last = nc.tensor.matmul(psum[0:1, 2, 0:FW], F["fe"][:, j, NH:NH + 1], F["cc"][:, j, :], start=(j == 0), stop=(j == 1))
                last.then_inc(S("f_ch"), 1)
                for t in (0, 1):
                    for part, tab in enumerate((F["cc"], F["cs"])):
                        for j in (0, 1):
                            last = nc.tensor.matmul(psum[:, 3 + t, part * FW:(part + 1) * FW], F["fa"][:, j, NS + t * P:NS + (t + 1) * P], tab[:, j, :], start=(j == 0), stop=(j == 1))
                    last.then_inc(S("f_ch"), 1)
                pe.wait_ge(S("f_tab"), 64 * (l + 1))
                pe.wait_ge(S("f_pq"), 11 * (l + 1))
                for ct in (0, 1):
                    c = ct * P
                    for t in range(8):
                        nc.tensor.matmul(psum[:, 0, ct:ct + 1], F["pq"][:, t, c:c + P], F["scol"][:, 0:1], start=(t == 0), stop=False)
                    last = nc.tensor.matmul(psum[:, 0, ct:ct + 1], F["plast"][0:1, c:c + P], ones[0:1, 0:1], start=False, stop=True)
                last.then_inc(S("f_nyq"), 1)
                for ct in (0, 1):
                    c = ct * P
                    for t in (0, 1):
                        nc.tensor.matmul(psum[:, 1, ct * NP:(ct + 1) * NP], F["pqp"][:, t, c:c + P], F["pc"][:, t, :], start=(t == 0), stop=False)
                        last = nc.tensor.matmul(psum[:, 1, ct * NP:(ct + 1) * NP], F["pqp"][:, t, FW + c:FW + c + P], F["ps"][:, t, :], start=False, stop=(t == 1))
                last.then_inc(S("f_nyq"), 1)
                for n in range(4):
                    ct, kc = n // 2, n % 2
                    c = ct * P
                    pe.wait_ge(S(f"f_tab{kc}"), 32 * (l + 1))
                    if n >= 2:
                        pe.wait_ge(S("f_out"), 4 * l + n - 1)
                    cb, sb_ = ((5, 6), (7, 2))[n % 2]
                    for t in range(8):
                        nc.tensor.matmul(psum[:, cb, :], F["pq"][:, t, c:c + P], F[f"ct{kc}"][:, t, :], start=(t == 0), stop=False)
                    nc.tensor.matmul(psum[:, cb, :], F["plast"][0:1, c:c + P], F["sr"][0:1, :], start=False, stop=True)
                    for t in range(8):
                        last = nc.tensor.matmul(psum[:, sb_, :], F["pq"][:, t, FW + c:FW + c + P], F[f"st{kc}"][:, t, :], start=(t == 0), stop=(t == 7))
                    last.then_inc(S("f_sd"), 1)
                stage_end(pe)

                stage_begin(pe, l, 3)
                for q in range(4):
                    fill_pe(pe, "n_", N, l, 0, q)

                def dup_fill(n, dups, f):
                    pe.wait_ge(S("n_dup"), upto(dups))
                    if not (isinstance(n, int) and n < 2):
                        pe.wait_ge(S("n_fhi"), upto(n - 1))
                        pe.wait_ge(S("n_flo"), upto(n - 1))
                    for j in range(4):
                        last = nc.tensor.transpose(psum[:, 4 + f, j * P:(j + 1) * P], N["dup"][:, 4 * f + j].rearrange("p a d -> p (a d)"), id_sb[:])
                    last.then_inc(S("n_ftr"), 1)

                def first_tile():
                    for c in range(PIECES):
                        for f in (0, 1):
                            dup_fill(l * 80 + 2 * c + f, l * 40 + c + 1, f)
                        pe.wait_ge(S("n_wl"), l * PIECES + c + 1)
                        for n in range(4):
                            for k in (2 * c, 2 * c + 1):
                                hh, hl = N["hh0"][:, k, 0:P], N["hl0"][:, k, 0:P]
                                wh, wl = N["wh"][:, k, n * AW:(n + 1) * AW], N["wl"][:, k, n * AW:(n + 1) * AW]
                                nc.tensor.matmul(psum[:, n, :], hh, wh, start=(k == 0), stop=False)
                                nc.tensor.matmul(psum[:, n, :], hh, wl, start=False, stop=False)
                                last = nc.tensor.matmul(psum[:, n, :], hl, wh, start=False, stop=(k == KT - 1))
                            if c == PIECES - 1:
                                last.then_inc(S("n_mm"), 1)

                def n_group(i, b, nxt=True):
                    pe.wait_ge(S("n_lo"), 4 * (l * NG + i + 1))
                    first = isinstance(i, int) and i == 0
                    for s in (0, 1):
                        tt = 2 * i + s
                        for n in range(4):
                            if first and s == 0:
                                if n == 0:
                                    first_tile()
                            else:
                                if n < 2:
                                    pe.wait_ge(S("n_rope"), upto(4 * (l * TILES + tt - 1) + 2 * n + 2))
                                else:
                                    pe.wait_ge(S("n_vs" if n == 2 else "n_gs"), upto(l * TILES + tt))
                                split_products(psum[:, n, :],
                                               [((N[f"hh{b}"][:, k, s * P:(s + 1) * P], N[f"hl{b}"][:, k, s * P:(s + 1) * P]),
                                                 (N["wh"][:, k, n * AW:(n + 1) * AW], N["wl"][:, k, n * AW:(n + 1) * AW])) for k in range(KT)]).then_inc(S("n_mm"), 1)
                            for qk, back in dups_after(i, s, n):
                                for f in (0, 1):
                                    dup_fill(l * 80 + 8 + 4 * (tt - back) + 2 * qk + f, l * 40 + 4 + 2 * (tt - back) + qk + 1, f)
                            if nxt and 4 * s + n in N_FILL_AFTER:
                                fill_pe(pe, "n_", N, l, i + 1, N_FILL_AFTER[4 * s + n])
                groups(pe, n_group, n_group, lambda i, b: n_group(i, b, False))
                stage_end(pe)

                stage_begin(pe, l, 4)
                U = l * 64

                pe.wait_ge(S("b_k"), 16 * (l + 1))
                for t in (0, 1):
                    pe.wait_ge(S(f"b_q{t}"), 16 * (l + 1))
                    for j in range(8):
                        out = psum[:, 4 * t + j // 2, (j % 2) * NP:(j % 2 + 1) * NP]
                        nc.tensor.matmul(out, B[f"q{t}"][:, j, 0, :], B["kt"][:, j, :], start=True, stop=False)
                        last = nc.tensor.matmul(out, B[f"q{t}"][:, j, 1, :], B["kt"][:, j, :], start=False, stop=True)
                    last.then_inc(S("b_qk"), 1)
                pe.wait_ge(S("b_v"), 16 * (l + 1))
                for t in (0, 1):
                    n = 2 * l + t
                    pe.wait_ge(S("b_d"), n + 1)
                    for h in range(HEADS):
                        for k in (0, 1):
                            j = 2 * h + k
                            last = nc.tensor.transpose(psum[:, 4 * t + j // 4, (j % 4) * P:(j % 4 + 1) * P], B[f"d{t}"][:, h, k * P:(k + 1) * P], id_sb[:])
                    last.then_inc(S("b_tr"), 1)
                    pe.wait_ge(S("b_dt"), n + 1)
                    for h in range(HEADS):
                        for k in (0, 1):
                            last = nc.tensor.matmul(psum[:, 4 * t + 2, h * P:(h + 1) * P], B[f"dt{t}"][:, 2 * h + k, :], B["v"][:, k, h * P:(h + 1) * P], start=(k == 0), stop=(k == 1))
                    last.then_inc(S("b_o"), 1)
                pe.wait_ge(S("b_os"), 2 * (l + 1))

                def scores(h, t, b, part):
                    half, kp = part // 2, part % 2
                    u = U + 16 * h + t
                    if part == 0:
                        pe.wait_ge(S(f"a_q{b}"), 16 * (l * 32 + (8 * h + (t - b) // 2 if isinstance(t, int) else 8 * h + t_pair[0]) + 1))
                        if isinstance(t, int) and t == 0:
                            pe.wait_ge(S(f"a_k{h % 2}"), 16 * (2 * l + h // 2 + 1))
                    if not (isinstance(t, int) and 16 * h + t == 0 and part < 2):
                        pe.wait_ge(S("a_exp"), upto(4 * u + part - 1))
                    q = A[f"q{b}"]
                    kt = A[f"kt{h % 2}"]
                    for bank in ((0, 1, 2), (3, 4))[kp]:
                        keys = kt[:, half, bank * 512:(bank + 1) * 512]
                        nc.tensor.matmul(psum[:, bank, :], q[:, half, 0, :], keys, start=True, stop=False)
                        last = nc.tensor.matmul(psum[:, bank, :], q[:, half, 1, :], keys, start=False, stop=True)
                    last.then_inc(S("a_qk"), 1)

                def turn(u, b, f):
                    if f == 0:
                        pe.wait_ge(S("a_dA"), u + 1)
                    if f == 3:
                        pe.wait_ge(S("a_dB"), u + 1)
                    if f >= 2:
                        if f % 2 == 0:
                            pe.wait_ge(S("a_tevS"), 3 * u + f // 2)
                        else:
                            pe.wait_ge(S("a_tevV"), 2 * u + 1)
                    elif not (isinstance(u, int) and u == 0):
                        if f == 0:
                            pe.wait_ge(S("a_tevV"), 2 * u)
                        else:
                            pe.wait_ge(S("a_tevS"), 3 * u)
                    for j in range(4):
                        kt_ = 4 * f + j
                        last = nc.tensor.transpose(psum[:, 5 + (b + f) % 2, j * P:(j + 1) * P], A[f"d{b}"][:, kt_ * P:(kt_ + 1) * P], id_sb[:])
                    last.then_inc(S("a_tr"), 1)

                def values(h, u, f):
                    if f == 0:
                        if not (isinstance(u, int) and u == 0):
                            pe.wait_ge(S("a_os"), upto(u))
                        pe.wait_ge(S(f"a_v{h % 2}"), 32 * (2 * l + h // 2 + 1))
                    if f % 2 == 0:
                        pe.wait_ge(S("a_tevS"), 3 * u + f // 2 + 1)
                    else:
                        pe.wait_ge(S("a_tevV"), 2 * u + f // 2 + 1)
                    for j in range(4):
                        last = nc.tensor.matmul(psum[:, 7, 0:P], A["dt"][:, f, j * P:(j + 1) * P], A[f"v{h % 2}"][:, 4 * f + j, :],
                                                start=(f == 0 and j == 0), stop=(f == 4 and j == 3))
                    if f == 4:
                        last.then_inc(S("a_o"), 1)

                t_pair = [0]

                def unit(h, t, b, prev):
                    for what, n in A_ORDER:
                        if what == "q":
                            scores(h, t, b, n)
                        elif prev is None:
                            continue
                        elif what == "t":
                            turn(prev[1], b, n)
                        else:
                            values(prev[0], prev[1], n)

                for h in range(HEADS):
                    for b in (0, 1):
                        t_pair[0] = 0
                        unit(h, b, b, (h - 1, U + 16 * h - 2 + b) if h else None)

                    def pair(m):
                        t_pair[0] = m
                        for b in (0, 1):
                            unit(h, 2 * m + b, b, (h, U + 16 * h + 2 * m - 2 + b))
                    head_pairs(pe, h, pair)
                for b in (0, 1):
                    for f in range(5):
                        turn(U + 62 + b, b, f)
                        if f:
                            values(HEADS - 1, U + 62 + b, f - 1)
                    values(HEADS - 1, U + 62 + b, 4)
                stage_end(pe)

                stage_begin(pe, l, 5)
                pe.wait_ge(S("o_wl"), (l + 1) * KT)

                def turn(t, b):
                    n = l * TILES + t
                    pe.wait_ge(S("o_gated"), n + 1)
                    if not (isinstance(t, int) and t < 2):
                        pe.wait_ge(S("o_yf"), n - 1)
                    for j in range(4):
                        last = nc.tensor.transpose(psum[:, 6 + b, j * P:(j + 1) * P], O[f"gated{b}"][:, j * P:(j + 1) * P], id_sb[:])
                    last.then_inc(S("o_tr"), 1)

                def products(t, b):
                    n = l * TILES + t
                    pe.wait_ge(S("o_lo"), n + 1)
                    for c in (0, 1):
                        if not (isinstance(t, int) and t < 2):
                            pe.wait_ge(S("o_mg"), 2 * (n - 2) + c + 1)
                        split_products(psum[:, 2 * b + c, :],
                                       [((O[f"yh{b}"][:, k, :], O[f"yl{b}"][:, k, :]), (O["wh"][:, k, c * 512:(c + 1) * 512], O["wl"][:, k, c * 512:(c + 1) * 512]))
                                        for k in range(KT)]).then_inc(S("o_mm"), 1)

                turn(0, 0)

                def step(t, b, m):
                    if near(t, 1):
                        turn(t + 1, 1 - b)
                    if near(t, 0):
                        products(t, b)
                out_steps(pe, step)
                stage_end(pe)

        @block.scalar
        def _(act):
            act.wait_ge(S("consts"), 16 * 5)
            nc.scalar.activation(cond_act[:], cond_in[:], ACT.Silu).then_inc(S("cond_act"), 1)
            for l in range(DEPTH):
                stage_begin(act, l, 0)
                act.wait_ge(S("lam_sum"), l + 1)
                nc.scalar.activation(lam_exp[:], lam_sum[:], ACT.Exp).then_inc(S("lam_exp"), 1)
                act.wait_ge(S("mod_mm"), KT * (l + 1))
                nc.scalar.activation(M["row"][0:2, :].rearrange("p (a b) -> p a b", a=6), psum[0:2, 0:6, :], ACT.Copy).then_inc(S("mod_row"), 1)
                weights_act(act, "t_", l, T)
                stage_end(act)

                stage_begin(act, l, 1)
                norm_act(act, "t_", T, l, 0)
                for q in range(4):
                    fill_act(act, "t_", T, l, 0, q)

                def t_group(i, b, nxt=True):
                    if nxt:
                        norm_act(act, "t_", T, l, i + 1)
                    gi = l * NG + i
                    for m, (w, j) in enumerate(T_ORDER):
                        if m in T_ACT:
                            act.wait_ge(S("t_mm"), MT * gi + m + 1)
                            src = psum[:, m % T_BANKS, 0:G]
                            if w in ("fa", "ga"):
                                if j == 0:
                                    act.wait_ge(S("t_st_" + w), upto(16 * gi))
                                ins_ = nc.scalar.activation(T[w][:, j, :], src, ACT.Copy if w == "fa" else ACT.Silu)
                            elif w == "cg":
                                act.wait_ge(S("t_dve"), upto(4 * gi + (1 if j else 0)))
                                ins_ = nc.scalar.activation(T["cg"][:], src, ACT.Copy)
                            else:
                                act.wait_ge(S("t_dve"), upto(4 * gi + (2 if j else 0)))
                                ins_ = nc.scalar.activation(T["gb"][:], src, ACT.Silu)
                            ins_.then_inc(S("t_act"), 1)
                        if nxt and m in T_FILL_AFTER:
                            fill_act(act, "t_", T, l, i + 1, T_FILL_AFTER[m])
                groups(act, t_group, t_group, lambda i, b: t_group(i, b, False))
                stage_end(act)

                stage_begin(act, l, 2)
                for t in range(8):
                    act.wait_ge(S("f_ch"), l * 11 + t + 1)
                    nc.scalar.activation(F["pq"][:, t, :], psum[:, t % 2, :], ACT.Copy).then_inc(S("f_pq"), 1)
                act.wait_ge(S("f_ch"), upto(l * 11 + 9))
                nc.scalar.activation(F["plast"][0:1, :], psum[0:1, 2, 0:FW], ACT.Copy).then_inc(S("f_pq"), 1)
                for t in (0, 1):
                    act.wait_ge(S("f_ch"), upto(l * 11 + 10 + t))
                    nc.scalar.activation(F["pqp"][:, t, :], psum[:, 3 + t, :], ACT.Copy).then_inc(S("f_pq"), 1)
                def conv_middle(j):
                    act.wait_ge(S("cv_st"), upto(16 * (2 * l + j)))
                    nc.scalar.activation(F["cy"][:], z[:, j, :], ACT.Identity, bias=conv_sb[:, l, j, 3:4], scale=conv_sb[:, l, j, 1:2]).then_inc(S("cv_mid"), 1)

                conv_middle(0)
                for n in range(4):
                    act.wait_ge(S("f_sd"), l * 4 + n + 1)
                    if n >= 2:
                        act.wait_ge(S("f_out"), 4 * l + n - 1)
                    nc.scalar.activation(F[f"sq{n % 2}"][:], psum[:, (6, 2)[n % 2], :], ACT.Copy).then_inc(S("f_sq"), 1)
                    if n == 0:
                        conv_middle(1)
                stage_end(act)

                stage_begin(act, l, 3)
                for q in range(4):
                    fill_act(act, "n_", N, l, 0, q)

                def dup_hi(n, kind, stores, f):
                    act.wait_ge(S("n_ftr"), n + 1)
                    act.wait_ge(S(f"n_{kind}{f}"), upto(16 * stores))
                    src = psum[:, 4 + f, :].rearrange("p (j n) -> p j n", j=4)
                    dst = N[f"qst{f}"][:, :, 0, :] if kind == "qst" else N[f"kst{f}"][:]
                    nc.scalar.activation(dst.bitcast(F32R), src, ACT.Copy).then_inc(S("n_fhi"), 1)

                def cached_hi(t):
                    for f in (0, 1):
                        act.wait_ge(S("n_ftr"), l * 80 + 2 * t + f + 1)
                        nc.scalar.activation(CACHED_T[f"cached{2 * t + f}"][:].bitcast(F32R), psum[:, 4 + f, :].rearrange("p (j n) -> p j n", j=4),
                                             ACT.Copy).then_inc(S("n_fhi"), 1)
                assert PIECES == PAST // P
                weights_act(act, "n_", l, N, cached_hi)

                def n_group(i, b, nxt=True):
                    for s in (0, 1):
                        tt = 2 * i + s
                        nt = l * TILES + tt
                        for n in range(4):
                            if n == 2:
                                act.wait_ge(S("n_mm"), upto(4 * nt + 3))
                                act.wait_ge(S("n_vst"), upto(16 * nt))
                                if isinstance(i, int) and i == NG - 1:
                                    act.wait_ge(S("n_newv"), upto(16 * (2 * l + s)))
                                nc.scalar.activation(N["vs"][:], psum[:, 2, :], ACT.Copy).then_inc(S("n_vs"), 1)
                            if n == 3:
                                act.wait_ge(S("n_mm"), upto(4 * nt + 4))
                                act.wait_ge(S("n_gst"), upto(16 * nt))
                                nc.scalar.activation(N["gs"][:], psum[:, 3, :], ACT.Silu).then_inc(S("n_gs"), 1)
                            for qk, back in dups_after(i, s, n):
                                for f in (0, 1):
                                    dup_hi(l * 80 + 8 + 4 * (tt - back) + 2 * qk + f, ("qst", "kst")[qk], nt - back, f)
                            if nxt and 4 * s + n in N_FILL_AFTER:
                                fill_act(act, "n_", N, l, i + 1, N_FILL_AFTER[4 * s + n])
                groups(act, n_group, n_group, lambda i, b: n_group(i, b, False))
                stage_end(act)

                stage_begin(act, l, 4)
                U = l * 64

                for t in (0, 1):
                    act.wait_ge(S("b_nb"), 2 * l + t + 1)
                    for j in range(8):
                        last = nc.scalar.activation(B[f"e{t}"][:, j, :], psum[:, 4 * t + j // 2, (j % 2) * NP:(j % 2 + 1) * NP], ACT.Exp,
                                                    bias=B[f"nb{t}"][:, j:j + 1], scale=SCALE, accum_out=B[f"ls{t}"][:, j:j + 1])
                    last.then_inc(S("b_exp"), 1)
                for t in (0, 1):
                    act.wait_ge(S("b_tr"), 2 * l + t + 1)
                    nc.scalar.activation(B[f"dt{t}"][:].rearrange("p (a b) n -> p a (b n)", a=2), psum[:, 4 * t:4 * t + 2, :], ACT.Copy).then_inc(S("b_dt"), 1)
                act.wait_ge(S("b_os"), 2 * (l + 1))

                def exps(u, b, part):
                    half, kp = part // 2, part % 2
                    st = A[f"s{b}"]
                    act.wait_ge(S("a_nb"), 4 * u + part + 1)
                    if part == 0 and not (isinstance(u, int) and u < 2):
                        act.wait_ge(S("a_dA"), upto(u - 1))
                        act.wait_ge(S("a_dB"), upto(u - 1))
                    keys = slice(0, KEYS_A) if kp == 0 else slice(KEYS_A, KEYS)
                    nc.scalar.activation(A[f"e{b}"][:, half, keys].rearrange("p (o w) -> p o w", w=512), psum[:, 3 * kp:5 if kp else 3, :],
                                         ACT.Exp, bias=st[:, 4 + part:5 + part], scale=SCALE, accum_out=st[:, 8 + part:9 + part]).then_inc(S("a_exp"), 1)
                    if kp == 1:
                        nc.scalar.activation(st[:, 12 + half:13 + half], st[:, part - 1:part], ACT.Exp, bias=st[:, 4 + part:5 + part],
                                             scale=SCALE).then_inc(S("a_al"), 1)

                def turn_act(u, b, f):
                    act.wait_ge(S("a_tr"), 5 * u + f + 1)
                    nc.scalar.activation(A["dt"][:, f, :], psum[:, 5 + (b + f) % 2, :], ACT.Copy).then_inc(S("a_tevS"), 1)

                def output(u, b, stored):
                    act.wait_ge(S("a_o"), u + 1)
                    act.wait_ge(S(f"a_st{b}"), upto(16 * stored))
                    nc.scalar.activation(A[f"os{b}"][:], psum[:, 7, 0:P], ACT.Identity, scale=A[f"s{b}"][:, 20:21]).then_inc(S("a_os"), 1)

                def unit(u, b, prev):
                    if prev is not None:
                        turn_act(prev, b, 0)
                    exps(u, b, 0)
                    if prev is not None:
                        turn_act(prev, b, 2)
                    exps(u, b, 1)
                    if prev is not None:
                        turn_act(prev, b, 4)
                    exps(u, b, 2)
                    exps(u, b, 3)

                for h in range(HEADS):
                    u0 = U + 16 * h
                    for b in (0, 1):
                        if h:
                            output(u0 - 3 + b, 1 - b, u0 // 2 - 2 + b)
                        unit(u0 + b, b, u0 - 2 + b if h else None)
                        for k in W_OUT_SLOTS[h][b]:
                            act.wait_ge(S(f"piece{k // 2}"), loaded("o_", l))
                            nc.scalar.activation(O["wh"][:, k, :], O["wraw"][:, k, :], ACT.Copy).then_inc(S("o_wh"), 1)

                    def pair(m):
                        for b in (0, 1):
                            if isinstance(m, int) and h == 0 and 2 * m + b == 2:
                                act.wait_ge(S("b_st"), 32 * (l + 1))
                            if not (isinstance(m, int) and h == 0 and 2 * m + b < 3):
                                output(u0 + 2 * m - 3 + b, 1 - b, u0 // 2 + m - 2 + b)
                            unit(u0 + 2 * m + b, b, u0 + 2 * m - 2 + b)
                    head_pairs(act, h, pair)
                for b in (0, 1):
                    output(U + 61 + b, 1 - b, U // 2 + 30 + b)
                    for f in (0, 2, 4):
                        turn_act(U + 62 + b, b, f)
                output(U + 63, 1, U // 2 + 31)
                stage_end(act)

                stage_begin(act, l, 5)
                def norm(t, b, half):
                    n = l * TILES + t
                    act.wait_ge(S(f"o_og{b}"), 32 * (l * TILES // 2 + half + 1))
                    if not (isinstance(t, int) and t < 2):
                        act.wait_ge(S("o_ms"), n - 1)
                    act.wait_ge(S("o_sq"), upto(n))
                    for h in range(HEADS):
                        last = nc.scalar.activation(O["junk"][:, h * P:(h + 1) * P], O[f"o{b}"][:, h * P:(h + 1) * P], ACT.Square,
                                                    accum_out=O[f"sm{b}"][:, h:h + 1])
                    last.then_inc(S("o_sq"), 1)

                def hi(t, b, half):
                    n = l * TILES + t
                    act.wait_ge(S("o_tr"), n + 1)
                    if not (isinstance(t, int) and t < 2):
                        act.wait_ge(S("o_lo"), n - 1)
                    nc.scalar.activation(O[f"yf{b}"][:, 4:8, :].rearrange("p a n -> p (a n)"), psum[:, 6 + b, :], ACT.Copy).then_inc(S("o_yf"), 1)
                    act.wait_ge(S("o_yf"), n + 1)
                    act.wait_ge(S(f"o_yt{b}"), 16 * (l * TILES // 2 + half + 1))
                    if not (isinstance(t, int) and t < 2):
                        act.wait_ge(S("o_mm"), 2 * (n - 1))
                    nc.scalar.activation(O[f"yh{b}"][:], O[f"yf{b}"][:], ACT.Copy).then_inc(S("o_hi"), 1)

                def final_square(t, b):
                    act.wait_ge(S("o_xn"), l * TILES + t + 1)
                    act.wait_ge(S("o_fsq"), upto(t))
                    nc.scalar.activation(O["junk2"][:], O[f"xn{b}"][:], ACT.Square, accum_out=O[f"sm{b}"][:, 12:13]).then_inc(S("o_fsq"), 1)

                norm(0, 0, 0)
                norm(1, 1, 0)
                hi(0, 0, 0)

                def step(t, b, m):
                    if near(t, 1):
                        hi(t + 1, 1 - b, m + b)
                    if near(t, 2):
                        norm(t + 2, b, m + 1)
                    if near(t, -1) and l == DEPTH - 1:
                        final_square(t - 1, 1 - b)
                out_steps(act, step)
                stage_end(act)

        @block.vector
        def _(dve):
            chain = [0]

            def linked(instruction):
                chain[0] += 1
                instruction.then_inc(S("dve_chain"), 1)
                dve.wait_ge(S("dve_chain"), chain[0])

            nc.vector.memset(ones[:], 1.0).then_inc(S("ones_set"), 1)
            nc.vector.memset(neg_half[:], -0.5).then_inc(S("ones_set"), 1)
            nc.vector.memset(lam_sum[:], 0.0).then_inc(S("ones_set"), 1)
            dve.wait_ge(S("consts"), 16 * 5)
            for l in range(DEPTH):
                stage_begin(dve, l, 0)
                dve.wait_ge(S("lam_in"), 16 * (l + 1))
                linked(nc.vector.tensor_tensor(lam_pr[:], lam_in[:, 0::2, :], lam_in[:, 1::2, :], ALU.mult))
                nc.vector.tensor_reduce(lam_sum[:], lam_pr[:], AX_X, ALU.add).then_inc(S("lam_sum"), 1)
                dve.wait_ge(S("lam_exp"), l + 1)
                lam_init = 0.8 - 0.6 * math.exp(-0.3 * l)
                linked(nc.vector.scalar_tensor_tensor(lam[:], lam_exp[:, 0:1], lam_init, lam_exp[:, 1:2], ALU.add, ALU.subtract))
                dve.wait_ge(S("mod_col"), l + 1)
                linked(nc.vector.tensor_tensor(mod[:], psum[:, 6, 0:32].rearrange("p (m g) -> p m g", g=2),
                                               bmod_sb[:, l, 0:16].unsqueeze(2).broadcast_to([P, 16, 2]), ALU.add))
                linked(nc.vector.tensor_scalar(one_scale[:], mod[:, 8:16, :], 1.0, None, ALU.add))
                linked(nc.vector.tensor_tensor(one_scale[:], one_scale[:], ng_sb[:, l].unsqueeze(2).broadcast_to([P, KT, 2]), ALU.mult))
                weights_dve(dve, "t_", l, T)
                stage_end(dve)

                stage_begin(dve, l, 1)
                norm_dve(dve, "t_", T, l, 0, True)
                for q in range(4):
                    fill_dve(dve, "t_", T, l, 0, 0, q, MT)

                def t_group(i, b, nxt=True):
                    if nxt:
                        norm_dve(dve, "t_", T, l, i + 1, True)
                    gi = l * NG + i
                    for m, (w, j) in enumerate(T_ORDER):
                        if m in T_DVE:
                            dve.wait_ge(S("t_mm"), MT * gi + m + 1)
                            dve.wait_ge(S("t_act"), len(T_ACT) * gi + T_ACT.index(m - 1) + 1)
                            dst, other = (z, T["cg"]) if w == "hc" else (bgs, T["gb"])
                            nc.vector.tensor_tensor(dst[:, j, bass.ds(i * G, G)], psum[:, m % T_BANKS, 0:G], other[:], ALU.mult).then_inc(S("t_dve"), 1)
                        if nxt and m in T_FILL_AFTER:
                            fill_dve(dve, "t_", T, l, i + 1, 1 - b, T_FILL_AFTER[m], MT)
                groups(dve, t_group, t_group, lambda i, b: t_group(i, b, False))
                stage_end(dve)

                stage_begin(dve, l, 2)
                dve.wait_ge(S("f_in"), 64 * (l + 1))
                fa, fe, fo, ya, sga = F["fa"], F["fe"], F["fo"], F["fa"], F["sga"]
                for j in (0, 1):
                    nc.vector.tensor_tensor(fe[:, j, 1:NH], fa[:, j, 1:NH], fa[:, j, NS - 1:NH:-1], ALU.add)
                    nc.vector.tensor_tensor(fo[:, j, 1:NH], fa[:, j, 1:NH], fa[:, j, NS - 1:NH:-1], ALU.subtract)
                nc.vector.tensor_copy(fe[:, :, 0:NH + 1:NH], fa[:, :, 0:NH + 1:NH])
                nc.vector.memset(fo[:, :, 0:1], 0.0).then_inc(S("f_fold"), 1)
                def conv_outer(j):
                    dve.wait_ge(S("cv_mid"), 2 * l + j + 1)
                    cy = F["cy"]
                    for tap, to, frm in ((0, 1, 0), (2, 0, 1)):
                        for a, b in ((0, NS), (NS, NTOK)):
                            ins_ = nc.vector.scalar_tensor_tensor(cy[:, a + to:b - frm], z[:, j, a + frm:b - to], conv_sb[:, l, j, tap:tap + 1],
                                                                  cy[:, a + to:b - frm], ALU.mult, ALU.add)
                        linked(ins_)
                    nc.vector.tensor_tensor(cy[:], cy[:], bgs[:, j, :], ALU.mult).then_inc(S("cv_y"), 1)

                conv_outer(0)
                dve.wait_ge(S("f_nyq"), 2 * (l + 1))
                dve.wait_ge(S("f_sga"), 32 * (l + 1))
                nc.vector.tensor_tensor(ya[:, :, NH:NH + 1], psum[:, 0, 0:2].unsqueeze(2), sga[:, :, NH:NH + 1], ALU.mult)
                nc.vector.tensor_tensor(ya[:, :, NS:NTOK], psum[:, 1, :].rearrange("p (a b) -> p a b", a=2), sga[:, :, NS:NTOK], ALU.mult).then_inc(S("f_ya"), 1)
                for n in range(4):
                    ct, kc = n // 2, n % 2
                    dve.wait_ge(S("f_sq"), l * 4 + n + 1)
                    cb = psum[:, (5, 7)[n % 2], :]
                    sq = F[f"sq{n % 2}"]
                    a = kc * 512
                    o = 1 if kc == 0 else 0
                    top = NS - a - o
                    low = slice(a, a + 512)
                    high = slice(top - (512 - o) + 1, top + 1)
                    nc.vector.tensor_tensor(ya[:, ct, low], cb, sq[:], ALU.subtract)
                    nc.vector.tensor_tensor(ya[:, ct, top:top - (512 - o):-1], cb[:, o:512], sq[:, o:512], ALU.add).then_inc(S("f_out"), 1)
                    dve.wait_ge(S("f_out"), 4 * l + n + 1)
                    for part in (low, high):
                        ins_ = nc.vector.tensor_tensor(ya[:, ct, part], ya[:, ct, part], sga[:, ct, part], ALU.mult)
                    ins_.then_inc(S("f_ya"), 1)
                    if n == 0:
                        conv_outer(1)
                stage_end(dve)

                stage_begin(dve, l, 3)
                norm_dve(dve, "n_", N, l, 0, False)
                for q in range(4):
                    fill_dve(dve, "n_", N, l, 0, 0, q, 8)

                def dup_lo(n, kind, f):
                    dve.wait_ge(S("n_fhi"), n + 1)
                    if kind == "qst":
                        src = psum[:, 4 + f, :].rearrange("p (j n) -> p j n", j=4)
                        ins_ = nc.vector.tensor_tensor(N[f"qst{f}"][:, :, 1, :].bitcast(F32R), src, N[f"qst{f}"][:, :, 0, :], ALU.subtract)
                    else:
                        src = psum[HD:P, 4 + f, :].rearrange("p (j n) -> p j n", j=4)
                        ins_ = nc.vector.tensor_tensor(N[f"kst{f}"][HD:P].bitcast(F32R), src, N[f"kst{f}"][HD:P], ALU.subtract)
                    ins_.then_inc(S("n_flo"), 1)
                    return ins_

                def cached_lo(t):
                    for f in (0, 1):
                        cached = CACHED_T[f"cached{2 * t + f}"]
                        dve.wait_ge(S("n_fhi"), l * 80 + 2 * t + f + 1)
                        nc.vector.tensor_tensor(cached[HD:P].bitcast(F32R), psum[HD:P, 4 + f, :].rearrange("p (j n) -> p j n", j=4), cached[HD:P],
                                                ALU.subtract).then_inc(S("n_flo"), 1)
                weights_dve(dve, "n_", l, N, cached_lo)

                def rope(tt, n):
                    nt = l * TILES + tt
                    dve.wait_ge(S("n_mm"), 4 * nt + n + 1)
                    dve.wait_ge(S("n_tab"), 16 * (nt + 1))
                    dve.wait_ge(S("n_dup"), upto(l * 40 + 4 + 2 * tt + n))
                    cos = N["rope"][:, 0].unsqueeze(1).broadcast_to([P, 8, HD])
                    nc.vector.tensor_tensor(N["m1"][:].rearrange("p (j d) -> p j d", j=8), psum[:, n, :].rearrange("p (j d) -> p j d", j=8), cos, ALU.mult).then_inc(S("n_rope"), 1)
                    src = psum[:, n, :].rearrange("p (j r a w) -> p j r a w", j=8, r=2, a=2)
                    dst = N["m2"][:].rearrange("p (j r a w) -> p j r a w", j=8, r=2, a=2)
                    sin = N["rope"][:, 1].rearrange("p (r a w) -> p r a w", r=2, a=2)
                    for a in (0, 1):
                        ins_ = nc.vector.tensor_tensor(dst[:, :, :, a, :], src[:, :, :, 1 - a, :], sin[:, :, a, :].unsqueeze(1).broadcast_to([P, 8, 2, 16]), ALU.mult)
                    ins_.then_inc(S("n_rope"), 1)

                def n_group(i, b, nxt=True):
                    if nxt:
                        norm_dve(dve, "n_", N, l, i + 1, False)
                    for s in (0, 1):
                        tt = 2 * i + s
                        for n in range(4):
                            for qk, back in dups_after(i, s, n):
                                for f in (0, 1):
                                    dup_lo(l * 80 + 8 + 4 * (tt - back) + 2 * qk + f, ("qst", "kst")[qk], f)
                            if n < 2:
                                rope(tt, n)
                            if nxt and 4 * s + n in N_FILL_AFTER:
                                fill_dve(dve, "n_", N, l, i + 1, 1 - b, N_FILL_AFTER[4 * s + n], 8)
                groups(dve, n_group, n_group, lambda i, b: n_group(i, b, False))
                stage_end(dve)

                stage_begin(dve, l, 4)
                U = l * 64

                for t in (0, 1):
                    dve.wait_ge(S("b_qk"), 2 * l + t + 1)
                    linked(nc.vector.tensor_reduce(B[f"mx{t}"][:], psum[:, 4 * t:4 * t + 4, :].rearrange("p a (b n) -> p (a b) n", b=2), AX_X, ALU.max))
                    nc.vector.tensor_scalar(B[f"nb{t}"][:], B[f"mx{t}"][:], -SCALE, None, ALU.mult).then_inc(S("b_nb"), 1)
                for t in (0, 1):
                    dve.wait_ge(S("b_exp"), 2 * l + t + 1)
                    linked(nc.vector.reciprocal(B[f"rl{t}"][:], B[f"ls{t}"][:]))
                    linked(nc.vector.tensor_scalar(B[f"nr{t}"][:], B[f"rl{t}"][:, 0::2], -1.0, None, ALU.mult))
                    linked(nc.vector.scalar_tensor_tensor(B[f"c{t}"][:], B[f"ls{t}"][:, 0::2], lam[:, 0:1], B[f"rl{t}"][:, 1::2], ALU.mult, ALU.mult))
                    for h in range(HEADS):
                        last = nc.vector.scalar_tensor_tensor(B[f"d{t}"][:, h, :], B[f"e{t}"][:, 2 * h + 1, :], B[f"c{t}"][:, h:h + 1],
                                                              B[f"e{t}"][:, 2 * h, :], ALU.mult, ALU.subtract)
                    last.then_inc(S("b_d"), 1)
                for t in (0, 1):
                    dve.wait_ge(S("b_o"), 2 * l + t + 1)
                    nc.vector.tensor_tensor(B[f"os{t}"][:].rearrange("p (h d) -> p h d", h=HEADS), psum[:, 4 * t + 2, :].rearrange("p (h d) -> p h d", h=HEADS),
                                            B[f"nr{t}"][:].unsqueeze(2).broadcast_to([P, HEADS, P]), ALU.mult).then_inc(S("b_os"), 1)

                def maxima(u, b, part):
                    half, kp = part // 2, part % 2
                    st = A[f"s{b}"]
                    dve.wait_ge(S("a_qk"), 4 * u + part + 1)
                    if part == 0 and not (isinstance(u, int) and u < 2):
                        dve.wait_ge(S("a_dB"), upto(u - 1))
                    nc.vector.tensor_reduce(st[:, part:part + 1], psum[:, 3 * kp:5 if kp else 3, :], mybir.AxisListType.XY,
                                            ALU.max).then_inc(S("a_mx"), 1)
                    dve.wait_ge(S("a_mx"), 4 * u + part + 1)
                    if kp == 0:
                        nc.vector.tensor_scalar(st[:, 4 + part:5 + part], st[:, part:part + 1], -SCALE, None, ALU.mult).then_inc(S("a_nb"), 1)
                    else:
                        nc.vector.tensor_scalar(st[:, 4 + part:5 + part], st[:, part:part + 1], st[:, part - 1:part], -SCALE, ALU.max, ALU.mult).then_inc(S("a_nb"), 1)

                SMALL = 3

                def small(u, n, ins_):
                    ins_.then_inc(S("a_sm"), 1)
                    dve.wait_ge(S("a_sm"), SMALL * u + n + 1)

                def factors(u, b):
                    st = A[f"s{b}"]
                    c = lambda i, w=1: st[:, i:i + w]
                    dve.wait_ge(S("a_exp"), upto(4 * u + 4))
                    dve.wait_ge(S("a_al"), upto(2 * u + 2))
                    if not (isinstance(u, int) and u < 2):
                        dve.wait_ge(S("a_os"), upto(u - 1))
                    for half in (0, 1):
                        ins_ = nc.vector.scalar_tensor_tensor(c(14 + half), c(8 + 2 * half), c(12 + half), c(9 + 2 * half), ALU.mult, ALU.add)
                    small(u, 0, ins_)
                    small(u, 1, nc.vector.reciprocal(c(16, 2), c(14, 2)))
                    nc.vector.tensor_scalar(c(20), c(16), -1.0, None, ALU.mult)
                    small(u, 2, nc.vector.scalar_tensor_tensor(c(18), c(14), lam[:, 0:1], c(17), ALU.mult, ALU.mult))
                    nc.vector.tensor_scalar(c(19), c(18), c(13), None, ALU.mult).then_inc(S("a_c"), 1)

                def combine(u, b):
                    e = A[f"e{b}"]
                    dve.wait_ge(S("a_c"), u + 1)
                    dve.wait_ge(S("a_e1"), u + 1)
                    if not (isinstance(u, int) and u < 2):
                        dve.wait_ge(S("a_tr"), upto(5 * (u - 1)))
                    nc.vector.scalar_tensor_tensor(A[f"d{b}"][:, 0:KEYS_A], e[:, 1, 0:KEYS_A], A[f"s{b}"][:, 19:20], e[:, 0, 0:KEYS_A],
                                                   ALU.mult, ALU.subtract).then_inc(S("a_dA"), 1)

                def turn_dve(u, b, f):
                    dve.wait_ge(S("a_tr"), 5 * u + f + 1)
                    nc.vector.tensor_copy(A["dt"][:, f, :], psum[:, 5 + (b + f) % 2, :]).then_inc(S("a_tevV"), 1)

                def unit(u, b, first=False):
                    lone = first and b == 0
                    maxima(u, b, 0)
                    if not first:
                        turn_dve(u - 2, b, 1)
                    if not lone:
                        factors(u - 1, 1 - b)
                    maxima(u, b, 1)
                    if not first:
                        turn_dve(u - 2, b, 3)
                    maxima(u, b, 2)
                    maxima(u, b, 3)
                    if not lone:
                        combine(u - 1, 1 - b)

                for h in range(HEADS):
                    u0 = U + 16 * h
                    for b in (0, 1):
                        unit(u0 + b, b, h == 0)

                    def pair(m):
                        if isinstance(m, int) and h == 0 and m == 1:
                            dve.wait_ge(S("b_st"), 32 * (l + 1))
                        for b in (0, 1):
                            unit(u0 + 2 * m + b, b)
                    head_pairs(dve, h, pair)
                factors(U + 63, 1)
                turn_dve(U + 62, 0, 1)
                turn_dve(U + 62, 0, 3)
                combine(U + 63, 1)
                turn_dve(U + 63, 1, 1)
                turn_dve(U + 63, 1, 3)
                stage_end(dve)

                stage_begin(dve, l, 5)
                dve.wait_ge(S("o_c"), 32 * (l + 1))
                linked(nc.vector.tensor_scalar(O["subln"][:], O["subln"][:], 1.0 - lam_init, None, ALU.mult))

                def scale(t, b):
                    n = l * TILES + t
                    sm = O[f"sm{b}"]
                    dve.wait_ge(S("o_sq"), n + 1)
                    nc.vector.tensor_scalar(sm[:, 4:8], sm[:, 0:4], 1.0 / P, EPS, ALU.mult, ALU.add).then_inc(S("o_ms"), 1)
                    dve.wait_ge(S("o_rs"), n + 1)
                    hv = lambda x: x[:].rearrange("p (h d) -> p h d", h=HEADS)
                    nc.vector.tensor_tensor(hv(O["on"]), hv(O[f"o{b}"]), sm[:, 8:12].unsqueeze(2).broadcast_to([P, HEADS, P]), ALU.mult).then_inc(S("o_y1"), 1)
                    dve.wait_ge(S("o_y1"), n + 1)
                    nc.vector.tensor_tensor(hv(O["on2"]), hv(O["on"]), O["subln"][:].unsqueeze(1).broadcast_to([P, HEADS, P]), ALU.mult).then_inc(S("o_y2"), 1)
                    dve.wait_ge(S("o_y2"), n + 1)
                    if not (isinstance(t, int) and t < 2):
                        dve.wait_ge(S("o_tr"), n - 1)
                    nc.vector.tensor_tensor(O[f"gated{b}"][:], O["on2"][:], O[f"g{b}"][:], ALU.mult).then_inc(S("o_gated"), 1)

                def lo(t, b):
                    dve.wait_ge(S("o_hi"), l * TILES + t + 1)
                    nc.vector.tensor_tensor(O[f"yl{b}"][:], O[f"yf{b}"][:], O[f"yh{b}"][:].bitcast(F32), ALU.subtract).then_inc(S("o_lo"), 1)

                def mod_gate(t, b, g):
                    n = l * TILES + t
                    if not (isinstance(t, int) and t < 2):
                        dve.wait_ge(S("o_xn"), n - 1)
                    for c in (0, 1):
                        dve.wait_ge(S("o_mm"), 2 * n + c + 1)
                        nc.vector.tensor_tensor(O[f"t{b}"][:, c * 512:(c + 1) * 512], psum[:, 2 * b + c, :], O["gate"][:, g, c * 512:(c + 1) * 512], ALU.mult).then_inc(S("o_mg"), 1)

                def final_norm(t, b, half):
                    sm = O[f"sm{b}"]
                    dve.wait_ge(S("o_fsq"), t + 1)
                    nc.vector.tensor_scalar(sm[:, 13:14], sm[:, 12:13], 1.0 / D, EPS, ALU.mult, ALU.add).then_inc(S("o_fms"), 1)
                    dve.wait_ge(S("o_frs"), t + 1)
                    dve.wait_ge(S(f"o_st{b}"), upto(16 * (l * TILES // 2 + half)))
                    nc.vector.scalar_tensor_tensor(O[f"y{b}"][:], O[f"xn{b}"][:], sm[:, 14:15], O["fg"][:], ALU.mult, ALU.mult).then_inc(S("o_y"), 1)

                scale(0, 0)
                scale(1, 1)
                lo(0, 0)
                dve.wait_ge(S("o_g"), 48 * (l + 1))
                linked(nc.vector.tensor_tensor(O["gate"][:], O["gate"][:], O["gate_bias"][:].unsqueeze(1).broadcast_to([P, 2, D]), ALU.add))

                def step(t, b, m):
                    if near(t, -1):
                        mod_gate(t - 1, 1 - b, 1 if isinstance(t, int) and (t - 1) * P >= NS else 0)
                    if near(t, 1):
                        lo(t + 1, 1 - b)
                    if near(t, 2):
                        scale(t + 2, b)
                    if near(t, -1) and l == DEPTH - 1:
                        final_norm(t - 1, 1 - b, m - 1 + b)
                out_steps(dve, step)
                stage_end(dve)

        @block.gpsimd
        def _(pool):
            pool.wait_ge(S("ones_set"), 3)
            for l in range(DEPTH):
                stage_begin(pool, l, 0)
                stage_end(pool)

                stage_begin(pool, l, 1)
                norm_pool(pool, "t_", l, 0)
                for q in range(4):
                    fill_pool(pool, "t_", T, l, 0, 0, q, MT)

                def t_group(i, b, nxt=True):
                    if nxt:
                        norm_pool(pool, "t_", l, i + 1)
                        for q in range(4):
                            fill_pool(pool, "t_", T, l, i + 1, 1 - b, q, MT)
                groups(pool, t_group, t_group, lambda i, b: t_group(i, b, False))
                stage_end(pool)

                stage_begin(pool, l, 2)
                stage_end(pool)

                stage_begin(pool, l, 3)
                for q in range(4):
                    fill_pool(pool, "n_", N, l, 0, 0, q, 8)
                dup = N["dup"]
                for t in range(PAST // P):
                    pool.wait_ge(S(f"n_ck{t}"), 16 * (l + 1))
                    pool.wait_ge(S("n_ftr"), upto(l * 80 + 2 * t))
                    for a in (0, 1):
                        ins_ = nc.gpsimd.tensor_copy(dup[:, :, a, :], CACHED[t][:].rearrange("p (j d) -> p j d", j=8))
                    ins_.then_inc(S("n_dup"), 1)

                def n_group(i, b, nxt=True):
                    for s in (0, 1):
                        tt = 2 * i + s
                        for n in range(4):
                            if nxt and 4 * s + n in N_FILL_AFTER:
                                fill_pool(pool, "n_", N, l, i + 1, 1 - b, N_FILL_AFTER[4 * s + n], 8)
                            if n < 2:
                                pool.wait_ge(S("n_rope"), upto(4 * (l * TILES + tt) + 2 * n + 2))
                                pool.wait_ge(S("n_ftr"), upto(l * 80 + 8 + 4 * tt + 2 * n))
                                if isinstance(i, int) and i == NG - 1:
                                    pool.wait_ge(S("n_newk"), upto(16 * (2 * l + s)))
                                for a in (0, 1):
                                    ins_ = nc.gpsimd.tensor_tensor(dup[:, :, a, :], N["m1"][:].rearrange("p (j d) -> p j d", j=8),
                                                                   N["m2"][:].rearrange("p (j d) -> p j d", j=8), ALU.add)
                                ins_.then_inc(S("n_dup"), 1)
                groups(pool, n_group, n_group, lambda i, b: n_group(i, b, False))
                stage_end(pool)

                stage_begin(pool, l, 4)
                U = l * 64

                def combine(u, b):
                    e = A[f"e{b}"]
                    st = A[f"s{b}"]
                    pool.wait_ge(S("a_c"), u + 1)
                    e1 = e[:, 0, 0:KEYS_A]
                    nc.gpsimd.tensor_tensor(e1, e1, st[:, 12:13].broadcast_to([P, KEYS_A]), ALU.mult).then_inc(S("a_e1"), 1)
                    e2 = e[:, 1, KEYS_A:KEYS]
                    nc.gpsimd.tensor_tensor(e2, e2, st[:, 18:19].broadcast_to([P, KEYS - KEYS_A]), ALU.mult).then_inc(S("a_e2"), 1)
                    pool.wait_ge(S("a_e2"), u + 1)
                    if not (isinstance(u, int) and u < 2):
                        pool.wait_ge(S("a_tr"), upto(5 * (u - 1)))
                    nc.gpsimd.tensor_tensor(A[f"d{b}"][:, KEYS_A:KEYS], e2, e[:, 0, KEYS_A:KEYS], ALU.subtract).then_inc(S("a_dB"), 1)

                for h in range(HEADS):
                    u0 = U + 16 * h
                    for b in (0, 1):
                        if h or b:
                            combine(u0 + b - 1, 1 - b)
                        for k in W_OUT_SLOTS[h][b]:
                            pool.wait_ge(S("o_wh"), l * KT + k + 1)
                            nc.gpsimd.tensor_tensor(O["wl"][:, k, :], O["wraw"][:, k, :], O["wh"][:, k, :].bitcast(F32),
                                                    ALU.subtract).then_inc(S("o_wl"), 1)

                    def pair(m):
                        for b in (0, 1):
                            combine(u0 + 2 * m + b - 1, 1 - b)
                    head_pairs(pool, h, pair)
                combine(U + 63, 1)
                stage_end(pool)

                stage_begin(pool, l, 5)

                def rstd_heads(t, b):
                    sm = O[f"sm{b}"]
                    pool.wait_ge(S("o_ms"), l * TILES + t + 1)
                    nc.gpsimd.tensor_tensor(sm[:, 8:12], sm[:, 4:8], neg_half[:], ALU.pow).then_inc(S("o_rs"), 1)

                def residual(t, b, half):
                    n = l * TILES + t
                    pool.wait_ge(S("o_mg"), 2 * n + 2)
                    pool.wait_ge(S(f"o_x{b}"), 16 * (l * TILES // 2 + half + 1))
                    if not (isinstance(t, int) and t < 2):
                        if l < DEPTH - 1:
                            pool.wait_ge(S(f"o_st{b}"), 16 * (l * TILES // 2 + half))
                        else:
                            pool.wait_ge(S("o_y"), t - 1)
                    nc.gpsimd.tensor_tensor(O[f"xn{b}"][:], O[f"t{b}"][:], O[f"x{b}"][:], ALU.add).then_inc(S("o_xn"), 1)

                def final_rstd(t, b):
                    sm = O[f"sm{b}"]
                    pool.wait_ge(S("o_fms"), t + 1)
                    nc.gpsimd.tensor_tensor(sm[:, 14:15], sm[:, 13:14], neg_half[:, 0:1], ALU.pow).then_inc(S("o_frs"), 1)

                rstd_heads(0, 0)
                rstd_heads(1, 1)

                def step(t, b, m):
                    if near(t, -1):
                        residual(t - 1, 1 - b, m - 1 + b)
                    if near(t, 2):
                        rstd_heads(t + 2, b)
                    if near(t, -1) and l == DEPTH - 1:
                        final_rstd(t - 1, 1 - b)
                out_steps(pool, step)
                stage_end(pool)


def _tables():
    f32 = np.float32
    t = {}
    c = np.arange(FW)
    ang = 2 * np.pi * ((c[:, None] * c[None, :]) % FW) / FW
    norm = 1.0 / math.sqrt(NS * FW)
    lay = lambda a: np.ascontiguousarray(a.reshape(-1, P, a.shape[1]).transpose(1, 0, 2))
    t["chan_cos"] = lay((np.cos(ang) * norm).astype(f32))
    t["chan_sin"] = lay((np.sin(ang) * norm).astype(f32))
    n = np.arange(NH)
    ang = 2 * np.pi * ((n[:, None] * n[None, :]) % NS) / NS
    for name, tab in (("seq_cos", np.cos(ang)), ("seq_sin", np.sin(ang))):
        tab = tab.astype(f32).reshape(8, P, 2, 512)
        t[name] = np.ascontiguousarray(tab.transpose(2, 1, 0, 3))
    sign = np.where(np.arange(512) % 2, -1.0, 1.0).astype(f32)
    t["sign_row"] = sign[None, :]
    t["sign_col"] = np.ascontiguousarray(sign[:P, None])
    n = np.arange(NP)
    ang = 2 * np.pi * ((n[:, None] * n[None, :]) % NP) / NP
    up = math.sqrt(NS / NP)
    t["prompt_cos"] = lay((np.cos(ang) * up).astype(f32))
    t["prompt_sin"] = lay((-np.sin(ang) * up).astype(f32))
    t["ident"] = np.eye(P, dtype=f32)
    half = HD // 2
    inv = (f32(1.0) / (f32(10000.0) ** (np.arange(0, half, 2, dtype=f32) / f32(half)))).astype(f32)
    tok = np.arange(NS)
    rope = np.zeros((NTOK, 2, HD), f32)
    rope[NS:, 0] = 1.0
    for a, pos in enumerate((tok // GRID_W, tok % GRID_W)):
        ang = (pos.astype(f32)[:, None] * inv[None, :]).astype(f32).astype(np.float64)
        w = half // 2
        for b in (0, 1):
            col = a * half + b * w
            rope[:NS, 0, col:col + w] = np.cos(ang)
            rope[:NS, 1, col:col + w] = np.sin(ang) * (-1.0 if b == 0 else 1.0)
    t["rope"] = rope
    return t


def kernel(x_prompt, x_sample, cache_k, cache_v, c, c_ctx, norm_g, w_mod, b_mod, w_in, conv_w, conv_b, lam_vec,
           subln_g, w_out, final_g):
    import concourse.bacc as _bacc
    from concourse.bass_utils import run_bass_kernel_spmd as _run

    a = lambda x: np.ascontiguousarray(np.asarray(x))
    arrays = {
        "x_all": a(np.concatenate([np.asarray(x_sample)[0], np.asarray(x_prompt)[0]])),
        "cond": a(np.stack([np.asarray(c)[0], np.asarray(c_ctx)]).reshape(2, KT, P).transpose(2, 1, 0)),
        "b_mod": a(np.asarray(b_mod).reshape(DEPTH, 24, P).transpose(2, 0, 1)),
        "norm_g": a(np.asarray(norm_g).reshape(DEPTH, KT, P).transpose(2, 0, 1)),
        "b_mod_row": a(b_mod),
        "w_mod": a(w_mod),
        "w_in_t": a(np.asarray(w_in)[:, :, :WT]),
        "w_in_n": a(np.asarray(w_in)[:, :, WT:]),
        "conv_wb": a(np.concatenate([np.asarray(conv_w), np.asarray(conv_b)[:, None]], 1).reshape(DEPTH, 4, 2, P).transpose(3, 0, 2, 1)),
        "lam_vec": a(lam_vec),
        "subln_g": a(subln_g),
        "w_out": a(w_out),
        "final_g": a(np.asarray(final_g)[None]),
        "cache_k": a(np.asarray(cache_k)[0].reshape(DEPTH, PAST, AW)),
        "cache_v": a(np.asarray(cache_v)[0].reshape(DEPTH, PAST, AW)),
        **_tables(),
    }
    nc = _bacc.Bacc("TRN2", target_bir_lowering=False, num_devices=1)
    ins = {n: nc.dram_tensor(n, v.shape, F32, kind="ExternalInput").ap() for n, v in arrays.items()}
    y_all = nc.dram_tensor("y_all", (NTOK, D), F32, kind="ExternalOutput").ap()
    new_k = nc.dram_tensor("new_k", (DEPTH, NP, AW), F32, kind="ExternalOutput").ap()
    new_v = nc.dram_tensor("new_v", (DEPTH, NP, AW), F32, kind="ExternalOutput").ap()
    backbone(nc, ins, y_all, new_k, new_v)
    r = _run(nc, [arrays], core_ids=[0]).results[0]
    y = r["y_all"]
    return (y[NS:].reshape(1, NP, D), y[:NS].reshape(1, NS, D), r["new_k"].reshape(1, DEPTH, NP, HEADS, QKW),
            r["new_v"].reshape(1, DEPTH, NP, HEADS, QKW))
```
